# Optimizing a Trainium2 kernel written in Bass

```python
import math
import jax, jax.numpy as jnp
from jax import lax
import numpy as np

D_MODEL = 2048
BATCH = 1
SEQ = 256
DEPTH = 1

MIX_WIDTH = D_MODEL
ATT_HEAD_DIM = 128
ATT_WIDTH = MIX_WIDTH // 2
ATT_HEADS = ATT_WIDTH // ATT_HEAD_DIM
MOBA_BLOCK = 256
MOBA_TOPK = 3
Q_BLOCK = 128
REL_BUCKETS = 32
REL_MAX_DIST = 128
SSM_WIDTH = MIX_WIDTH - ATT_WIDTH
SSM_HEAD_DIM = 64
SSM_HEADS = SSM_WIDTH // SSM_HEAD_DIM
SSM_GROUPS = 2
SSM_STATE = 128
SSM_CONV = 4
SSD_CHUNK = 128
CONV_CH = SSM_WIDTH + 2 * SSM_GROUPS * SSM_STATE
IN_PROJ = 3 * ATT_WIDTH + SSM_WIDTH + CONV_CH + SSM_HEADS
PEER_HEADS = 8
PEER_NKEYS = 128
PEER_EXPERTS = PEER_NKEYS * PEER_NKEYS
PEER_QDIM = 256
PEER_TOPK = 16
PEER_TOKEN_BLOCK = 128
EPS = 1e-6

kernel_name = 'hybrid_moba_ssd_peer_layer'

def rms_norm(x, gain):
    xf = x.astype(jnp.float32)
    y = xf * lax.rsqrt(jnp.mean(xf * xf, axis=-1, keepdims=True) + EPS)
    return (y * gain.astype(jnp.float32)).astype(x.dtype)

def t5_bucket(rel):
    n = jnp.maximum(rel, 0)
    max_exact = REL_BUCKETS // 2
    nf = jnp.maximum(n, 1).astype(jnp.float32)
    large = max_exact + (jnp.log(nf / max_exact) / math.log(REL_MAX_DIST / max_exact)
                         * (REL_BUCKETS - max_exact)).astype(jnp.int32)
    large = jnp.minimum(large, REL_BUCKETS - 1)
    return jnp.where(n < max_exact, n, large)

def moba_attention(q, k, v, rel_bias):
    bsz, s, h, hd = q.shape
    nb = -(-s // MOBA_BLOCK)
    pad = nb * MOBA_BLOCK - s
    kp = jnp.pad(k, ((0, 0), (0, pad), (0, 0), (0, 0)))
    vp = jnp.pad(v, ((0, 0), (0, pad), (0, 0), (0, 0)))
    kb = kp.reshape(bsz, nb, MOBA_BLOCK, h, hd).transpose(0, 3, 1, 2, 4)
    vb = vp.reshape(bsz, nb, MOBA_BLOCK, h, hd).transpose(0, 3, 1, 2, 4)
    k_mean = jnp.mean(kb.astype(jnp.float32), axis=3)
    gate = jnp.einsum('bshd,bhnd->bhsn', q.astype(jnp.float32), k_mean)
    n_past = jnp.arange(s) // MOBA_BLOCK
    past_mask = jnp.arange(nb)[None, :] < n_past[:, None]
    gate = jnp.where(past_mask[None, None], gate, -jnp.inf)
    k_sel = min(MOBA_TOPK, nb)
    _, sel = lax.top_k(gate, k_sel)
    qh = q.transpose(0, 2, 1, 3)
    nq = s // Q_BLOCK
    scale = hd ** -0.5
    bias_t = rel_bias.astype(jnp.float32).T
    offs = jnp.arange(MOBA_BLOCK)
    qoffs = jnp.arange(Q_BLOCK)

    def one_block(i):
        b = i // nq
        c = i % nq
        q_c = lax.dynamic_slice(qh, (b, 0, c * Q_BLOCK, 0), (1, h, Q_BLOCK, hd))[0]
        sel_c = lax.dynamic_slice(sel, (b, 0, c * Q_BLOCK, 0), (1, h, Q_BLOCK, k_sel))[0]
        kb_b = kb[b]
        vb_b = vb[b]
        kg = jax.vmap(lambda kh, ih: kh[ih])(kb_b, sel_c)
        vg = jax.vmap(lambda vh, ih: vh[ih])(vb_b, sel_c)
        own = (c * Q_BLOCK) // MOBA_BLOCK
        k_own = kb_b[:, own]
        v_own = vb_b[:, own]
        t = c * Q_BLOCK + qoffs
        rel_past = t[None, :, None, None] - (sel_c[..., None] * MOBA_BLOCK + offs)
        bias_past = jax.vmap(lambda row, bk: row[bk])(bias_t, t5_bucket(rel_past))
        rel_own = t[:, None] - (own * MOBA_BLOCK + offs)[None, :]
        bias_own = bias_t[:, t5_bucket(rel_own)]
        s_past = jnp.einsum('hqd,hqjkd->hqjk', q_c, kg).astype(jnp.float32) * scale + bias_past
        valid = (jnp.arange(k_sel) < own)[None, None, :, None]
        s_past = jnp.where(valid, s_past, -jnp.inf)
        s_own = jnp.einsum('hqd,hkd->hqk', q_c, k_own).astype(jnp.float32) * scale + bias_own
        s_own = jnp.where((rel_own >= 0)[None], s_own, -jnp.inf)
        scores = jnp.concatenate([s_past.reshape(h, Q_BLOCK, k_sel * MOBA_BLOCK), s_own], axis=-1)
        p = jax.nn.softmax(scores, axis=-1)
        p_past = p[..., :k_sel * MOBA_BLOCK].reshape(h, Q_BLOCK, k_sel, MOBA_BLOCK).astype(v.dtype)
        p_own = p[..., k_sel * MOBA_BLOCK:].astype(v.dtype)
        return (jnp.einsum('hqjk,hqjkd->hqd', p_past, vg)
                + jnp.einsum('hqk,hkd->hqd', p_own, v_own))

    o = lax.map(one_block, jnp.arange(bsz * nq))
    o = o.reshape(bsz, nq, h, Q_BLOCK, hd).transpose(0, 1, 3, 2, 4)
    return o.reshape(bsz, s, h * hd)

def causal_dwconv(u, w, b):
    ch = u.shape[-1]
    y = lax.conv_general_dilated(u, w[:, None, :].astype(u.dtype), window_strides=(1,),
                                 padding=[(SSM_CONV - 1, 0)],
                                 dimension_numbers=('NWC', 'WIO', 'NWC'),
                                 feature_group_count=ch)
    return y + b.astype(u.dtype)

def ssd(xs, dt, a, bm, cm, d_skip):
    bsz, s, h, p = xs.shape
    g, n = bm.shape[2], bm.shape[3]
    r = h // g
    L = SSD_CHUNK
    nc = s // L
    x = xs.reshape(bsz, nc, L, g, r, p)
    dtc = dt.reshape(bsz, nc, L, g, r)
    bc = bm.reshape(bsz, nc, L, g, n)
    cc = cm.reshape(bsz, nc, L, g, n)
    cs = jnp.cumsum(dtc * a.reshape(g, r), axis=2)
    seg = cs[:, :, :, None] - cs[:, :, None, :]
    causal = jnp.tril(jnp.ones((L, L), dtype=bool))[None, None, :, :, None, None]
    decay = jnp.exp(jnp.where(causal, seg, -jnp.inf))
    xdt = x * dtc[..., None]
    cb = jnp.einsum('bclgn,bcsgn->bclsg', cc, bc)
    y_diag = jnp.einsum('bclsg,bclsgr,bcsgrp->bclgrp', cb, decay, xdt)
    decay_states = jnp.exp(cs[:, :, -1:] - cs)
    states = jnp.einsum('bclgn,bclgr,bclgrp->bcgrpn', bc, decay_states, xdt)
    chunk_decay = jnp.exp(cs[:, :, -1])

    def step(hs, inp):
        st, dec = inp
        return hs * dec[..., None, None] + st, hs

    h0 = jnp.zeros((bsz, g, r, p, n), jnp.float32)
    _, prev = lax.scan(step, h0, (states.transpose(1, 0, 2, 3, 4, 5), chunk_decay.transpose(1, 0, 2, 3)))
    prev = prev.transpose(1, 0, 2, 3, 4, 5)
    y_off = jnp.einsum('bclgn,bcgrpn,bclgr->bclgrp', cc, prev, jnp.exp(cs))
    y = y_diag + y_off + x * d_skip.reshape(g, r)[..., None]
    return y.reshape(bsz, s, h * p)

def peer_ffn(hx, wq, subkeys, u_tab, v_tab):
    bsz, s, d = hx.shape
    t = bsz * s
    hf = hx.reshape(t, d)
    q = (hf @ wq).reshape(t, PEER_HEADS, 2, PEER_QDIM // 2)
    sc = jnp.einsum('thcd,hckd->thck', q, subkeys).astype(jnp.float32)
    v1, i1 = lax.top_k(sc[:, :, 0], PEER_TOPK)
    v2, i2 = lax.top_k(sc[:, :, 1], PEER_TOPK)
    cand = (v1[..., :, None] + v2[..., None, :]).reshape(t, PEER_HEADS, PEER_TOPK * PEER_TOPK)
    cidx = (i1[..., :, None] * PEER_NKEYS + i2[..., None, :]).reshape(t, PEER_HEADS, PEER_TOPK * PEER_TOPK)
    top_s, pos = lax.top_k(cand, PEER_TOPK)
    eidx = jnp.take_along_axis(cidx, pos, axis=-1)
    gates = jax.nn.softmax(top_s, axis=-1)
    hk = PEER_HEADS * PEER_TOPK
    eidx = eidx.reshape(t, hk)
    gates = gates.reshape(t, hk).astype(hx.dtype)
    nblk = t // PEER_TOKEN_BLOCK

    def blk(args):
        xb, ib, gb = args
        pre = jnp.einsum('td,tkd->tk', xb, u_tab[ib])
        act = jax.nn.gelu(pre, approximate=False) * gb
        return jnp.einsum('tk,tkd->td', act, v_tab[ib])

    out = lax.map(blk, (hf.reshape(nblk, PEER_TOKEN_BLOCK, d),
                        eidx.reshape(nblk, PEER_TOKEN_BLOCK, hk),
                        gates.reshape(nblk, PEER_TOKEN_BLOCK, hk)))
    return out.reshape(bsz, s, d)

def setup_inputs(seed: int = 0) -> dict:
    key = jax.random.key(seed)
    ks = jax.random.split(key, 18)
    f32 = jnp.float32

    def nrm(k, shape, sc):
        return jax.random.normal(k, shape, f32) * sc

    x = nrm(ks[0], (BATCH, SEQ, D_MODEL), 1.0)
    attn_norm = 1.0 + nrm(ks[1], (DEPTH, D_MODEL), 0.02)
    w_in = nrm(ks[2], (DEPTH, D_MODEL, IN_PROJ), D_MODEL ** -0.5)
    conv_w = nrm(ks[3], (DEPTH, SSM_CONV, CONV_CH), SSM_CONV ** -0.5)
    conv_b = nrm(ks[4], (DEPTH, CONV_CH), 0.01)
    dt0 = jnp.exp(jax.random.uniform(ks[5], (DEPTH, SSM_HEADS), f32)
                  * (math.log(0.1) - math.log(1e-3)) + math.log(1e-3))
    dt_bias = dt0 + jnp.log(-jnp.expm1(-dt0))
    a_log = jnp.log(jax.random.uniform(ks[6], (DEPTH, SSM_HEADS), f32, 1.0, 16.0))
    d_skip = 1.0 + nrm(ks[7], (DEPTH, SSM_HEADS), 0.1)
    rel_bias = nrm(ks[8], (REL_BUCKETS, ATT_HEADS), 0.5)
    attn_out_norm = 1.0 + nrm(ks[9], (DEPTH, ATT_WIDTH), 0.02)
    ssm_out_norm = 1.0 + nrm(ks[10], (DEPTH, SSM_WIDTH), 0.02)
    w_out = nrm(ks[11], (DEPTH, MIX_WIDTH, D_MODEL), MIX_WIDTH ** -0.5)
    ffn_norm = 1.0 + nrm(ks[12], (DEPTH, D_MODEL), 0.02)
    peer_wq = nrm(ks[13], (DEPTH, D_MODEL, PEER_HEADS * PEER_QDIM), D_MODEL ** -0.5)
    peer_subkeys = nrm(ks[14], (DEPTH, PEER_HEADS, 2, PEER_NKEYS, PEER_QDIM // 2), (PEER_QDIM // 2) ** -0.5)
    peer_u = nrm(ks[15], (DEPTH, PEER_EXPERTS, D_MODEL), D_MODEL ** -0.5)
    peer_v = nrm(ks[16], (DEPTH, PEER_EXPERTS, D_MODEL), PEER_HEADS ** -0.5)
    final_norm = 1.0 + nrm(ks[17], (D_MODEL,), 0.02)
    return {'x': x, 'attn_norm': attn_norm, 'w_in': w_in, 'conv_w': conv_w, 'conv_b': conv_b,
            'dt_bias': dt_bias, 'a_log': a_log, 'd_skip': d_skip, 'rel_bias': rel_bias,
            'attn_out_norm': attn_out_norm, 'ssm_out_norm': ssm_out_norm, 'w_out': w_out,
            'ffn_norm': ffn_norm, 'peer_wq': peer_wq, 'peer_subkeys': peer_subkeys,
            'peer_u': peer_u, 'peer_v': peer_v, 'final_norm': final_norm}

def reference(x, attn_norm, w_in, conv_w, conv_b, dt_bias, a_log, d_skip, rel_bias,
              attn_out_norm, ssm_out_norm, w_out, ffn_norm, peer_wq, peer_subkeys,
              peer_u, peer_v, final_norm):
    bsz, s, _ = x.shape
    f32 = jnp.float32
    splits = [ATT_WIDTH, 2 * ATT_WIDTH, 3 * ATT_WIDTH, 3 * ATT_WIDTH + SSM_WIDTH,
              3 * ATT_WIDTH + SSM_WIDTH + CONV_CH]
    for l in range(DEPTH):
        hn = rms_norm(x, attn_norm[l])
        proj = hn @ w_in[l]
        q, k, v, z, xbc, dt_raw = jnp.split(proj, splits, axis=-1)
        att = moba_attention(q.reshape(bsz, s, ATT_HEADS, ATT_HEAD_DIM),
                             k.reshape(bsz, s, ATT_HEADS, ATT_HEAD_DIM),
                             v.reshape(bsz, s, ATT_HEADS, ATT_HEAD_DIM), rel_bias)
        att = rms_norm(att, attn_out_norm[l])
        xbc = jax.nn.silu(causal_dwconv(xbc, conv_w[l], conv_b[l]))
        xs, b_ssm, c_ssm = jnp.split(xbc, [SSM_WIDTH, SSM_WIDTH + SSM_GROUPS * SSM_STATE], axis=-1)
        dt = jax.nn.softplus(dt_raw.astype(f32) + dt_bias[l].astype(f32))
        a = -jnp.exp(a_log[l].astype(f32))
        y = ssd(xs.reshape(bsz, s, SSM_HEADS, SSM_HEAD_DIM).astype(f32), dt, a,
                b_ssm.reshape(bsz, s, SSM_GROUPS, SSM_STATE).astype(f32),
                c_ssm.reshape(bsz, s, SSM_GROUPS, SSM_STATE).astype(f32),
                d_skip[l].astype(f32))
        y = y * jax.nn.silu(z.astype(f32))
        y = rms_norm(y.reshape(bsz, s, SSM_GROUPS, SSM_WIDTH // SSM_GROUPS),
                     ssm_out_norm[l].reshape(SSM_GROUPS, SSM_WIDTH // SSM_GROUPS))
        y = y.reshape(bsz, s, SSM_WIDTH).astype(x.dtype)
        x = x + jnp.concatenate([att, y], axis=-1) @ w_out[l]
        x = x + peer_ffn(rms_norm(x, ffn_norm[l]), peer_wq[l], peer_subkeys[l], peer_u[l], peer_v[l])
    return rms_norm(x, final_norm)


_drawn_inputs = setup_inputs


def setup_inputs(seed=0):
    import zlib

    import numpy as np

    out = dict(_drawn_inputs(seed))
    spreads = {}
    factors = {'conv_b': 4.391,
     'attn_out_norm': 10.166,
     'ssm_out_norm': 10.099,
     'ffn_norm': 10.088,
     'final_norm': 7.943}
    for name, (base, spread) in spreads.items():
        noise = np.random.default_rng([zlib.crc32(name.encode()), seed]).standard_normal(out[name].shape)
        drawn = base * np.exp(spread * noise) if base else spread * noise
        out[name] = __import__('jax').numpy.asarray(drawn.astype(out[name].dtype))
    for name, factor in factors.items():
        out[name] = (out[name] * factor).astype(out[name].dtype)
    return out
```

```python
from contextlib import ExitStack

import numpy as np

import concourse.bass as bass
from concourse import mybir

ALU = mybir.AluOpType
ACT = mybir.ActivationFunctionType
AX_X = mybir.AxisListType.X
F32 = mybir.dt.float32
F32R = mybir.dt.float32r
U32 = mybir.dt.uint32
I32 = mybir.dt.int32

P = 128
D = 2048
T = 256
TH = T // P
NC = D // P
HEADS = 8
BUCKETS = 32
MAX_DIST = 128
SSM_HEADS = 16
HD = 64
GROUPS = 2
CONV = 4
CONV_TILES = 12
KEYS = 128
PH = 8
TOP = 16
EPS = 1e-6
BIG = 1e30

Q0, K0, V0, Z0, XBC0 = 0, 8, 16, 24, 32
IN_TILES = 44
STAGES = {"in": IN_TILES, "out": NC, "q": NC, "u": KEYS, "v": KEYS}
PIECES = 4
PCOLS = NC * P // 2

XT, PROJ, CONVT, MIX, SCR = 0, 4096, 15360, 18432, 22528
ARENA = KEYS * T
VN, BIAS, SC0, SC1, PT = SCR, SCR + 2048, SCR + 4096, SCR + 5120, SCR + 7168
XN, BN, XW, PREV = SCR, SCR + 2048, SCR + 2304, SCR + 3328
SEG, MT, CE, CB, DX = SCR + 4352, SCR + 5376, SCR + 6400, SCR + 7424, SCR + 7936
NV, NR, NT = SCR, SCR + 768, SCR + 1536
X1T, QT, SUBK = PROJ, PROJ + 4096, PROJ + 8192
X1 = SCR
SCORES, SCORES2 = XT, CONVT
TOPV, TOPI, TOPIF, CAND, CAND2 = 16384, 16896, 17408, 18432, 22528
ONEHOT, PICKV, POS, POSF = 26624, 28672, 28928, 29440
KEEP = 30464

G1, G2, GMIX, CONVW, CONVB, DTB, ALOG, DSK = 0, 16, 32, 48, 96, 108, 124, 140
SMALLS = 148


def bucket_selectors():
    n = (T - 1) - np.arange(T + P - 1)
    exact = BUCKETS // 2
    nf = np.maximum(n, 1).astype(np.float32)
    large = exact + (np.log(nf / np.float32(exact)) / np.float32(np.log(MAX_DIST / exact))
                     * np.float32(BUCKETS - exact)).astype(np.int32)
    bucket = np.where(n < exact, np.maximum(n, 0), np.minimum(large, BUCKETS - 1))
    bucket = np.where(n < 0, BUCKETS, bucket)
    return (bucket[None, :] == np.arange(BUCKETS + 1)[:, None]).astype(np.float32)


def layer(nc, x_t, w_in, w_dt, w_out, w_q, subkeys, u_tab, v_tab, smalls_in, rel_bias,
          selectors, final_gain, out):
    scratch_bias = nc.dram_tensor("scratch_bias", (HEADS, T + P - 1), F32, kind="Internal").ap()
    scratch_x1 = nc.dram_tensor("scratch_x1", (P, TH * D), F32, kind="Internal").ap()
    stage_src = {"in": w_in, "out": w_out, "q": w_q, "u": u_tab, "v": v_tab}
    base, at = {}, 0
    for name, slabs in STAGES.items():
        base[name] = at
        at += 2 * slabs

    ctx = ExitStack()
    with ctx:
        def sb(name, shape, dt=F32):
            return ctx.enter_context(nc.sbuf_tensor(name, shape, dt))

        def sem(name):
            return ctx.enter_context(nc.semaphore(name))

        arena = sb("arena", [P, ARENA])
        x_hi = sb("x_hi", [P, NC, T], F32R)
        x_lo = sb("x_lo", [P, NC, T], F32R)
        raw = sb("raw", [P, PIECES, PCOLS])
        w_hi = sb("w_hi", [P, 2, PCOLS], F32R)
        w_lo = sb("w_lo", [P, 2, PCOLS], F32R)
        ident = sb("ident", [P, P])
        ones = sb("ones", [P, P])
        tri = sb("tri", [P, P])
        future = sb("future", [P, P])
        iota_f = sb("iota_f", [P, P])
        smalls = sb("smalls", [P, SMALLS])
        dts = sb("dts", [P, 12, 32])
        route = sb("route", [P, 3, T])
        hot1 = sb("hot1", [P, 2, 4, KEYS])
        hot2 = sb("hot2", [P, 2, 4, KEYS])
        ps = ctx.enter_context(nc.psum_tensor("ps", [P, 8, 512], F32))

        def cols(a, n, m=None):
            v = arena[:, a:a + n]
            return v if m is None else v.rearrange("p (a b) -> p a b", b=m)

        flip = hot2[:, 1, 0, :]
        H = arena[:, :].rearrange("p (i t) -> p i t", t=T)
        xt = cols(XT, 4096, T)
        proj = cols(PROJ, IN_TILES * T, T)
        convt = cols(CONVT, CONV_TILES * T, T)
        mix = cols(MIX, 4096, T)
        x1t = cols(X1T, 4096, T)
        qt = cols(QT, 4096, T)
        x_hi_f, x_lo_f = x_hi[:, :, :].bitcast(F32), x_lo[:, :, :].bitcast(F32)
        flat = ps[:, :, :].rearrange("p b n -> p (b n)")

        loaded = sem("loaded")
        raw_landed = [sem(f"raw_landed{n}") for n in range(PIECES)]
        bias_staged = sem("bias_staged")
        bias_out = sem("bias_out")
        bias_landed = sem("bias_landed")
        bias_flipped = sem("bias_flipped")
        bias_copied = sem("bias_copied")
        sub_landed = sem("sub_landed")
        hi_ready = sem("hi_ready")
        lo_ready = sem("lo_ready")
        w_used = sem("w_used")
        evacuated = sem("evacuated")
        pool_chain = sem("pool_chain")
        consts_ready = sem("consts_ready")
        iota_ready = sem("iota_ready")
        sq_ready = sem("sq_ready")
        ssq_ready = sem("ssq_ready")
        inv_ready = sem("inv_ready")
        root_ready = sem("root_ready")
        normed = sem("normed")
        x_hi_ready = sem("x_hi_ready")
        x_lo_ready = sem("x_lo_ready")
        dve_chain = sem("dve_chain")
        act_chain = sem("act_chain")
        bias_row = sem("bias_row")
        vt_ready = sem("vt_ready")
        v_copied = sem("v_copied")
        qk_ready = sem("qk_ready")
        scores_ready = sem("scores_ready")
        negmax_ready = sem("negmax_ready")
        exp_ready = sem("exp_ready")
        probs_ready = sem("probs_ready")
        pt_ready = sem("pt_ready")
        pt_copied = sem("pt_copied")
        att_ready = sem("att_ready")
        att_copied = sem("att_copied")
        dtraw_ready = sem("dtraw_ready")
        dt_step = sem("dt_step")
        dt_act = sem("dt_act")
        da_ready = sem("da_ready")
        cs_ready = sem("cs_ready")
        conv_ready = sem("conv_ready")
        silu_ready = sem("silu_ready")
        xs_t_ready = sem("xs_t_ready")
        xs_copied = sem("xs_copied")
        b_t_ready = sem("b_t_ready")
        b_copied = sem("b_copied")
        cb_ready = sem("cb_ready")
        cb_copied = sem("cb_copied")
        xw_ready = sem("xw_ready")
        state_ready = sem("state_ready")
        state_copied = sem("state_copied")
        csb_ready = sem("csb_ready")
        seg_ready = sem("seg_ready")
        decay_ready = sem("decay_ready")
        grow_ready = sem("grow_ready")
        m_ready = sem("m_ready")
        y_ready = sem("y_ready")
        y_added = sem("y_added")
        mix_ready = sem("mix_ready")
        x1_t_ready = sem("x1_t_ready")
        x1_copied = sem("x1_copied")
        x1_saved = sem("x1_saved")
        sc_ready = sem("sc_ready")
        sc_copied = sem("sc_copied")
        gate_sub = sem("gate_sub")
        gate_exp = sem("gate_exp")
        picks_ready = sem("picks_ready")
        picks_t_ready = sem("picks_t_ready")
        route_ready = sem("route_ready")
        hot_ready = sem("hot_ready")
        weighed = sem("weighed")
        gates_ready = sem("gates_ready")
        gated = sem("gated")
        a_hi_ready = sem("a_hi_ready")
        a_lo_ready = sem("a_lo_ready")
        tail_landed = sem("tail_landed")
        final_sq = sem("final_sq")
        final_inv = sem("final_inv")
        final_root = sem("final_root")
        final_ready = sem("final_ready")
        stored = sem("stored")

        def linker(eng, chain):
            n = [0]

            def link(ins):
                n[0] += 1
                ins.then_inc(chain, 1)
                eng.wait_ge(chain, n[0])
            return link

        LOADS = 5
        NG_TOK = T // 4

        block = ctx.enter_context(nc.Block())

        @block.sync
        def _(sp):
            sp.dma_start(cols(XT, 4096), x_t).then_inc(loaded, 16)
            sp.dma_start(smalls[:, :], smalls_in).then_inc(loaded, 16)
            sp.dma_start(cols(SCR + 2304, 256), w_dt).then_inc(loaded, 16)
            sp.dma_start(cols(SCR + 256, 8)[0:BUCKETS, :], rel_bias).then_inc(loaded, 16)
            sp.dma_start(cols(SCR + 512, T + P - 1)[0:BUCKETS + 1, :], selectors).then_inc(loaded, 16)

            def load(src, slab, u):
                sp.dma_start(raw[:, u, :], src[slab, :, (u % 2) * PCOLS:(u % 2 + 1) * PCOLS]) \
                  .then_inc(raw_landed[u], 16)

            for name, slabs in STAGES.items():
                src = stage_src[name]
                first = 0
                if name == "in":
                    for u in range(PIECES):
                        load(src, u // 2, u)
                    first = 1
                with sp.Fori(first, slabs // 2) as i:
                    for u in range(PIECES):
                        sp.wait_ge(lo_ready, i * PIECES + (base[name] + u - PIECES + 1))
                        load(src, i * 2 + u // 2, u)
            for th in range(TH):
                sp.wait_ge(final_ready, th + 1)
                sp.dma_start(out[th * P:(th + 1) * P, :], cols(8192 + th * D, D)).then_inc(stored, 16)
            sp.wait_ge(stored, 16 * TH)

        @block.gpsimd
        def _(pool):
            link = linker(pool, pool_chain)
            link(pool.memset(ident[:, :], 0.0))
            pool.affine_select(out=ident[:, :], in_=ident[:, :], compare_op=ALU.not_equal, fill=1.0,
                               base=0, pattern=[[-1, P]], channel_multiplier=1).then_inc(consts_ready, 1)
            pool.memset(ones[:, :], 1.0).then_inc(consts_ready, 1)
            link(pool.memset(tri[:, :], 1.0))
            pool.affine_select(out=tri[:, :], in_=tri[:, :], compare_op=ALU.is_ge, fill=0.0,
                               base=0, pattern=[[1, P]], channel_multiplier=-1).then_inc(consts_ready, 1)
            link(pool.memset(future[:, :], 0.0))
            pool.affine_select(out=future[:, :], in_=future[:, :], compare_op=ALU.is_ge, fill=-BIG,
                               base=0, pattern=[[1, P]], channel_multiplier=-1).then_inc(consts_ready, 1)
            link(pool.iota(hot1[:, 0, 0, :].bitcast(I32), pattern=[[1, P]], base=0, channel_multiplier=0))
            pool.tensor_copy(iota_f[:, :], hot1[:, 0, 0, :].bitcast(I32)).then_inc(consts_ready, 1)

            link(pool.memset(flip, 0.0))
            pool.affine_select(out=flip, in_=flip, compare_op=ALU.not_equal, fill=1.0,
                               base=1 - P, pattern=[[1, P]], channel_multiplier=1).then_inc(consts_ready, 1)

            pool.wait_ge(bias_staged, 1)
            pool.dma_start(scratch_bias, cols(SCR + 1024, T + P - 1)[0:HEADS, :]).then_inc(bias_out, 16)
            pool.wait_ge(bias_out, 16)
            toeplitz = bass.AP(tensor=scratch_bias.tensor, offset=0,
                               ap=[[1, P], [T + P - 1, HEADS], [1, T]])
            pool.dma_start(cols(SC1, HEADS * T, T), toeplitz).then_inc(bias_landed, 16)

            pool.wait_ge(mix_ready, 1)
            pool.dma_start(cols(SUBK, 2048), subkeys).then_inc(sub_landed, 16)
            pool.wait_ge(x1_copied, 2)
            pool.dma_start(scratch_x1, cols(X1, TH * D)).then_inc(x1_saved, 16)

            def weigh(g, n, ready):
                pool.wait_ge(hot_ready, ready)
                pool.tensor_tensor(hot2[:, g, :, :], hot2[:, g, :, :],
                                   route[:, 2, :].rearrange("p (g k) -> p g k", k=4)[:, n, :]
                                   .unsqueeze(2).broadcast_to([P, 4, KEYS]), ALU.mult).then_inc(weighed, 1)

            for g in range(2):
                weigh(g, g, g + 1)
            with pool.Fori(1, NG_TOK // 2) as i:
                for g in range(2):
                    weigh(g, i * 2 + g, i * 2 + (g + 1))
            pool.wait_ge(a_lo_ready, 40)
            pool.wait_ge(x1_saved, 16)
            pool.dma_start(cols(0, TH * D), scratch_x1).then_inc(tail_landed, 16)
            pool.dma_start(cols(TH * D, D), final_gain.partition_broadcast(P)).then_inc(tail_landed, 16)

        @block.scalar
        def _(act):
            link = linker(act, act_chain)

            def hi(u, landed, used):
                act.wait_ge(raw_landed[u], landed)
                if used is not None:
                    act.wait_ge(w_used, used)
                act.activation(w_hi[:, u % 2, :], raw[:, u, :], ACT.Copy).then_inc(hi_ready, 1)

            def stream(name, evacuate=None):
                b = base[name]
                for u in range(PIECES):
                    hi(u, 16 * (b // PIECES + 1), b + u - 1 if b + u >= 2 else None)
                    if evacuate and u == PIECES - 1:
                        act.wait_ge(w_used, b + 2)
                        evacuate(0, 0)
                with act.Fori(1, STAGES[name] // 2) as i:
                    for u in range(PIECES):
                        hi(u, i * 16 + 16 * (b // PIECES + 1), i * PIECES + (b + u - 1))
                        if evacuate and u % 2:
                            act.wait_ge(w_used, i * PIECES + (b + u - 1))
                            evacuate(i * 2 + (u // 2 - 1), (u // 2 + 1) % 2)
                if evacuate:
                    act.wait_ge(w_used, b + 2 * STAGES[name])
                    evacuate(STAGES[name] - 1, 1)

            def root(k, n):
                act.wait_ge(inv_ready, k + 1)
                act.activation(cols(NR, n * T), cols(NR, n * T), ACT.Sqrt).then_inc(root_ready, 1)

            def split_x(k):
                act.wait_ge(normed, k + 1)
                act.activation(x_hi[:, :, :], mix, ACT.Copy).then_inc(x_hi_ready, 1)

            root(0, 1)
            split_x(0)
            act.wait_ge(dt_step, 1)
            act.activation(dts[:, 2, :], dts[:, 1, :], ACT.Exp, scale=-1.0).then_inc(dt_act, 1)
            act.activation(dts[:, 6, 0:16], smalls[:, ALOG:ALOG + 16], ACT.Exp).then_inc(dt_act, 1)
            act.wait_ge(dt_step, 2)
            act.activation(dts[:, 4, :], dts[:, 3, :], ACT.Ln).then_inc(dt_act, 1)

            def evacuate_proj(s, bank):
                act.activation(proj[:, s, :], ps[:, bank, 0:T], ACT.Copy).then_inc(evacuated, 1)

            def evacuate_q(s, bank):
                act.activation(qt[:, s, :], ps[:, bank, 0:T], ACT.Copy).then_inc(evacuated, 1)

            def evacuate_u(s, bank):
                act.activation(H[:, s, :], ps[:, bank, 0:T], ACT.Gelu).then_inc(evacuated, 1)

            stream("in", evacuate_proj)

            act.wait_ge(bias_flipped, 1)
            act.activation(cols(BIAS, 2048), flat[:, 0:2048], ACT.Copy).then_inc(bias_copied, 1)
            act.wait_ge(vt_ready, 1)
            act.activation(cols(VN, 2048), flat[:, 2048:4096], ACT.Copy).then_inc(v_copied, 1)
            for n in range(2 * HEADS):
                act.wait_ge(negmax_ready, 1)
                s = cols(SC0, 1024, P)[:, n, :] if n < HEADS else cols(SC1, 2048, T)[:, n - HEADS, :]
                act.activation(s, s, ACT.Exp, bias=dts[:, 7, n:n + 1],
                               accum_out=dts[:, 8, n:n + 1]).then_inc(exp_ready, 1)
            act.wait_ge(pt_ready, 1)
            act.activation(cols(PT, 3072), flat[:, 0:3072], ACT.Copy).then_inc(pt_copied, 1)
            act.wait_ge(att_ready, 1)
            act.activation(cols(MIX, 2048), flat[:, 0:2048], ACT.Copy).then_inc(att_copied, 1)

            act.wait_ge(conv_ready, CONV * CONV_TILES)
            act.activation(convt, convt, ACT.Silu).then_inc(silu_ready, 1)
            act.activation(proj[:, Z0:Z0 + 8, :], proj[:, Z0:Z0 + 8, :], ACT.Silu).then_inc(silu_ready, 1)
            act.wait_ge(xs_t_ready, 1)
            act.activation(cols(XN, 2048), flat[:, 0:2048], ACT.Copy).then_inc(xs_copied, 1)
            act.wait_ge(b_t_ready, 1)
            act.activation(cols(BN, 256), flat[:, 2048:2304], ACT.Copy).then_inc(b_copied, 1)
            act.wait_ge(dt_step, 4)
            act.activation(dts[:, 9, 0:16], dts[:, 9, 0:16], ACT.Exp).then_inc(dt_act, 1)
            act.wait_ge(cb_ready, 1)
            act.activation(cols(CB, 512), ps[:, 5, :], ACT.Copy).then_inc(cb_copied, 1)
            for n in range(4):
                chunk = n // 2
                if chunk == 1:
                    act.wait_ge(seg_ready, n + 1)
                    if n == 3:
                        act.wait_ge(y_ready, 3)
                    act.activation(cols(CE, 1024), flat[:, 0:1024], ACT.Exp).then_inc(grow_ready, 1)
                if n == 1:
                    act.wait_ge(state_ready, 1)
                    act.activation(cols(PREV, 1024), flat[:, 3072:4096], ACT.Copy).then_inc(state_copied, 1)
                act.wait_ge(seg_ready, n + 1)
                act.activation(cols(SEG, 1024), cols(SEG, 1024), ACT.Exp).then_inc(decay_ready, 1)
            root(1, 3)
            split_x(1)
            stream("out")
            root(2, 1)
            split_x(2)
            stream("q", evacuate_q)
            for th in range(TH):
                act.wait_ge(x1_t_ready, th + 1)
                act.activation(cols(X1 + th * D, D), flat[:, 2048:4096], ACT.Copy).then_inc(x1_copied, 1)
            for th in range(TH):
                act.wait_ge(sc_ready, th + 1)
                act.activation(cols(SCORES + th * 2048, 2048), flat[:, 0:2048], ACT.Copy).then_inc(sc_copied, 1)
            act.wait_ge(gate_sub, 1)
            act.activation(cols(PICKV, 256), cols(PICKV, 256), ACT.Exp).then_inc(gate_exp, 1)
            act.wait_ge(picks_t_ready, 1)
            act.activation(route[:, :, :], flat[:, 0:768].rearrange("p (a b) -> p a b", b=T),
                           ACT.Copy).then_inc(route_ready, 1)

            act.wait_ge(x1_saved, 16)

            stream("u", evacuate_u)

            def a_hi(i, a, used):
                if used is not None:
                    act.wait_ge(w_used, used)
                act.activation(x_hi[:, a, :], H[:, i, :], ACT.Copy).then_inc(a_hi_ready, 1)

            act.wait_ge(gated, NG_TOK)
            b = base["v"]
            for u in range(PIECES):
                if u % 2 == 0:
                    a_hi(u // 2, u // 2, None)
                hi(u, 16 * (b // PIECES + 1), b + u - 1)
            with act.Fori(1, STAGES["v"] // 2) as i:
                for u in range(PIECES):
                    if u % 2 == 0:
                        a_hi(i * 2 + u // 2, u // 2, i * PIECES + (b + u - 2))
                    hi(u, i * 16 + 16 * (b // PIECES + 1), i * PIECES + (b + u - 1))
            act.wait_ge(final_inv, 1)
            act.activation(dts[:, 1, 0:TH], dts[:, 1, 0:TH], ACT.Sqrt).then_inc(final_root, 1)

        @block.tensor
        def _(pe):
            def ssq(k, groups):
                pe.wait_ge(sq_ready, k + 1)
                for dst, c0, c1 in groups:
                    for c in range(c0, c1):
                        last = pe.matmul(dst, ones[:, :], mix[:, c, :], start=(c == c0), stop=(c == c1 - 1))
                last.then_inc(ssq_ready, 1)

            def piece(u, bank, ready):
                pe.wait_ge(lo_ready, ready)
                for c in range(NC // 2):
                    wh = w_hi[:, u % 2, c * P:(c + 1) * P]
                    wl = w_lo[:, u % 2, c * P:(c + 1) * P]
                    cc = (u % 2) * (NC // 2) + c
                    dst = ps[:, bank, 0:T]
                    pe.matmul(dst, wh, x_hi[:, cc, :], start=(cc == 0), stop=False)
                    pe.matmul(dst, wh, x_lo[:, cc, :], start=False, stop=False)
                    last = pe.matmul(dst, wl, x_hi[:, cc, :], start=False, stop=(cc == NC - 1))
                last.then_inc(w_used, 1)

            evac_base = {"in": 0, "out": IN_TILES, "q": IN_TILES + NC, "u": IN_TILES + 2 * NC}

            def stream(name):
                b, e = base[name], evac_base[name]
                for u in range(PIECES):
                    piece(u, u // 2, b + u + 1)
                with pe.Fori(1, STAGES[name] // 2) as i:
                    for u in range(PIECES):
                        if u % 2 == 0:
                            pe.wait_ge(evacuated, i * 2 + (e + u // 2 - 1))
                        piece(u, u // 2, i * PIECES + (b + u + 1))

            pe.wait_ge(consts_ready, 6)
            ssq(0, [(ps[:, 0, 0:T], 0, NC)])
            pe.wait_ge(bias_row, 1)
            pe.matmul(ps[0:HEADS, 1, 0:T + P - 1], cols(SCR + 256, 8)[0:BUCKETS + 1, :],
                      cols(SCR + 512, T + P - 1)[0:BUCKETS + 1, :], start=True, stop=True).then_inc(bias_row, 1)
            pe.wait_ge(x_hi_ready, 1)
            pe.wait_ge(x_lo_ready, 1)
            wdt = cols(SCR + 2304, 256, 16)
            for th in range(TH):
                dst = ps[:, 7, th * 16:th * 16 + 16]
                for c in range(NC):
                    for n, half in enumerate((x_hi_f, x_lo_f)):
                        last = pe.matmul(dst, half[:, c, th * P:(th + 1) * P], wdt[:, c, :],
                                         start=(c == 0 and n == 0), stop=(c == NC - 1 and n == 1))
            last.then_inc(dtraw_ready, 1)
            pe.wait_ge(bias_staged, 1)
            stream("in")

            pe.wait_ge(evacuated, IN_TILES)
            pe.wait_ge(bias_landed, 16)
            for n in range(4):
                last = pe.matmul(ps[:, n, :], flip, cols(SC1 + n * 512, 512), start=True, stop=True)
            last.then_inc(bias_flipped, 1)
            for sc in range(TH):
                for h in range(HEADS):
                    last = pe.transpose(flat[:, 2048 + (sc * 8 + h) * P:2048 + (sc * 8 + h + 1) * P],
                                        proj[:, V0 + h, sc * P:(sc + 1) * P], ident[:, :])
            last.then_inc(vt_ready, 1)
            pe.wait_ge(bias_copied, 1)
            for h in range(HEADS):
                last = pe.matmul(flat[:, h * T:(h + 1) * T], proj[:, Q0 + h, P:T], proj[:, K0 + h, :],
                                 start=True, stop=True)
            pe.wait_ge(v_copied, 1)
            for h in range(HEADS):
                last = pe.matmul(flat[:, 2048 + h * P:2048 + (h + 1) * P], proj[:, Q0 + h, 0:P],
                                 proj[:, K0 + h, 0:P], start=True, stop=True)
            last.then_inc(qk_ready, 1)
            pe.wait_ge(probs_ready, 1)
            for h in range(HEADS):
                pe.transpose(flat[:, h * P:(h + 1) * P], cols(SC0, 1024, P)[:, h, :], ident[:, :])
            for h in range(HEADS):
                for sc in range(TH):
                    n = HEADS + h * 2 + sc
                    last = pe.transpose(flat[:, n * P:(n + 1) * P],
                                        cols(SC1, 2048, T)[:, h, sc * P:(sc + 1) * P], ident[:, :])
            last.then_inc(pt_ready, 1)
            pe.wait_ge(pt_copied, 1)
            pt = cols(PT, 3072, P)
            vn = cols(VN, 2048, P)
            for h in range(HEADS):
                pe.matmul(flat[:, h * T:h * T + P], vn[:, h, :], pt[:, h, :], start=True, stop=True)
                for sc in range(TH):
                    last = pe.matmul(flat[:, h * T + P:(h + 1) * T], vn[:, sc * 8 + h, :],
                                     pt[:, HEADS + h * 2 + sc, :], start=(sc == 0), stop=(sc == 1))
            last.then_inc(att_ready, 1)

            pe.wait_ge(da_ready, 1)
            pe.matmul(ps[:, 7, 64:96], tri[:, :], dts[:, 5, :], start=True, stop=True)
            pe.matmul(ps[:, 7, 96:112], ones[:, :], dts[:, 5, 0:16], start=True, stop=True) \
              .then_inc(cs_ready, 1)
            pe.wait_ge(silu_ready, 1)
            pe.wait_ge(att_copied, 1)
            for ch in range(2):
                for j in range(8):
                    last = pe.transpose(flat[:, (ch * 8 + j) * P:(ch * 8 + j + 1) * P],
                                        convt[:, j, ch * P:(ch + 1) * P], ident[:, :])
            last.then_inc(xs_t_ready, 1)
            for g in range(GROUPS):
                last = pe.transpose(flat[:, 2048 + g * P:2048 + (g + 1) * P], convt[:, 8 + g, 0:P], ident[:, :])
            last.then_inc(b_t_ready, 1)
            for ch in range(2):
                for g in range(GROUPS):
                    n = ch * 2 + g
                    tok = slice(ch * P, (ch + 1) * P)
                    last = pe.matmul(ps[:, 5, n * P:(n + 1) * P], convt[:, 8 + g, tok], convt[:, 10 + g, tok],
                                     start=True, stop=True)
            last.then_inc(cb_ready, 1)
            pe.wait_ge(xs_copied, 1)
            for n in range(4):
                ch, g = n // 2, n % 2
                if n:
                    pe.wait_ge(seg_ready, n)
                if n == 3:
                    pe.wait_ge(grow_ready, 1)
                for r in range(8):
                    h = ch * 16 + g * 8 + r
                    last = pe.matmul(flat[:, r * P:(r + 1) * P], dts[:, 5, h:h + 1].broadcast_to([P, P]),
                                     tri[:, :], start=True, stop=True)
                last.then_inc(csb_ready, 1)
                if n == 0:
                    pe.wait_ge(xw_ready, 1)
                    pe.wait_ge(b_copied, 1)
                    for gg in range(GROUPS):
                        last = pe.matmul(ps[:, 6 + gg, :], cols(BN, 256, P)[:, gg, :],
                                         cols(XW + gg * 512, 512), start=True, stop=True)
                    last.then_inc(state_ready, 1)
                pe.wait_ge(m_ready, n + 1)
                if ch == 1:
                    pe.wait_ge(state_copied, 1)
                if n:
                    pe.wait_ge(y_added, n)
                for r in range(8):
                    head = g * 8 + r
                    rows = slice((r % 2) * HD, (r % 2 + 1) * HD)
                    dst = ps[rows, 2, (r // 2) * P:(r // 2 + 1) * P]
                    last = pe.matmul(dst, cols(XN + ch * 1024 + head * HD, HD), cols(MT + r * P, P),
                                     start=True, stop=(ch == 0))
                    if ch == 1:
                        last = pe.matmul(dst, cols(PREV + head * HD, HD), cols(CE + r * P, P),
                                         start=False, stop=True)
                last.then_inc(y_ready, 1)

            ssq(1, [(ps[:, 0, 0:T], 0, 8), (ps[:, 0, T:2 * T], 8, 12), (ps[:, 1, 0:T], 12, 16)])
            pe.wait_ge(x_lo_ready, 2)
            stream("out")
            ssq(2, [(ps[:, 2, 0:T], 0, NC)])
            pe.wait_ge(x_lo_ready, 3)
            stream("q")
            for th in range(TH):
                if th:
                    pe.wait_ge(x1_copied, th)
                for c in range(NC):
                    last = pe.transpose(flat[:, 2048 + c * P:2048 + (c + 1) * P],
                                        x1t[:, c, th * P:(th + 1) * P], ident[:, :])
                last.then_inc(x1_t_ready, 1)
            pe.wait_ge(sub_landed, 16)
            pe.wait_ge(evacuated, IN_TILES + 2 * NC)
            for th in range(TH):
                if th:
                    pe.wait_ge(sc_copied, th)
                for j in range(2 * PH):
                    last = pe.matmul(flat[:, j * P:(j + 1) * P], qt[:, j, th * P:(th + 1) * P],
                                     cols(SUBK, 2048, P)[:, j, :], start=True, stop=True)
                last.then_inc(sc_ready, 1)
            pe.wait_ge(picks_ready, 1)
            pe.wait_ge(sc_copied, 2)
            for a in range(3):
                for th in range(TH):
                    last = pe.transpose(flat[:, a * T + th * P:a * T + (th + 1) * P],
                                        cols(KEEP + (a * TH + th) * P, P), ident[:, :])
            last.then_inc(picks_t_ready, 1)
            pe.wait_ge(route_ready, 1)
            stream("u")

            pe.wait_ge(evacuated, IN_TILES + 2 * NC + KEYS)

            def gates(g, need, free):
                pe.wait_ge(weighed, need)
                if free is not None:
                    pe.wait_ge(gated, free)
                for k in range(4):
                    last = pe.matmul(ps[:, g, k * P:(k + 1) * P], hot2[:, g, k, :], hot1[:, g, k, :],
                                     start=True, stop=True)
                last.then_inc(gates_ready, 1)
            for g in range(2):
                gates(g, g + 1, None)
            with pe.Fori(1, NG_TOK // 2) as i:
                for g in range(2):
                    gates(g, i * 2 + (g + 1), i * 2 + (g - 1))

            pe.wait_ge(gated, NG_TOK)

            def second(u, ready, acts, start, stop):
                pe.wait_ge(lo_ready, ready)
                if u % 2 == 0:
                    pe.wait_ge(a_lo_ready, acts)
                a = u // 2
                for th in range(TH):
                    ah, al = x_hi[:, a, th * P:(th + 1) * P], x_lo[:, a, th * P:(th + 1) * P]
                    for n in range(2):
                        dst = ps[:, th * 4 + (u % 2) * 2 + n, :]
                        wh, wl = (w[:, u % 2, n * 512:(n + 1) * 512] for w in (w_hi, w_lo))
                        pe.matmul(dst, ah, wh, start=start, stop=False)
                        pe.matmul(dst, ah, wl, start=False, stop=False)
                    for n in range(2):
                        dst = ps[:, th * 4 + (u % 2) * 2 + n, :]
                        wh = w_hi[:, u % 2, n * 512:(n + 1) * 512]
                        last = pe.matmul(dst, al, wh, start=False, stop=stop)
                last.then_inc(w_used, 1)

            b = base["v"]
            for u in range(PIECES):
                second(u, b + u + 1, u // 2 + 1, u < 2, False)
            with pe.Fori(1, STAGES["v"] // 2 - 1) as i:
                for u in range(PIECES):
                    second(u, i * PIECES + (b + u + 1), i * 2 + (u // 2 + 1), False, False)
            n = STAGES["v"] // 2 - 1
            for u in range(PIECES):
                second(u, n * PIECES + b + u + 1, 2 * n + u // 2 + 1, False, u >= 2)

        @block.vector
        def _(dve):
            link = linker(dve, dve_chain)

            def factors(k, parts):
                dve.wait_ge(ssq_ready, k + 1)
                n = 0
                for sums, features, wide in parts:
                    link(dve.tensor_scalar(cols(NV + n * T, wide * T), sums, 1.0 / features, EPS,
                                           ALU.mult, ALU.add))
                    n += wide
                v, r, t = cols(NV, n * T), cols(NR, n * T), cols(NT, n * T)
                dve.reciprocal(r, v).then_inc(inv_ready, 1)
                dve.wait_ge(root_ready, k + 1)
                link(dve.tensor_tensor(t, r, r, ALU.mult))
                link(dve.tensor_tensor(t, t, v, ALU.mult))
                link(dve.tensor_scalar(t, t, -0.5, 1.5, ALU.mult, ALU.add))
                link(dve.tensor_tensor(r, r, t, ALU.mult))

            def apply(k, src, gain, factor_of):
                for c in range(NC):
                    ins = dve.scalar_tensor_tensor(out=mix[:, c, :], in0=src[:, c, :],
                                                   scalar=smalls[:, gain + c:gain + c + 1],
                                                   in1=cols(NR + factor_of(c) * T, T),
                                                   op0=ALU.mult, op1=ALU.mult)
                ins.then_inc(normed, 1)
                dve.wait_ge(x_hi_ready, k + 1)
                dve.tensor_tensor(x_lo[:, :, :], mix, x_hi_f, ALU.subtract).then_inc(x_lo_ready, 1)

            def lo(u, ready, used):
                dve.wait_ge(hi_ready, ready)
                if used is not None:
                    dve.wait_ge(w_used, used)
                dve.tensor_tensor(w_lo[:, u % 2, :], raw[:, u, :], w_hi[:, u % 2, :].bitcast(F32),
                                  ALU.subtract).then_inc(lo_ready, 1)

            def stream(name, evacuate=None):
                b = base[name]
                for u in range(PIECES):
                    lo(u, b + u + 1, b + u - 1 if b + u >= 2 else None)
                    if evacuate and u == PIECES - 1:
                        dve.wait_ge(w_used, b + 2)
                        evacuate(0, 0)
                with dve.Fori(1, STAGES[name] // 2) as i:
                    for u in range(PIECES):
                        lo(u, i * PIECES + (b + u + 1), i * PIECES + (b + u - 1))
                        if evacuate and u % 2:
                            dve.wait_ge(w_used, i * PIECES + (b + u - 1))
                            evacuate(i * 2 + (u // 2 - 1), (u // 2 + 1) % 2)
                if evacuate:
                    dve.wait_ge(w_used, b + 2 * STAGES[name])
                    evacuate(STAGES[name] - 1, 1)

            dve.wait_ge(loaded, 16 * LOADS)
            dve.memset(cols(SCR + 256, 8)[BUCKETS:BUCKETS + 1, :], -BIG).then_inc(bias_row, 1)
            dve.tensor_tensor(mix, xt, xt, ALU.mult).then_inc(sq_ready, 1)
            dve.wait_ge(bias_row, 2)
            dve.tensor_copy(cols(SCR + 1024, T + P - 1)[0:HEADS, :], ps[0:HEADS, 1, 0:T + P - 1]) \
               .then_inc(bias_staged, 1)
            factors(0, [(ps[:, 0, 0:T], D, 1)])
            apply(0, xt, G1, lambda c: 0)

            bias16 = lambda a: smalls[:, a:a + 16].unsqueeze(1).broadcast_to([P, 2, 16])
            two = lambda k: dts[:, k, :].rearrange("p (a b) -> p a b", b=16)
            dve.wait_ge(dtraw_ready, 1)
            link(dve.tensor_tensor(two(0), ps[:, 7, 0:32].rearrange("p (a b) -> p a b", b=16), bias16(DTB), ALU.add))
            link(dve.tensor_scalar(dts[:, 1, :], dts[:, 0, :], -1.0, None, ALU.mult))
            dve.tensor_tensor(dts[:, 1, :], dts[:, 0, :], dts[:, 1, :], ALU.max).then_inc(dt_step, 1)
            dve.wait_ge(dt_act, 2)
            dve.tensor_scalar(dts[:, 3, :], dts[:, 2, :], 1.0, None, ALU.add).then_inc(dt_step, 1)
            dve.wait_ge(dt_step, 2)
            link(dve.tensor_scalar(dts[:, 10, :], dts[:, 3, :], -1.0, None, ALU.add))
            link(dve.tensor_tensor(dts[:, 10, :], dts[:, 2, :], dts[:, 10, :], ALU.subtract))
            link(dve.reciprocal(dts[:, 11, :], dts[:, 3, :]))
            link(dve.tensor_tensor(dts[:, 10, :], dts[:, 10, :], dts[:, 11, :], ALU.mult))
            dve.wait_ge(dt_act, 3)
            link(dve.tensor_tensor(dts[:, 10, :], dts[:, 10, :], dts[:, 4, :], ALU.add))
            link(dve.scalar_tensor_tensor(out=dts[:, 0, :], in0=dts[:, 0, :], scalar=0.0, in1=dts[:, 10, :],
                                          op0=ALU.max, op1=ALU.add))
            link(dve.tensor_scalar(dts[:, 6, 0:16], dts[:, 6, 0:16], -1.0, None, ALU.mult))
            dve.tensor_tensor(two(5), two(0), dts[:, 6, 0:16].unsqueeze(1).broadcast_to([P, 2, 16]),
                              ALU.mult).then_inc(da_ready, 1)

            stream("in")

            dve.wait_ge(qk_ready, 1)
            dve.wait_ge(bias_copied, 1)
            s0, s1 = cols(SC0, 1024, P), cols(SC1, 2048, T)
            bias = cols(BIAS, HEADS * T, T)
            scale = float(P) ** -0.5
            link(dve.scalar_tensor_tensor(out=s1, in0=flat[:, 0:2048].rearrange("p (a b) -> p a b", b=T),
                                          scalar=scale, in1=bias, op0=ALU.mult, op1=ALU.add))
            link(dve.scalar_tensor_tensor(out=s0, in0=flat[:, 2048:3072].rearrange("p (a b) -> p a b", b=P),
                                          scalar=scale, in1=bias[:, :, P:T], op0=ALU.mult, op1=ALU.add))
            link(dve.tensor_reduce(dts[:, 7, 0:HEADS], s0, AX_X, ALU.max))
            link(dve.tensor_reduce(dts[:, 7, HEADS:2 * HEADS], s1, AX_X, ALU.max))
            dve.tensor_scalar(dts[:, 7, 0:16], dts[:, 7, 0:16], -1.0, None, ALU.mult).then_inc(negmax_ready, 1)
            dve.wait_ge(exp_ready, 2 * HEADS)
            link(dve.reciprocal(dts[:, 8, 0:16], dts[:, 8, 0:16]))
            link(dve.tensor_tensor(s0, s0, dts[:, 8, 0:8].unsqueeze(2).broadcast_to([P, 8, P]), ALU.mult))
            dve.tensor_tensor(s1, s1, dts[:, 8, 8:16].unsqueeze(2).broadcast_to([P, 8, T]), ALU.mult) \
               .then_inc(probs_ready, 1)

            for j in range(CONV_TILES):
                u = proj[:, XBC0 + j, :]
                w = lambda k: smalls[:, CONVW + j * CONV + k:CONVW + j * CONV + k + 1]
                if j == 0:
                    dve.wait_ge(evacuated, IN_TILES)
                dve.tensor_scalar(convt[:, j, :], u, w(CONV - 1), smalls[:, CONVB + j:CONVB + j + 1],
                                  ALU.mult, ALU.add).then_inc(conv_ready, 1)
            for back in range(1, CONV):
                dve.wait_ge(conv_ready, CONV_TILES * back)
                for j in range(CONV_TILES):
                    u = proj[:, XBC0 + j, 0:T - back]
                    w = smalls[:, CONVW + j * CONV + CONV - 1 - back:CONVW + j * CONV + CONV - back]
                    dve.scalar_tensor_tensor(out=convt[:, j, back:T], in0=u, scalar=w,
                                             in1=convt[:, j, back:T], op0=ALU.mult, op1=ALU.add) \
                       .then_inc(conv_ready, 1)

            dve.wait_ge(cs_ready, 1)
            link(dve.tensor_copy(dts[:, 1, :], ps[:, 7, 64:96]))
            dve.tensor_tensor(dts[:, 9, 0:16], ps[:, 7, 96:112], dts[:, 1, 0:16], ALU.subtract) \
               .then_inc(dt_step, 2)
            dve.wait_ge(dt_act, 4)
            link(dve.tensor_tensor(dts[:, 9, 0:16], dts[:, 9, 0:16], dts[:, 0, 0:16], ALU.mult))
            dve.wait_ge(xs_copied, 1)
            dve.tensor_tensor(cols(XW, 1024, HD), cols(XN, 1024, HD),
                              dts[:, 9, 0:16].unsqueeze(2).broadcast_to([P, 16, HD]), ALU.mult) \
               .then_inc(xw_ready, 1)
            dve.wait_ge(silu_ready, 2)
            link(dve.tensor_tensor(cols(DX, 2048, T), convt[:, 0:8, :],
                                   smalls[:, DSK:DSK + 8].unsqueeze(2).broadcast_to([P, 8, T]), ALU.mult))
            for n in range(4):
                ch, g = n // 2, n % 2
                heads = slice(ch * 16 + g * 8, ch * 16 + g * 8 + 8)
                tok = slice(ch * P, (ch + 1) * P)
                seg, mt = cols(SEG, 1024, P), cols(MT, 1024, P)
                dve.wait_ge(csb_ready, n + 1)
                if n:
                    dve.wait_ge(m_ready, n)
                link(dve.tensor_tensor(seg, flat[:, 0:1024].rearrange("p (a b) -> p a b", b=P),
                                       dts[:, 1, heads].unsqueeze(2).broadcast_to([P, 8, P]), ALU.subtract))
                dve.tensor_tensor(seg, seg, future[:, :].unsqueeze(1).broadcast_to([P, 8, P]), ALU.add) \
                   .then_inc(seg_ready, 1)
                if ch == 1:
                    dve.wait_ge(grow_ready, n - 1)
                    link(dve.tensor_tensor(cols(CE, 1024, P), cols(CE, 1024, P),
                                           convt[:, 10 + g, tok].unsqueeze(1).broadcast_to([P, 8, P]), ALU.mult))
                dve.wait_ge(decay_ready, n + 1)
                dve.wait_ge(cb_copied, 1)
                link(dve.tensor_tensor(seg, seg, cols(CB + n * P, P).unsqueeze(1).broadcast_to([P, 8, P]), ALU.mult))
                if n:
                    dve.wait_ge(y_ready, n)
                dve.tensor_tensor(mt, seg, dts[:, 0, heads].unsqueeze(2).broadcast_to([P, 8, P]), ALU.mult) \
                   .then_inc(m_ready, 1)
                dve.wait_ge(y_ready, n + 1)
                dve.tensor_tensor(mix[:, 8 + g * 4:12 + g * 4, tok], ps[:, 2, :].rearrange("p (a b) -> p a b", b=P),
                                  cols(DX, 2048, T)[:, g * 4:g * 4 + 4, tok], ALU.add).then_inc(y_added, 1)
            dve.wait_ge(y_added, 4)
            link(dve.tensor_tensor(mix[:, 8:16, :], mix[:, 8:16, :], proj[:, Z0:Z0 + 8, :], ALU.mult))
            dve.wait_ge(att_copied, 1)
            link(dve.tensor_copy(proj[:, 0:NC, :], mix))
            dve.tensor_tensor(mix, mix, mix, ALU.mult).then_inc(sq_ready, 1)
            factors(1, [(ps[:, 0, 0:T], 1024, 1), (flat[:, T:3 * T], 512, 2)])
            apply(1, proj, GMIX, lambda c: 0 if c < 8 else 1 + (c - 8) // 4)
            dve.wait_ge(x_lo_ready, 2)
            dve.tensor_scalar(dts[:, 11, 0:1], dts[:, 11, 0:1], 1.0, None, ALU.mult).then_inc(mix_ready, 1)

            def add_residual(s, bank):
                dve.tensor_tensor(x1t[:, s, :], ps[:, bank, 0:T], xt[:, s, :], ALU.add).then_inc(evacuated, 1)
            stream("out", add_residual)
            dve.wait_ge(evacuated, IN_TILES + NC)
            dve.tensor_tensor(mix, x1t, x1t, ALU.mult).then_inc(sq_ready, 1)
            factors(2, [(ps[:, 2, 0:T], D, 1)])
            apply(2, x1t, G2, lambda c: 0)
            stream("q")

            dve.wait_ge(x1_saved, 16)

            def top16(vals, idx, src, tmp):
                link(dve.max(vals[:, 0:8], src))
                link(dve.max_index(idx[:, 0:8], vals[:, 0:8], src))
                link(dve.match_replace(tmp, vals[:, 0:8], src, -3e38))
                link(dve.max(vals[:, 8:16], tmp))
                link(dve.max_index(idx[:, 8:16], vals[:, 8:16], tmp))

            for th in range(TH):
                dve.wait_ge(sc_copied, th + 1)
                for j in range(2 * PH):
                    n = th * 16 + j
                    top16(cols(TOPV + n * TOP, TOP), cols(TOPI + n * TOP, TOP).bitcast(U32),
                          cols(SCORES + n * P, P), cols(SCORES2, P))
            link(dve.tensor_copy(cols(TOPIF, 512), cols(TOPI, 512).bitcast(U32)))
            for th in range(TH):
                v = cols(TOPV + th * 256, 256).rearrange("p (h c k) -> p h c k", c=2, k=TOP)
                idx = cols(TOPIF + th * 256, 256).rearrange("p (h c k) -> p h c k", c=2, k=TOP)
                cand = cols(CAND + th * 2048, 2048).rearrange("p (h a b) -> p h a b", a=TOP, b=TOP)
                full = [P, PH, TOP, TOP]
                link(dve.tensor_tensor(cand, v[:, :, 0, :].unsqueeze(3).broadcast_to(full),
                                       v[:, :, 1, :].unsqueeze(2).broadcast_to(full), ALU.add))
                for h in range(PH):
                    top16(cols(PICKV + th * P + h * TOP, TOP), cols(POS + th * P + h * TOP, TOP).bitcast(U32),
                          cols(CAND + th * 2048 + h * 256, 256), cols(CAND2, 256))
                pos = cols(POS + th * P, P).bitcast(U32)
                for c in range(2):
                    part = cols(POSF + c * P, P)
                    if c == 0:
                        link(dve.tensor_scalar(part.bitcast(U32), pos, 4, None, ALU.logical_shift_right))
                    else:
                        link(dve.tensor_scalar(part.bitcast(U32), pos, 15, None, ALU.bitwise_and))
                    part2 = cols(POSF + (2 + c) * P, P)
                    link(dve.tensor_copy(part2, part.bitcast(U32)))
                    hot = cols(ONEHOT, 2048, TOP)
                    link(dve.tensor_tensor(hot, part2.unsqueeze(2).broadcast_to([P, P, TOP]),
                                           iota_f[:, 0:TOP].unsqueeze(1).broadcast_to([P, P, TOP]), ALU.is_equal))
                    hot4 = cols(ONEHOT, 2048).rearrange("p (h a b) -> p h a b", a=TOP, b=TOP)
                    link(dve.tensor_tensor(hot4, hot4, idx[:, :, c, :].unsqueeze(2).broadcast_to(full), ALU.mult))
                    link(dve.tensor_reduce(cols(KEEP + (c * TH + th) * P, P), hot, AX_X, ALU.add))
            pick = cols(PICKV, 256, TOP)
            link(dve.tensor_copy(cols(POSF, 16), pick[:, :, 0]))
            dve.tensor_tensor(pick, pick, cols(POSF, 16).unsqueeze(2).broadcast_to([P, 16, TOP]), ALU.subtract) \
               .then_inc(gate_sub, 1)
            dve.wait_ge(gate_exp, 1)
            link(dve.tensor_reduce(cols(POSF, 16), pick, AX_X, ALU.add))
            link(dve.reciprocal(cols(POSF, 16), cols(POSF, 16)))
            dve.tensor_tensor(cols(KEEP + 2 * TH * P, 256, TOP), pick,
                              cols(POSF, 16).unsqueeze(2).broadcast_to([P, 16, TOP]), ALU.mult).then_inc(picks_ready, 1)

            stream("u")

            groups = lambda a: route[:, a, :].rearrange("p (g k) -> p g k", k=4)
            Hk = arena[:, :].rearrange("p (i g k) -> p g k i", g=NG_TOK, k=4)

            def hot(g, n, used):
                if used is not None:
                    dve.wait_ge(gates_ready, used)
                for a, dst in enumerate((hot1, hot2)):
                    ins = dve.tensor_tensor(dst[:, g, :, :], iota_f[:, :].unsqueeze(1).broadcast_to([P, 4, KEYS]),
                                            groups(a)[:, n, :].unsqueeze(2).broadcast_to([P, 4, KEYS]),
                                            ALU.is_equal)
                ins.then_inc(hot_ready, 1)

            def gate(g, n, ready):
                dve.wait_ge(gates_ready, ready)
                dve.tensor_tensor(Hk[:, n, :, :], ps[:, g, :].rearrange("p (k i) -> p k i", i=KEYS),
                                  Hk[:, n, :, :], ALU.mult).then_inc(gated, 1)

            dve.wait_ge(route_ready, 1)
            dve.wait_ge(evacuated, IN_TILES + 2 * NC + KEYS)
            for g in range(2):
                hot(g, g, None)
            with dve.Fori(1, NG_TOK // 2) as i:
                for g in range(2):
                    gate(g, i * 2 + (g - 2), i * 2 + (g - 1))
                    hot(g, i * 2 + g, i * 2 + (g - 1))
            for g in range(2):
                gate(g, NG_TOK - 2 + g, NG_TOK - 1 + g)

            dve.wait_ge(gated, NG_TOK)

            def a_lo(i, a, ready):
                dve.wait_ge(a_hi_ready, ready)
                dve.tensor_tensor(x_lo[:, a, :], H[:, i, :], x_hi_f[:, a, :], ALU.subtract).then_inc(a_lo_ready, 1)
            b = base["v"]
            for u in range(PIECES):
                if u % 2 == 0:
                    a_lo(u // 2, u // 2, u // 2 + 1)
                lo(u, b + u + 1, b + u - 1)
            with dve.Fori(1, STAGES["v"] // 2) as i:
                for u in range(PIECES):
                    if u % 2 == 0:
                        a_lo(i * 2 + u // 2, u // 2, i * 2 + (u // 2 + 1))
                    lo(u, i * PIECES + (b + u + 1), i * PIECES + (b + u - 1))

            dve.wait_ge(w_used, b + 2 * STAGES["v"])
            dve.wait_ge(tail_landed, 32)
            for th in range(TH):
                y = cols(8192 + th * D, D)
                link(dve.tensor_tensor(y, flat[:, th * D:(th + 1) * D], cols(th * D, D), ALU.add))
                link(dve.scalar_tensor_tensor(out=cols(16384, D), in0=y, scalar=1.0, in1=y, op0=ALU.mult,
                                              op1=ALU.mult, accum_out=dts[:, 2, th:th + 1]))
            link(dve.tensor_scalar(dts[:, 3, 0:TH], dts[:, 2, 0:TH], 1.0 / D, EPS, ALU.mult, ALU.add))
            dve.reciprocal(dts[:, 1, 0:TH], dts[:, 3, 0:TH]).then_inc(final_inv, 1)
            dve.wait_ge(final_root, 1)
            r, t = dts[:, 1, 0:TH], dts[:, 4, 0:TH]
            link(dve.tensor_tensor(t, r, r, ALU.mult))
            link(dve.tensor_tensor(t, t, dts[:, 3, 0:TH], ALU.mult))
            link(dve.tensor_scalar(t, t, -0.5, 1.5, ALU.mult, ALU.add))
            link(dve.tensor_tensor(r, r, t, ALU.mult))
            for th in range(TH):
                y = cols(8192 + th * D, D)
                dve.scalar_tensor_tensor(out=y, in0=y, scalar=dts[:, 1, th:th + 1], in1=cols(TH * D, D),
                                         op0=ALU.mult, op1=ALU.mult).then_inc(final_ready, 1)


def slabs_of(w, tiles):
    return np.ascontiguousarray(w.reshape(NC, P, tiles, P).transpose(2, 1, 0, 3)).reshape(tiles, P, NC * P)


def kernel(**inputs):
    import concourse.bacc as bacc
    from concourse.bass_utils import run_bass_kernel_spmd

    a = {k: np.asarray(v) for k, v in inputs.items()}
    w_in = a["w_in"][0]
    main = IN_TILES * P
    wide = lambda row: np.broadcast_to(row, (P, row.shape[-1]))
    tiles = lambda v, n: v.reshape(n, P).T
    smalls = np.concatenate([
        tiles(a["attn_norm"][0], NC), tiles(a["ffn_norm"][0], NC),
        tiles(a["attn_out_norm"][0], 8), tiles(a["ssm_out_norm"][0], 8),
        a["conv_w"][0].reshape(CONV, CONV_TILES, P).transpose(2, 1, 0).reshape(P, CONV_TILES * CONV),
        tiles(a["conv_b"][0], CONV_TILES), wide(a["dt_bias"]), wide(a["a_log"]),
        tiles(np.repeat(a["d_skip"][0], HD), 8)], axis=1)
    arrays = {
        "x_t": a["x"][0].T.reshape(NC, P, T).transpose(1, 0, 2).reshape(P, NC * T),
        "w_in": slabs_of(w_in[:, :main], IN_TILES),
        "w_dt": w_in[:, main:].reshape(NC, P, SSM_HEADS).transpose(1, 0, 2).reshape(P, NC * SSM_HEADS),
        "w_out": slabs_of(a["w_out"][0], NC),
        "w_q": slabs_of(a["peer_wq"][0], NC),
        "subkeys": a["peer_subkeys"][0].transpose(3, 0, 1, 2).reshape(P, 2 * PH * KEYS),
        "u_tab": a["peer_u"][0].reshape(KEYS, KEYS, NC, P).transpose(0, 3, 2, 1).reshape(KEYS, P, D),
        "v_tab": a["peer_v"][0].reshape(KEYS, KEYS, D),
        "smalls_in": smalls,
        "rel_bias": a["rel_bias"],
        "selectors": bucket_selectors(),
        "final_gain": a["final_norm"],
    }
    nc = bacc.Bacc("TRN2", target_bir_lowering=False, num_devices=1)
    args, sent = [], {}
    for name, v in arrays.items():
        v = np.ascontiguousarray(v)
        sent["in_" + name] = v
        args.append(nc.dram_tensor("in_" + name, v.shape, mybir.dt.from_np(v.dtype), kind="ExternalInput").ap())
    out = nc.dram_tensor("out", (T, D), F32, kind="ExternalOutput").ap()
    layer(nc, *args, out)
    r = run_bass_kernel_spmd(nc, [sent], core_ids=[0])
    return r.results[0]["out"].reshape(1, T, D)
```

```python
from contextlib import ExitStack

import numpy as np

import concourse.bass as bass
from concourse import mybir

ALU = mybir.AluOpType
ACT = mybir.ActivationFunctionType
AX_X = mybir.AxisListType.X
F32 = mybir.dt.float32
F32R = mybir.dt.float32r
U32 = mybir.dt.uint32
I32 = mybir.dt.int32

P = 128
D = 2048
T = 256
TH = T // P
NC = D // P
HEADS = 8
BUCKETS = 32
MAX_DIST = 128
SSM_HEADS = 16
HD = 64
GROUPS = 2
CONV = 4
CONV_TILES = 12
KEYS = 128
PH = 8
TOP = 16
EPS = 1e-6
BIG = 1e30

XBC0, Q0, K0, V0, Z0 = 0, 12, 20, 28, 36
IN_TILES = 44
STAGES = {"in": IN_TILES, "out": NC, "q": NC, "u": KEYS, "v": KEYS}
PIECES = 4
PCOLS = NC * P // 2

XT, PROJ, CONVT, MIX, SCR = 0, 4096, 15360, 18432, 22528
ARENA = KEYS * T
XG = PROJ + 28 * T
WDT, RELB, SEL, BROW = SCR, SCR + 256, SCR + 512, SCR + 1024
XN, BN, XW, PREV = SCR, SCR + 2048, SCR + 2304, SCR + 3328
SEG, MT, CE, CB, BIAS = SCR + 4352, SCR + 5376, SCR + 6400, SCR + 7424, SCR + 7936
FACTOR0 = SCR + 9984
BIAS_UP = SEG
VN, SC0, SC1, PT = XN, XW, MIX, PROJ
MHI, MLO = PROJ, PROJ + 4096
X1T, SQ1, X1G = MIX, SCR, SCR + 4096
QT, SCORES, SUBK, X1 = PROJ, PROJ + 4096, XT, SCR
SCORES2, TOPV, TOPI, TOPIF, CAND, CAND2 = 12288, 12416, 12928, 13440, 13952, 18048
ONEHOT, PICKV, POS, POSF, KEEP = 2048, 27136, 27392, 27648, 28160

G1, G2, GMIX, CONVW, CONVB, DTB, ALOG, DSK = 0, 16, 32, 48, 96, 108, 124, 140
SMALLS = 148

SSD_AT, SSD_STEP = 26, 7
SCORES_AT, EXP_AT, PROBS_AT, VT_AT, PT_AT, ATT_AT = 58, 67, 74, 74, 78, 82
TOP_AT = 7
GATES_AT = 25
NG = T // 8


def bucket_selectors():
    n = (T - 1) - np.arange(T + P - 1)
    exact = BUCKETS // 2
    nf = np.maximum(n, 1).astype(np.float32)
    large = exact + (np.log(nf / np.float32(exact)) / np.float32(np.log(MAX_DIST / exact))
                     * np.float32(BUCKETS - exact)).astype(np.int32)
    bucket = np.where(n < exact, np.maximum(n, 0), np.minimum(large, BUCKETS - 1))
    bucket = np.where(n < 0, BUCKETS, bucket)
    return (bucket[None, :] == np.arange(BUCKETS + 1)[:, None]).astype(np.float32)


def layer(nc, x_t, w_in, w_dt, w_out, w_q, subkeys, u_tab, v_tab, smalls_in, rel_bias,
          selectors, final_gain, out):
    scratch_bias = nc.dram_tensor("scratch_bias", (HEADS, T + P - 1), F32, kind="Internal").ap()
    scratch_x1 = nc.dram_tensor("scratch_x1", (P, TH * D), F32, kind="Internal").ap()
    scratch_h = nc.dram_tensor("scratch_h", (KEYS, P, T), F32, kind="Internal").ap()
    stage_src = {"in": w_in, "out": w_out, "q": w_q, "u": u_tab, "v": v_tab}
    base, at = {}, 0
    for name, slabs in STAGES.items():
        base[name] = at
        at += 2 * slabs

    ctx = ExitStack()
    with ctx:
        def sb(name, shape, dt=F32):
            return ctx.enter_context(nc.sbuf_tensor(name, shape, dt))

        def sem(name):
            return ctx.enter_context(nc.semaphore(name))

        arena = sb("arena", [P, ARENA])
        arena_at = nc.sbuf_base - 4 * ARENA
        m_hi = nc.alloc_sbuf_tensor_at("m_hi", [P, NC, T], F32R, offset=arena_at + 4 * MHI)
        m_lo = nc.alloc_sbuf_tensor_at("m_lo", [P, NC, T], F32R, offset=arena_at + 4 * MLO)
        x_hi = sb("x_hi", [P, NC, T], F32R)
        x_lo = sb("x_lo", [P, NC, T], F32R)
        raw = sb("raw", [P, PIECES, PCOLS])
        w_hi = sb("w_hi", [P, 2, PCOLS], F32R)
        w_lo = sb("w_lo", [P, 2, PCOLS], F32R)
        aux = sb("aux", [P, 512])
        tri, future, flip, ones = (aux[:, n * P:(n + 1) * P] for n in range(4))
        gelu_out, factor2 = aux[:, 0:T], aux[:, T:2 * T]
        ident = sb("ident", [P, P])
        iota_f = sb("iota_f", [P, P])
        smalls = sb("smalls", [P, SMALLS])
        dts = sb("dts", [P, 9, 32])
        route = sb("route", [P, 3, T])
        hot1 = sb("hot1", [P, 8, KEYS])
        hot2 = sb("hot2", [P, 8, KEYS])
        ps = ctx.enter_context(nc.psum_tensor("ps", [P, 8, 512], F32))
        h_in = hot1[:, 0:4, :].rearrange("p (a b) k -> p a (b k)", a=2)
        act_f = hot2[:, 0:4, :].rearrange("p (a b) k -> p a (b k)", a=2)

        def cols(a, n, m=None):
            v = arena[:, a:a + n]
            return v if m is None else v.rearrange("p (a b) -> p a b", b=m)

        xt, xg = cols(XT, 4096, T), cols(XG, 4096, T)
        proj = cols(PROJ, IN_TILES * T, T)
        convt = cols(CONVT, CONV_TILES * T, T)
        mix = cols(MIX, 4096, T)
        x1t, sq1 = cols(X1T, 4096, T), cols(SQ1, 4096, T)
        qt = cols(QT, 4096, T)
        G = arena[:, :].rearrange("p (i t) -> p i t", t=T)
        G_by_token = arena[:, :].rearrange("p (i g k) -> p g k i", g=NG, k=8)
        x_hi_f, x_lo_f, m_hi_f = (v[:, :, :].bitcast(F32) for v in (x_hi, x_lo, m_hi))
        flat = ps[:, :, :].rearrange("p b n -> p (b n)")
        A, B, C = 1024, 2048, 3072

        x_landed = [sem(f"x_landed{n}") for n in range(4)]
        smalls_landed = sem("smalls_landed")
        wdt_landed = sem("wdt_landed")
        bias_in_landed = sem("bias_in_landed")
        raw_landed = [sem(f"raw_landed{n}") for n in range(PIECES)]
        bias_staged = sem("bias_staged")
        bias_out = sem("bias_out")
        bias_landed = sem("bias_landed")
        bias_flipped = sem("bias_flipped")
        bias_copied = sem("bias_copied")
        sub_landed = sem("sub_landed")
        hi_ready = sem("hi_ready")
        lo_ready = sem("lo_ready")
        w_hi_used = sem("w_hi_used")
        w_used = sem("w_used")
        evacuated = sem("evacuated")
        pool_chain = sem("pool_chain")
        consts_ready = sem("consts_ready")
        xg_ready = sem("xg_ready")
        sq_ready = sem("sq_ready")
        ssq_ready = sem("ssq_ready")
        mean_ready = sem("mean_ready")
        ln_ready = sem("ln_ready")
        root_ready = sem("root_ready")
        factor_ready = sem("factor_ready")
        x_hi_ready = sem("x_hi_ready")
        x_lo_ready = sem("x_lo_ready")
        normed = sem("normed")
        m_hi_ready = sem("m_hi_ready")
        m_lo_ready = sem("m_lo_ready")
        dve_chain = sem("dve_chain")
        bias_row = sem("bias_row")
        vt_ready = sem("vt_ready")
        v_copied = sem("v_copied")
        qk_ready = sem("qk_ready")
        negmax_ready = sem("negmax_ready")
        exp_ready = sem("exp_ready")
        probs_ready = sem("probs_ready")
        pt_ready = sem("pt_ready")
        pt_copied = sem("pt_copied")
        att_ready = sem("att_ready")
        att_copied = sem("att_copied")
        dtraw_ready = sem("dtraw_ready")
        factor_t_ready = sem("factor_t_ready")
        dt_step = sem("dt_step")
        dt_act = sem("dt_act")
        da_ready = sem("da_ready")
        cs_ready = sem("cs_ready")
        conv_step = sem("conv_step")
        conv_ready = sem("conv_ready")
        silu_ready = sem("silu_ready")
        skip_ready = sem("skip_ready")
        xs_t_ready = sem("xs_t_ready")
        xs_copied = sem("xs_copied")
        bc_ready = sem("bc_ready")
        bc_copied = sem("bc_copied")
        w0_ready = sem("w0_ready")
        xw_ready = sem("xw_ready")
        state_ready = sem("state_ready")
        state_copied = sem("state_copied")
        csb_ready = sem("csb_ready")
        csb_read = sem("csb_read")
        seg_ready = sem("seg_ready")
        decay_ready = sem("decay_ready")
        grow_ready = sem("grow_ready")
        grown = sem("grown")
        m_ready = sem("m_ready")
        y_ready = sem("y_ready")
        y_added = sem("y_added")
        zsilu_ready = sem("zsilu_ready")
        gated_y = sem("gated_y")
        x1_ready = sem("x1_ready")
        x1g_ready = sem("x1g_ready")
        side_ready = sem("side_ready")
        side_copied = sem("side_copied")
        x1_saved = sem("x1_saved")
        gate_sub = sem("gate_sub")
        gate_exp = sem("gate_exp")
        picks_ready = sem("picks_ready")
        picks_t_ready = sem("picks_t_ready")
        route_ready = sem("route_ready")
        scaled = sem("scaled")
        gelu_done = sem("gelu_done")
        h_stored = sem("h_stored")
        hot1_ready = sem("hot1_ready")
        hot2_ready = sem("hot2_ready")
        weighed = sem("weighed")
        gates_ready = sem("gates_ready")
        gates_copied = sem("gates_copied")
        h_landed = [sem(f"h_landed{n}") for n in range(2)]
        acted = sem("acted")
        a_hi_ready = sem("a_hi_ready")
        a_lo_ready = sem("a_lo_ready")
        tail_landed = sem("tail_landed")
        final_y = sem("final_y")
        final_sq = sem("final_sq")
        final_mean = sem("final_mean")
        final_ln = sem("final_ln")
        final_root = sem("final_root")
        final_ready = sem("final_ready")
        stored = sem("stored")

        def linker(eng, chain):
            n = [0]

            def chained(ins):
                n[0] += 1
                ins.then_inc(chain, 1)

            def settle():
                eng.wait_ge(chain, n[0])

            def link(ins):
                chained(ins)
                settle()
            return link, chained, settle

        def pairs(eng, pair, first, end):
            if first == 0:
                pair(0)
                first = 1
            if end - first > 1:
                with eng.Fori(first, end) as i:
                    pair(i)
            elif end > first:
                pair(first)

        block = ctx.enter_context(nc.Block())

        @block.sync
        def _(sp):
            def load(src, slab, u):
                sp.dma_start(raw[:, u, :], src[slab, :, (u % 2) * PCOLS:(u % 2 + 1) * PCOLS]) \
                  .then_inc(raw_landed[u], 16)

            for n in range(4):
                sp.dma_start(cols(XT + n * 1024, 1024), x_t[:, n * 1024:(n + 1) * 1024]).then_inc(x_landed[n], 16)
                load(w_in, n // 2, n)
            for name, slabs in STAGES.items():
                src = stage_src[name]
                if name in "uv":
                    break
                with sp.Fori(1 if name == "in" else 0, slabs // 2) as i:
                    for u in range(PIECES):
                        sp.wait_ge(lo_ready, i * PIECES + (base[name] + u - PIECES + 1))
                        load(src, i * 2 + u // 2, u)

            def store_h(s):
                sp.wait_ge(evacuated, s + (IN_TILES + 2 * NC + 1))
                sp.dma_start(scratch_h[s], gelu_out).then_inc(h_stored, 16)

            def u_pair(i):
                for u in range(PIECES):
                    sp.wait_ge(lo_ready, i * PIECES + (base["u"] + u - PIECES + 1))
                    load(u_tab, i * 2 + u // 2, u)
                    if u % 2 and not (isinstance(i, int) and i * 2 + u // 2 < 3):
                        store_h(i * 2 + (u // 2 - 3))
            u_pair(0)
            u_pair(1)
            pairs(sp, u_pair, 2, KEYS // 2)

            def load_h(n, a):
                sp.dma_start(h_in[:, a, :], scratch_h[n]).then_inc(h_landed[a], 16)

            for u in range(PIECES):
                sp.wait_ge(lo_ready, base["v"] + u - PIECES + 1)
                load(v_tab, u // 2, u)
                if u % 2:
                    store_h(KEYS - 3 + u // 2)
            store_h(KEYS - 1)
            sp.wait_ge(h_stored, 16 * KEYS)
            sp.wait_ge(gates_ready, NG)
            for a in range(2):
                load_h(a, a)
            with sp.Fori(1, KEYS // 2) as i:
                for u in range(PIECES):
                    sp.wait_ge(lo_ready, i * PIECES + (base["v"] + u - PIECES + 1))
                    load(v_tab, i * 2 + u // 2, u)
                    if u % 2:
                        sp.wait_ge(acted, i * 2 + (u // 2 - 1))
                        load_h(i * 2 + u // 2, u // 2)
            for th in range(TH):
                sp.wait_ge(final_ready, th + 1)
                sp.dma_start(out[th * P:(th + 1) * P, :], cols(8192 + th * D, D)).then_inc(stored, 16)
            sp.wait_ge(stored, 16 * TH)

        @block.gpsimd
        def _(pool):
            link, _, _ = linker(pool, pool_chain)
            pool.memset(ones, 1.0).then_inc(consts_ready, 1)
            link(pool.memset(ident[:, :], 0.0))
            pool.affine_select(out=ident[:, :], in_=ident[:, :], compare_op=ALU.not_equal, fill=1.0,
                               base=0, pattern=[[-1, P]], channel_multiplier=1).then_inc(consts_ready, 1)
            link(pool.memset(tri, 1.0))
            pool.affine_select(out=tri, in_=tri, compare_op=ALU.is_ge, fill=0.0,
                               base=0, pattern=[[1, P]], channel_multiplier=-1).then_inc(consts_ready, 1)
            link(pool.memset(future, 0.0))
            pool.affine_select(out=future, in_=future, compare_op=ALU.is_ge, fill=-BIG,
                               base=0, pattern=[[1, P]], channel_multiplier=-1).then_inc(consts_ready, 1)
            link(pool.iota(hot1[:, 0, :].bitcast(I32), pattern=[[1, P]], base=0, channel_multiplier=0))
            pool.tensor_copy(iota_f[:, :], hot1[:, 0, :].bitcast(I32)).then_inc(consts_ready, 1)
            link(pool.memset(flip, 0.0))
            pool.affine_select(out=flip, in_=flip, compare_op=ALU.not_equal, fill=1.0,
                               base=1 - P, pattern=[[1, P]], channel_multiplier=1).then_inc(consts_ready, 1)

            pool.wait_ge(bias_staged, 1)
            pool.dma_start(scratch_bias, cols(BROW, T + P - 1)[0:HEADS, :]).then_inc(bias_out, 16)
            pool.wait_ge(bias_out, 16)
            toeplitz = bass.AP(tensor=scratch_bias.tensor, offset=0,
                               ap=[[1, P], [T + P - 1, HEADS], [1, T]])
            pool.dma_start(cols(BIAS_UP, HEADS * T, T), toeplitz).then_inc(bias_landed, 16)

            pool.wait_ge(xs_copied, 1)
            pool.wait_ge(w0_ready, 1)
            pool.tensor_tensor(cols(XW, 1024, HD), cols(XN, 1024, HD),
                               dts[:, 4, 0:16].unsqueeze(2).broadcast_to([P, 16, HD]), ALU.mult) \
                .then_inc(xw_ready, 1)
            pool.wait_ge(ssq_ready, 1)
            pool.tensor_tensor(mix[:, 8:16, :], convt[:, 0:8, :],
                               smalls[:, DSK:DSK + 8].unsqueeze(2).broadcast_to([P, 8, T]), ALU.mult) \
                .then_inc(skip_ready, 1)

            pool.wait_ge(evacuated, IN_TILES + NC)
            pool.dma_start(cols(SUBK, 2048), subkeys).then_inc(sub_landed, 16)
            pool.wait_ge(side_copied, 8)
            pool.dma_start(scratch_x1, cols(X1, TH * D)).then_inc(x1_saved, 16)

            def weigh(g, ready):
                pool.wait_ge(hot2_ready, ready)
                pool.tensor_tensor(hot2[:, :, :], hot2[:, :, :],
                                   route[:, 2, :].rearrange("p (g k) -> p g k", k=8)[:, g, :]
                                   .unsqueeze(2).broadcast_to([P, 8, KEYS]), ALU.mult).then_inc(weighed, 1)

            weigh(0, 1)
            with pool.Fori(1, NG) as g:
                weigh(g, g + 1)
            pool.wait_ge(acted, 40)
            pool.wait_ge(x1_saved, 16)
            pool.dma_start(cols(0, TH * D), scratch_x1).then_inc(tail_landed, 16)
            pool.dma_start(cols(TH * D, D), final_gain.partition_broadcast(P)).then_inc(tail_landed, 16)

        @block.scalar
        def _(act):
            def hi(b, i, u):
                act.wait_ge(raw_landed[u], i * 16 + 16 * (b // PIECES + 1))
                if not (isinstance(i, int) and b + i * PIECES + u < 2):
                    act.wait_ge(w_hi_used, i * PIECES + (b + u - 1))
                    act.wait_ge(lo_ready, i * PIECES + (b + u - 1))
                act.activation(w_hi[:, u % 2, :], raw[:, u, :], ACT.Copy).then_inc(hi_ready, 1)

            def root(k, v, r):
                act.wait_ge(mean_ready, k + 1)
                act.activation(r, v, ACT.Ln).then_inc(ln_ready, 1)
                act.wait_ge(ln_ready, k + 1)
                act.activation(r, r, ACT.Exp, scale=-0.5).then_inc(root_ready, 1)

            act.dma_start(smalls[:, :], smalls_in).then_inc(smalls_landed, 16)
            act.dma_start(cols(WDT, 256), w_dt).then_inc(wdt_landed, 16)
            act.dma_start(cols(RELB, 8)[0:BUCKETS, :], rel_bias).then_inc(bias_in_landed, 16)
            act.dma_start(cols(SEL, T + P - 1)[0:BUCKETS + 1, :], selectors).then_inc(bias_in_landed, 16)

            b = base["in"]
            for n in range(2):
                hi(b, 0, n)
            for n in range(4):
                act.wait_ge(xg_ready, n + 1)
                act.activation(x_hi[:, 4 * n:4 * n + 4, :], xg[:, 4 * n:4 * n + 4, :], ACT.Copy) \
                   .then_inc(x_hi_ready, 1)
            for n in range(4):
                act.activation(cols(MIX + n * 1024, 1024), cols(XT + n * 1024, 1024), ACT.Square) \
                   .then_inc(sq_ready, 1)
            root(0, cols(CE, T), cols(FACTOR0, T))

            for p in range(2, 2 * IN_TILES):
                hi(b, p // PIECES, p % PIECES)
                if p == 6:
                    act.wait_ge(dt_step, 1)
                    act.activation(dts[:, 2, :], dts[:, 1, :], ACT.Exp, scale=-1.0).then_inc(dt_act, 1)
                    act.activation(dts[:, 6, 0:16], smalls[:, ALOG:ALOG + 16], ACT.Exp).then_inc(dt_act, 1)
                if p == 8:
                    act.wait_ge(dt_step, 2)
                    act.activation(dts[:, 4, :], dts[:, 3, :], ACT.Ln).then_inc(dt_act, 1)
                if p in (18, 20):
                    n = (p - 18) // 2
                    act.wait_ge(bias_flipped, n + 1)
                    act.activation(cols(BIAS + n * 1024, 1024), flat[:, C:C + 1024], ACT.Copy).then_inc(bias_copied, 1)
                if p == 22:
                    act.wait_ge(dt_step, 3)
                    act.activation(dts[:, 4, 0:16], dts[:, 4, 0:16], ACT.Exp).then_inc(dt_act, 1)
                if p in (23, 25, 28):
                    t0, t1 = {23: (0, 8), 25: (8, 10), 28: (10, 12)}[p]
                    act.wait_ge(conv_ready, t1)
                    act.activation(convt[:, t0:t1, :], convt[:, t0:t1, :], ACT.Silu).then_inc(silu_ready, 1)
                if p in (26, 27):
                    n = p - 26
                    act.wait_ge(xs_t_ready, n + 1)
                    act.activation(cols(XN + n * 1024, 1024), flat[:, (A, B)[n]:(A, B)[n] + 1024], ACT.Copy) \
                       .then_inc(xs_copied, 1)
                if p == 32:
                    act.wait_ge(bc_ready, 1)
                    act.activation(cols(BN, 256), flat[:, C:C + 256], ACT.Copy).then_inc(bc_copied, 1)
                    act.activation(cols(CB, 512), flat[:, C + 512:C + 1024], ACT.Copy).then_inc(bc_copied, 1)
                if p == 36:
                    act.wait_ge(state_ready, 1)
                    act.activation(cols(PREV, 1024), flat[:, B:B + 1024], ACT.Copy).then_inc(state_copied, 1)
                n, at = (p - SSD_AT) // SSD_STEP, (p - SSD_AT) % SSD_STEP
                if n in (2, 3) and at == 3:
                    act.wait_ge(csb_read, n + 1)
                    if n == 3:
                        act.wait_ge(y_ready, 3)
                    act.activation(cols(CE, 1024), flat[:, A:A + 1024], ACT.Exp).then_inc(grow_ready, 1)
                if 0 <= n < 4 and at == 5:
                    act.wait_ge(seg_ready, n + 1)
                    act.activation(cols(SEG, 1024), cols(SEG, 1024), ACT.Exp).then_inc(decay_ready, 1)
                if EXP_AT <= p < EXP_AT + 6:
                    for n in range(3 * (p - EXP_AT), min(3 * (p - EXP_AT) + 3, 2 * HEADS)):
                        act.wait_ge(negmax_ready, 1)
                        s = cols(SC0, 1024, P)[:, n, :] if n < HEADS else cols(SC1, 2048, T)[:, n - HEADS, :]
                        act.activation(s, s, ACT.Exp, bias=dts[:, 2, n:n + 1],
                                       accum_out=dts[:, 3, n:n + 1]).then_inc(exp_ready, 1)
                if p in (VT_AT + 2, VT_AT + 3):
                    n = p - VT_AT - 2
                    act.wait_ge(vt_ready, n + 1)
                    act.activation(cols(VN + n * 1024, 1024), flat[:, (A, B)[n]:(A, B)[n] + 1024], ACT.Copy) \
                       .then_inc(v_copied, 1)
                if PT_AT + 2 <= p < PT_AT + 5:
                    n = p - PT_AT - 2
                    act.wait_ge(pt_ready, n + 1)
                    act.activation(cols(PT + n * 1024, 1024), flat[:, (A, B, C)[n]:(A, B, C)[n] + 1024], ACT.Copy) \
                       .then_inc(pt_copied, 1)
                if p in (ATT_AT + 1, ATT_AT + 2):
                    n = p - ATT_AT - 1
                    act.wait_ge(att_ready, n + 1)
                    act.activation(cols(MIX + n * 1024, 1024), flat[:, (A, B)[n]:(A, B)[n] + 1024], ACT.Copy) \
                       .then_inc(att_copied, 1)
                    act.activation(cols(CONVT + n * 1024, 1024), flat[:, (A, B)[n]:(A, B)[n] + 1024], ACT.Square) \
                       .then_inc(sq_ready, 1)
                if p == ATT_AT + 3:
                    act.wait_ge(evacuated, Z0 + 4)
                    act.activation(proj[:, Z0:Z0 + 4, :], proj[:, Z0:Z0 + 4, :], ACT.Silu).then_inc(zsilu_ready, 1)

            def square_y(g):
                act.wait_ge(gated_y, g + 1)
                dst = cols(CONVT + (2048 if g == 0 else 0), 1024)
                if g == 1:
                    act.wait_ge(ssq_ready, 2)
                act.activation(dst, cols(MIX + 2048 + g * 1024, 1024), ACT.Square).then_inc(sq_ready, 1)

            def m_upper(c0, c1, k):
                act.wait_ge(normed, k)
                act.activation(m_hi[:, c0:c1, :], mix[:, c0:c1, :], ACT.Copy).then_inc(m_hi_ready, 1)

            square_y(0)
            b = base["out"]
            for u in range(2):
                hi(b, 0, u)
            root(1, cols(SEG, T), cols(MT, T))
            act.wait_ge(evacuated, IN_TILES)
            act.activation(proj[:, Z0 + 4:Z0 + 8, :], proj[:, Z0 + 4:Z0 + 8, :], ACT.Silu).then_inc(zsilu_ready, 1)
            square_y(1)
            m_upper(0, 8, 1)
            root(2, cols(SEG + T, T), cols(MT + T, T))
            m_upper(8, 12, 2)
            root(3, cols(SEG + 2 * T, T), cols(MT + 2 * T, T))
            m_upper(12, 16, 3)

            def take_x1(s, ring):
                act.wait_ge(x1g_ready, s + 1)
                act.activation(x_hi[:, s, :], cols(X1G + ring * T, T), ACT.Copy).then_inc(x_hi_ready, 1)
                act.activation(sq1[:, s, :], x1t[:, s, :], ACT.Square).then_inc(sq_ready, 1)

            def out_pair(i):
                for u in range(PIECES):
                    if isinstance(i, int) and i == 0 and u < 2:
                        continue
                    hi(b, i, u)
                    if isinstance(i, int) and i == 0 and u == 3:
                        take_x1(0, 0)
                    elif u % 2 and not (isinstance(i, int) and i == 0):
                        take_x1(i * 2 + (u // 2 - 1), (u // 2 + 1) % 2)
            pairs(act, out_pair, 0, NC // 2)

            b = base["q"]
            for u in range(2):
                hi(b, 0, u)
            take_x1(NC - 1, 1)
            root(4, cols(CAND, T), factor2)
            for u in range(2, PIECES):
                hi(b, 0, u)

            def plain_pair(i):
                for u in range(PIECES):
                    hi(b, i, u)
            pairs(act, plain_pair, 1, NC // 2)

            def gelu(s, bank):
                act.wait_ge(scaled, s + 1)
                if not (isinstance(s, int) and s == 0):
                    act.wait_ge(h_stored, s * 16)
                act.activation(gelu_out, ps[:, bank, 0:T], ACT.Gelu).then_inc(evacuated, 1)

            b = base["u"]

            def u_piece(i, u):
                hi(b, i, u)
                if u % 2 == 0 and not (isinstance(i, int) and i == 0):
                    gelu(i * 2 + (u // 2 - 2), u // 2)

            for p in range(16):
                u_piece(p // PIECES, p % PIECES)
                if 5 <= p < 13:
                    n = p - 5
                    dst = (SCORES if n < 4 else X1) + n % 4 * 1024
                    act.wait_ge(side_ready, n + 1)
                    act.activation(cols(dst, 1024), flat[:, (A, B, C)[n % 3]:(A, B, C)[n % 3] + 1024], ACT.Copy) \
                       .then_inc(side_copied, 1)

            def u_pair(i):
                for u in range(PIECES):
                    u_piece(i, u)
            pairs(act, u_pair, 4, GATES_AT - 1)
            for u in range(PIECES):
                u_piece(GATES_AT - 1, u)
                if u == 0:
                    act.wait_ge(gate_sub, 1)
                    act.activation(cols(PICKV, 256), cols(PICKV, 256), ACT.Exp).then_inc(gate_exp, 1)
                if u == 3:
                    act.wait_ge(picks_t_ready, 1)
                    act.activation(route[:, :, :], flat[:, A:A + 768].rearrange("p (a b) -> p a b", b=T),
                                   ACT.Copy).then_inc(route_ready, 1)
            u_pair(GATES_AT)
            act.wait_ge(x1_saved, 16)
            with act.Fori(GATES_AT + 1, GATES_AT + 1 + NG) as i:
                for u in range(PIECES):
                    u_piece(i, u)
                    if u == 2:
                        act.wait_ge(gates_ready, i - GATES_AT)
                        act.activation(G_by_token[:, i - (GATES_AT + 1), :, :],
                                       flat[:, A:A + 1024].rearrange("p (k i) -> p k i", i=KEYS), ACT.Copy) \
                           .then_inc(gates_copied, 1)
            pairs(act, u_pair, GATES_AT + 1 + NG, KEYS // 2)

            b = base["v"]

            def v_pair(i):
                for u in range(PIECES):
                    hi(b, i, u)
                    if u % 2 == 0:
                        act.wait_ge(acted, i * 2 + (u // 2 + 1))
                        act.wait_ge(w_used, i * PIECES + (b + u - 2))
                        act.activation(x_hi[:, u // 2, :], act_f[:, u // 2, :], ACT.Copy).then_inc(a_hi_ready, 1)
            for n in range(2):
                hi(b, 0, n)
                gelu(KEYS - 2 + n, n)
            for n in range(2):
                act.wait_ge(acted, n + 1)
                act.wait_ge(w_used, b)
                act.activation(x_hi[:, n, :], act_f[:, n, :], ACT.Copy).then_inc(a_hi_ready, 1)
            hi(b, 0, 2)
            hi(b, 0, 3)
            pairs(act, v_pair, 1, KEYS // 2)

            for th in range(TH):
                act.wait_ge(final_y, th + 1)
                act.activation(cols(16384 + th * D, D), cols(8192 + th * D, D), ACT.Square,
                               accum_out=dts[:, 2, th:th + 1]).then_inc(final_sq, 1)
            act.wait_ge(final_mean, 1)
            act.activation(dts[:, 1, 0:TH], dts[:, 3, 0:TH], ACT.Ln).then_inc(final_ln, 1)
            act.wait_ge(final_ln, 1)
            act.activation(dts[:, 1, 0:TH], dts[:, 1, 0:TH], ACT.Exp, scale=-0.5).then_inc(final_root, 1)

        @block.tensor
        def _(pe):
            def ssq(need, tiles, dst):
                pe.wait_ge(sq_ready, need)
                for c, tile in enumerate(tiles):
                    last = pe.matmul(dst, ones, tile, start=(c == 0), stop=(c == len(tiles) - 1))
                last.then_inc(ssq_ready, 1)

            def piece(b, i, u, xh, xl):
                first = isinstance(i, int) and b == 0 and i == 0
                if u % 2 == 0 and not first:
                    pe.wait_ge(evacuated, i * 2 + (b // 2 + u // 2 - 1))
                pe.wait_ge(hi_ready, i * PIECES + (b + u + 1))
                dst = ps[:, u // 2, 0:T]
                c0 = (u % 2) * (NC // 2)
                for c in range(NC // 2):
                    wh = w_hi[:, u % 2, c * P:(c + 1) * P]
                    pe.matmul(dst, wh, xh[:, c0 + c, :], start=(c0 + c == 0), stop=False)
                    last = pe.matmul(dst, wh, xl[:, c0 + c, :], start=False, stop=False)
                last.then_inc(w_hi_used, 1)
                pe.wait_ge(lo_ready, i * PIECES + (b + u + 1))
                for c in range(NC // 2):
                    last = pe.matmul(dst, w_lo[:, u % 2, c * P:(c + 1) * P], xh[:, c0 + c, :],
                                     start=False, stop=(c0 + c == NC - 1))
                last.then_inc(w_used, 1)

            b = base["in"]

            def in_piece(p):
                piece(b, p // PIECES, p % PIECES, x_hi, x_lo)

            def in_to(p0, p1):
                while p0 < p1 and p0 % PIECES:
                    in_piece(p0)
                    p0 += 1
                whole = (p1 - p0) // PIECES
                if whole > 0:
                    def one(i):
                        for u in range(PIECES):
                            piece(b, i, u, x_hi, x_lo)
                    pairs(pe, one, p0 // PIECES, p0 // PIECES + whole)
                    p0 += whole * PIECES
                for p in range(p0, p1):
                    in_piece(p)

            pe.wait_ge(consts_ready, 6)
            pe.wait_ge(x_lo_ready, 2)
            in_piece(0)
            pe.wait_ge(x_lo_ready, 4)
            in_piece(1)
            ssq(4, [mix[:, c, :] for c in range(NC)], flat[:, A:A + T])
            pe.wait_ge(bias_row, 1)
            pe.matmul(ps[0:HEADS, 3, 0:T + P - 1], cols(RELB, 8)[0:BUCKETS + 1, :],
                      cols(SEL, T + P - 1)[0:BUCKETS + 1, :], start=True, stop=True).then_inc(bias_row, 1)
            in_to(2, 4)
            pe.wait_ge(wdt_landed, 16)
            wdt = cols(WDT, 256, 16)
            for th in range(TH):
                dst = flat[:, B + th * 16:B + th * 16 + 16]
                for c in range(NC):
                    for n, half in enumerate((x_hi_f, x_lo_f)):
                        last = pe.matmul(dst, half[:, c, th * P:(th + 1) * P], wdt[:, c, :],
                                         start=(c == 0 and n == 0), stop=(c == NC - 1 and n == 1))
            last.then_inc(dtraw_ready, 1)
            pe.wait_ge(factor_ready, 1)
            for th in range(TH):
                last = pe.transpose(flat[:, B + 512 + th * P:B + 512 + (th + 1) * P],
                                    cols(FACTOR0 + th * P, P), ident[:, :])
            last.then_inc(factor_t_ready, 1)
            in_to(4, 16)
            pe.wait_ge(da_ready, 1)
            pe.matmul(flat[:, B + 64:B + 96], tri, dts[:, 5, :], start=True, stop=True)
            pe.matmul(flat[:, B + 96:B + 112], ones, dts[:, 5, 0:16], start=True, stop=True) \
              .then_inc(cs_ready, 1)
            pe.wait_ge(bias_landed, 16)
            for n in range(2):
                if n:
                    in_to(16, 19)
                    pe.wait_ge(bias_copied, 1)
                for m in range(2):
                    last = pe.matmul(flat[:, C + m * 512:C + (m + 1) * 512], flip,
                                     cols(BIAS_UP + n * 1024 + m * 512, 512), start=True, stop=True)
                last.then_inc(bias_flipped, 1)
            in_to(19, 25)
            pe.wait_ge(silu_ready, 1)
            pe.wait_ge(dt_step, 3)
            pe.wait_ge(bias_staged, 1)
            for ch in range(2):
                for j in range(8):
                    last = pe.transpose(flat[:, (A, B)[ch] + j * P:(A, B)[ch] + (j + 1) * P],
                                        convt[:, j, ch * P:(ch + 1) * P], ident[:, :])
                last.then_inc(xs_t_ready, 1)

            def running(n):
                ch, g = n // 2, n % 2
                if n:
                    pe.wait_ge(csb_read, n)
                if n == 3:
                    pe.wait_ge(grow_ready, 1)
                for r in range(8):
                    h = ch * 16 + g * 8 + r
                    last = pe.matmul(flat[:, A + r * P:A + (r + 1) * P], dts[:, 5, h:h + 1].broadcast_to([P, P]),
                                     tri, start=True, stop=True)
                last.then_inc(csb_ready, 1)

            def b_and_cb():
                pe.wait_ge(silu_ready, 3)
                pe.wait_ge(bias_copied, 2)
                for g in range(GROUPS):
                    pe.transpose(flat[:, C + g * P:C + (g + 1) * P], convt[:, 8 + g, 0:P], ident[:, :])
                for n in range(4):
                    tok = slice(n // 2 * P, (n // 2 + 1) * P)
                    last = pe.matmul(flat[:, C + 512 + n * P:C + 512 + (n + 1) * P], convt[:, 8 + n % 2, tok],
                                     convt[:, 10 + n % 2, tok], start=True, stop=True)
                last.then_inc(bc_ready, 1)

            def state():
                pe.wait_ge(xw_ready, 1)
                pe.wait_ge(bc_copied, 1)
                pe.wait_ge(xs_copied, 2)
                for g in range(GROUPS):
                    last = pe.matmul(flat[:, B + g * 512:B + (g + 1) * 512], cols(BN, 256, P)[:, g, :],
                                     cols(XW + g * 512, 512), start=True, stop=True)
                last.then_inc(state_ready, 1)

            def outputs(n):
                ch, g = n // 2, n % 2
                pe.wait_ge(m_ready, n + 1)
                pe.wait_ge(bc_copied, 2)
                if ch == 1:
                    pe.wait_ge(state_copied, 1)
                if n >= 2:
                    pe.wait_ge(y_added, n - 1)
                for r in range(8):
                    head = g * 8 + r
                    rows = slice((r % 2) * HD, (r % 2 + 1) * HD)
                    dst = ps[rows, 6 + n % 2, (r // 2) * P:(r // 2 + 1) * P]
                    last = pe.matmul(dst, cols(XN + ch * 1024 + head * HD, HD), cols(MT + r * P, P),
                                     start=True, stop=(ch == 0))
                    if ch == 1:
                        last = pe.matmul(dst, cols(PREV + head * HD, HD), cols(CE + r * P, P),
                                         start=False, stop=True)
                last.then_inc(y_ready, 1)

            done = 25
            in_to(done, SSD_AT + 2)
            done = SSD_AT + 2
            pe.wait_ge(xs_copied, 1)
            running(0)
            in_to(done, 31)
            b_and_cb()
            in_to(31, 34)
            running(1)
            state()
            in_to(34, 36)
            outputs(0)
            in_to(36, 41)
            running(2)
            in_to(41, 43)
            outputs(1)
            in_to(43, 48)
            running(3)
            in_to(48, 50)
            outputs(2)
            in_to(50, 57)
            outputs(3)
            in_to(57, SCORES_AT + 1)
            pe.wait_ge(evacuated, V0)
            pe.wait_ge(y_added, 4)
            for h in range(HEADS):
                last = pe.matmul(flat[:, A + h * T:A + (h + 1) * T], proj[:, Q0 + h, P:T], proj[:, K0 + h, :],
                                 start=True, stop=True)
            last.then_inc(qk_ready, 1)
            in_to(SCORES_AT + 1, SCORES_AT + 2)
            for h in range(HEADS):
                last = pe.matmul(flat[:, C + h * P:C + (h + 1) * P], proj[:, Q0 + h, 0:P],
                                 proj[:, K0 + h, 0:P], start=True, stop=True)
            last.then_inc(qk_ready, 1)
            in_to(SCORES_AT + 2, VT_AT + 1)
            pe.wait_ge(evacuated, Z0)
            pe.wait_ge(negmax_ready, 1)
            for sc in range(TH):
                for h in range(HEADS):
                    last = pe.transpose(flat[:, (A, B)[sc] + h * P:(A, B)[sc] + (h + 1) * P],
                                        proj[:, V0 + h, sc * P:(sc + 1) * P], ident[:, :])
                last.then_inc(vt_ready, 1)
            in_to(VT_AT + 1, PT_AT + 1)
            pe.wait_ge(probs_ready, 1)
            pe.wait_ge(v_copied, 2)
            for n in range(24):
                if n < HEADS:
                    src = cols(SC0, 1024, P)[:, n, :]
                else:
                    h, sc = (n - HEADS) // 2, (n - HEADS) % 2
                    src = cols(SC1, 2048, T)[:, h, sc * P:(sc + 1) * P]
                last = pe.transpose(flat[:, A + n * P:A + (n + 1) * P], src, ident[:, :])
                if n % 8 == 7:
                    last.then_inc(pt_ready, 1)
            in_to(PT_AT + 1, ATT_AT + 1)
            pe.wait_ge(pt_copied, 3)
            pt = cols(PT, 3072, P)
            vn = cols(VN, 2048, P)
            for h in range(HEADS):
                pe.matmul(flat[:, A + h * T:A + h * T + P], vn[:, h, :], pt[:, h, :], start=True, stop=True)
                for sc in range(TH):
                    last = pe.matmul(flat[:, A + h * T + P:A + (h + 1) * T], vn[:, sc * 8 + h, :],
                                     pt[:, HEADS + h * 2 + sc, :], start=(sc == 0), stop=(sc == 1))
                if h % 4 == 3:
                    last.then_inc(att_ready, 1)
            in_to(ATT_AT + 1, 2 * IN_TILES)

            ssq(6, [convt[:, c, :] for c in range(8)], flat[:, C:C + T])
            ssq(7, [convt[:, 8 + c, :] for c in range(4)], flat[:, C + 512:C + 512 + T])
            ssq(8, [convt[:, c, :] for c in range(4)], flat[:, B:B + T])

            b = base["out"]
            pe.wait_ge(m_lo_ready, 1)
            piece(b, 0, 0, m_hi, m_lo)
            pe.wait_ge(m_lo_ready, 3)
            for u in range(1, PIECES):
                piece(b, 0, u, m_hi, m_lo)

            def out_pair(i):
                for u in range(PIECES):
                    piece(b, i, u, m_hi, m_lo)
            pairs(pe, out_pair, 1, NC // 2)
            ssq(8 + NC, [sq1[:, c, :] for c in range(NC)], flat[:, A:A + T])
            pe.wait_ge(x_lo_ready, 4 + NC)
            b = base["q"]

            def x_pair(i):
                for u in range(PIECES):
                    piece(b, i, u, x_hi, x_lo)
            pairs(pe, x_pair, 0, NC // 2)

            b = base["u"]
            for p in range(12):
                piece(b, p // PIECES, p % PIECES, x_hi, x_lo)
                if p >= 4:
                    n = p - 4
                    bank = (A, B, C)[n % 3]
                    if n == 0:
                        pe.wait_ge(evacuated, IN_TILES + 2 * NC)
                        pe.wait_ge(sub_landed, 16)
                    if n >= 3:
                        pe.wait_ge(side_copied, n - 2)
                    th, c0 = n % 4 // 2, n % 2 * 8
                    for c in range(8):
                        dst = flat[:, bank + c * P:bank + (c + 1) * P]
                        if n < 4:
                            last = pe.matmul(dst, qt[:, c0 + c, th * P:(th + 1) * P],
                                             cols(SUBK, 2048, P)[:, c0 + c, :], start=True, stop=True)
                        else:
                            last = pe.transpose(dst, x1t[:, c0 + c, th * P:(th + 1) * P], ident[:, :])
                    last.then_inc(side_ready, 1)
            pairs(pe, x_pair, 3, GATES_AT - 1)
            for u in range(PIECES):
                piece(b, GATES_AT - 1, u, x_hi, x_lo)
                if u == 2:
                    pe.wait_ge(picks_ready, 1)
                    for a in range(3):
                        for th in range(TH):
                            last = pe.transpose(flat[:, A + a * T + th * P:A + a * T + (th + 1) * P],
                                                cols(KEEP + (a * TH + th) * P, P), ident[:, :])
                    last.then_inc(picks_t_ready, 1)
            x_pair(GATES_AT)

            def gates_pair(i):
                for u in range(PIECES):
                    piece(b, i, u, x_hi, x_lo)
                    if u == 0:
                        pe.wait_ge(weighed, i - GATES_AT)
                        pe.wait_ge(hot1_ready, i - GATES_AT)
                        if not isinstance(i, int):
                            pe.wait_ge(gates_copied, i - (GATES_AT + 1))
                        for k in range(8):
                            last = pe.matmul(flat[:, A + k * P:A + (k + 1) * P], hot2[:, k, :], hot1[:, k, :],
                                             start=True, stop=True)
                        last.then_inc(gates_ready, 1)
            gates_pair(GATES_AT + 1)
            with pe.Fori(GATES_AT + 2, GATES_AT + 1 + NG) as i:
                gates_pair(i)
            pairs(pe, x_pair, GATES_AT + 1 + NG, KEYS // 2)

            b = base["v"]
            pe.wait_ge(evacuated, IN_TILES + 2 * NC + KEYS)
            pe.wait_ge(gates_copied, NG)

            def second(i, u, start, stop):
                a = u // 2
                pe.wait_ge(hi_ready, i * PIECES + (b + u + 1))
                if u % 2 == 0:
                    pe.wait_ge(a_lo_ready, i * 2 + (a + 1))

                def products(x, w, start, stop):
                    for th in range(TH):
                        for n in range(2):
                            last = pe.matmul(ps[:, th * 4 + (u % 2) * 2 + n, :], x[:, a, th * P:(th + 1) * P],
                                             w[:, u % 2, n * 512:(n + 1) * 512], start=start, stop=stop)
                    return last
                products(x_hi, w_hi, start, False)
                products(x_lo, w_hi, False, False).then_inc(w_hi_used, 1)
                pe.wait_ge(lo_ready, i * PIECES + (b + u + 1))
                products(x_hi, w_lo, False, stop).then_inc(w_used, 1)

            for u in range(PIECES):
                second(0, u, u < 2, False)
            with pe.Fori(1, KEYS // 2 - 1) as i:
                for u in range(PIECES):
                    second(i, u, False, False)
            for u in range(PIECES):
                second(KEYS // 2 - 1, u, False, u >= 2)

        @block.vector
        def _(dve):
            link, chained, settle = linker(dve, dve_chain)

            def mean(sums, features, v):
                dve.tensor_scalar(v, sums, 1.0 / features, EPS, ALU.mult, ALU.add).then_inc(mean_ready, 1)

            def newton(k, v, r, t):
                dve.wait_ge(root_ready, k + 1)
                link(dve.tensor_tensor(t, r, r, ALU.mult))
                link(dve.tensor_tensor(t, t, v, ALU.mult))
                link(dve.tensor_scalar(t, t, -0.5, 1.5, ALU.mult, ALU.add))
                dve.tensor_tensor(r, r, t, ALU.mult).then_inc(factor_ready, 1)
                dve.wait_ge(factor_ready, k + 1)

            def lo(b, i, u):
                dve.wait_ge(hi_ready, i * PIECES + (b + u + 1))
                if not (isinstance(i, int) and b + i * PIECES + u < 2):
                    dve.wait_ge(w_used, i * PIECES + (b + u - 1))
                dve.tensor_tensor(w_lo[:, u % 2, :], raw[:, u, :], w_hi[:, u % 2, :].bitcast(F32),
                                  ALU.subtract).then_inc(lo_ready, 1)

            def slab_done(slab):
                dve.wait_ge(w_used, slab * 2 + 2)

            dve.wait_ge(smalls_landed, 16)
            for n in range(4):
                dve.wait_ge(x_landed[n], 16)
                for c in range(4 * n, 4 * n + 4):
                    ins = dve.tensor_scalar(xg[:, c, :], xt[:, c, :], smalls[:, G1 + c:G1 + c + 1], None, ALU.mult)
                ins.then_inc(xg_ready, 1)
            dve.memset(cols(RELB, 8)[BUCKETS:BUCKETS + 1, :], -BIG)
            b = base["in"]
            for n in range(4):
                dve.wait_ge(x_hi_ready, n + 1)
                dve.tensor_tensor(x_lo[:, 4 * n:4 * n + 4, :], xg[:, 4 * n:4 * n + 4, :],
                                  x_hi_f[:, 4 * n:4 * n + 4, :], ALU.subtract).then_inc(x_lo_ready, 1)
                if n < 2:
                    lo(b, 0, n)
            dve.wait_ge(bias_in_landed, 32)
            dve.memset(cols(BROW, T + P - 1), 0.0).then_inc(bias_row, 1)
            f0 = cols(FACTOR0, T)
            dve.wait_ge(ssq_ready, 1)
            mean(flat[:, A:A + T], D, cols(CE, T))
            lo(b, 0, 2)
            newton(0, cols(CE, T), f0, cols(CE + T, T))
            dve.wait_ge(bias_row, 2)
            dve.tensor_copy(cols(BROW, T + P - 1)[0:HEADS, :], ps[0:HEADS, 3, 0:T + P - 1]) \
               .then_inc(bias_staged, 1)

            both = lambda a: smalls[:, a:a + 16].unsqueeze(1).broadcast_to([P, 2, 16])
            two = lambda k: dts[:, k, :].rearrange("p (a b) -> p a b", b=16)
            s0, s1 = cols(SC0, 1024, P), cols(SC1, 2048, T)
            bias = cols(BIAS, HEADS * T, T)
            scale = float(P) ** -0.5
            seg, mt, ce = cols(SEG, 1024, P), cols(MT, 1024, P), cols(CE, 1024, P)

            def project(s):
                slab_done(s)
                dve.tensor_tensor(proj[:, s, :], ps[:, s % 2, 0:T], f0, ALU.mult).then_inc(evacuated, 1)

            def convolve(j):
                dve.wait_ge(evacuated, j + 1)
                w = lambda k: smalls[:, CONVW + j * CONV + k:CONVW + j * CONV + k + 1]
                dve.tensor_scalar(convt[:, j, :], proj[:, XBC0 + j, :], w(CONV - 1),
                                  smalls[:, CONVB + j:CONVB + j + 1], ALU.mult, ALU.add).then_inc(conv_step, 1)
                for back in range(1, CONV):
                    dve.wait_ge(conv_step, j * (CONV - 1) + back)
                    dve.scalar_tensor_tensor(out=convt[:, j, back:T], in0=proj[:, XBC0 + j, 0:T - back],
                                             scalar=w(CONV - 1 - back), in1=convt[:, j, back:T],
                                             op0=ALU.mult, op1=ALU.add) \
                       .then_inc(conv_step if back < CONV - 1 else conv_ready, 1)

            def ssd(n, at):
                ch, g = n // 2, n % 2
                heads = slice(ch * 16 + g * 8, ch * 16 + g * 8 + 8)
                tok = slice(ch * P, (ch + 1) * P)
                if at == 2:
                    dve.wait_ge(csb_ready, n + 1)
                    if n:
                        dve.wait_ge(m_ready, n)
                    dve.tensor_tensor(seg, flat[:, A:A + 1024].rearrange("p (a b) -> p a b", b=P),
                                      dts[:, 1, heads].unsqueeze(2).broadcast_to([P, 8, P]), ALU.subtract) \
                       .then_inc(csb_read, 1)
                if at == 3:
                    dve.wait_ge(csb_read, n + 1)
                    dve.tensor_tensor(seg, seg, future.unsqueeze(1).broadcast_to([P, 8, P]), ALU.add) \
                       .then_inc(seg_ready, 1)
                if at == 5 and ch == 1:
                    dve.wait_ge(grow_ready, n - 1)
                    dve.tensor_tensor(ce, ce, convt[:, 10 + g, tok].unsqueeze(1).broadcast_to([P, 8, P]),
                                      ALU.mult).then_inc(grown, 1)
                if at == 6:
                    dve.wait_ge(decay_ready, n + 1)
                    dve.wait_ge(bc_copied, 2)
                    link(dve.tensor_tensor(seg, seg, cols(CB + n * P, P).unsqueeze(1).broadcast_to([P, 8, P]),
                                           ALU.mult))
                if at == 7:
                    if n:
                        dve.wait_ge(y_ready, n)
                    dve.tensor_tensor(mt, seg, dts[:, 0, heads].unsqueeze(2).broadcast_to([P, 8, P]), ALU.mult) \
                       .then_inc(m_ready, 1)
                if at == 9:
                    dve.wait_ge(y_ready, n + 1)
                    dve.wait_ge(skip_ready, 1)
                    y = mix[:, 8 + g * 4:12 + g * 4, tok]
                    dve.tensor_tensor(y, ps[:, 6 + n % 2, :].rearrange("p (a b) -> p a b", b=P), y, ALU.add) \
                       .then_inc(y_added, 1)

            for p in range(3, 2 * IN_TILES):
                lo(b, p // PIECES, p % PIECES)
                if p % 2:
                    s = (p - 3) // 2
                    project(s)
                    if s < CONV_TILES:
                        convolve(s)
                if p == 5:
                    dve.wait_ge(dtraw_ready, 1)
                    dve.wait_ge(factor_t_ready, 1)
                    link(dve.tensor_copy(dts[:, 7, 0:1], flat[:, B + 512:B + 513]))
                    link(dve.tensor_copy(dts[:, 7, 1:2], flat[:, B + 512 + P:B + 513 + P]))
                    for th in range(TH):
                        link(dve.tensor_scalar(dts[:, 0, th * 16:th * 16 + 16], flat[:, B + th * 16:B + th * 16 + 16],
                                               dts[:, 7, th:th + 1], None, ALU.mult))
                    link(dve.tensor_tensor(two(0), two(0), both(DTB), ALU.add))
                    link(dve.tensor_scalar(dts[:, 1, :], dts[:, 0, :], -1.0, None, ALU.mult))
                    dve.tensor_tensor(dts[:, 1, :], dts[:, 0, :], dts[:, 1, :], ALU.max).then_inc(dt_step, 1)
                if p == 8:
                    dve.wait_ge(dt_act, 2)
                    dve.tensor_scalar(dts[:, 3, :], dts[:, 2, :], 1.0, None, ALU.add).then_inc(dt_step, 1)
                    dve.wait_ge(dt_step, 2)
                    link(dve.tensor_scalar(dts[:, 7, :], dts[:, 3, :], -1.0, None, ALU.add))
                    link(dve.tensor_tensor(dts[:, 7, :], dts[:, 2, :], dts[:, 7, :], ALU.subtract))
                    link(dve.reciprocal(dts[:, 8, :], dts[:, 3, :]))
                    link(dve.tensor_tensor(dts[:, 7, :], dts[:, 7, :], dts[:, 8, :], ALU.mult))
                if p == 10:
                    dve.wait_ge(dt_act, 3)
                    link(dve.tensor_tensor(dts[:, 7, :], dts[:, 7, :], dts[:, 4, :], ALU.add))
                    link(dve.scalar_tensor_tensor(out=dts[:, 0, :], in0=dts[:, 0, :], scalar=0.0, in1=dts[:, 7, :],
                                                  op0=ALU.max, op1=ALU.add))
                    link(dve.tensor_scalar(dts[:, 6, 0:16], dts[:, 6, 0:16], -1.0, None, ALU.mult))
                    dve.tensor_tensor(two(5), two(0), dts[:, 6, 0:16].unsqueeze(1).broadcast_to([P, 2, 16]),
                                      ALU.mult).then_inc(da_ready, 1)
                if p == 20:
                    dve.wait_ge(cs_ready, 1)
                    link(dve.tensor_copy(dts[:, 1, :], flat[:, B + 64:B + 96]))
                    dve.tensor_tensor(dts[:, 4, 0:16], flat[:, B + 96:B + 112], dts[:, 1, 0:16], ALU.subtract) \
                       .then_inc(dt_step, 1)
                if p == 24:
                    dve.wait_ge(dt_act, 4)
                    dve.tensor_tensor(dts[:, 4, 0:16], dts[:, 4, 0:16], dts[:, 0, 0:16], ALU.mult) \
                       .then_inc(w0_ready, 1)
                for n in range(4):
                    ssd(n, p - (SSD_AT + SSD_STEP * n))
                if p in (SCORES_AT + 2, SCORES_AT + 3):
                    h0 = 4 * (p - SCORES_AT - 2)
                    dve.wait_ge(qk_ready, 1)
                    dve.wait_ge(bias_copied, 2)
                    link(dve.scalar_tensor_tensor(
                        out=s1[:, h0:h0 + 4, :],
                        in0=flat[:, A + h0 * T:A + (h0 + 4) * T].rearrange("p (a b) -> p a b", b=T),
                        scalar=scale, in1=bias[:, h0:h0 + 4, :], op0=ALU.mult, op1=ALU.add))
                if p == SCORES_AT + 4:
                    dve.wait_ge(qk_ready, 2)
                    link(dve.scalar_tensor_tensor(out=s0, in0=flat[:, C:C + 1024].rearrange("p (a b) -> p a b", b=P),
                                                  scalar=scale, in1=bias[:, :, P:T], op0=ALU.mult, op1=ALU.add))
                if p in (SCORES_AT + 5, SCORES_AT + 6):
                    h0 = 4 * (p - SCORES_AT - 5)
                    link(dve.tensor_reduce(dts[:, 2, 8 + h0:12 + h0], s1[:, h0:h0 + 4, :], AX_X, ALU.max))
                if p == SCORES_AT + 7:
                    link(dve.tensor_reduce(dts[:, 2, 0:8], s0, AX_X, ALU.max))
                    dve.tensor_scalar(dts[:, 2, 0:16], dts[:, 2, 0:16], -1.0, None, ALU.mult).then_inc(negmax_ready, 1)
                if p == PROBS_AT:
                    dve.wait_ge(exp_ready, 2 * HEADS)
                    link(dve.reciprocal(dts[:, 3, 0:16], dts[:, 3, 0:16]))
                    link(dve.tensor_tensor(s0, s0, dts[:, 3, 0:8].unsqueeze(2).broadcast_to([P, 8, P]), ALU.mult))
                if p in (PROBS_AT + 1, PROBS_AT + 2):
                    h0 = 4 * (p - PROBS_AT - 1)
                    ins = dve.tensor_tensor(s1[:, h0:h0 + 4, :], s1[:, h0:h0 + 4, :],
                                            dts[:, 3, 8 + h0:12 + h0].unsqueeze(2).broadcast_to([P, 4, T]), ALU.mult)
                    if h0:
                        ins.then_inc(probs_ready, 1)

            def gate_y(g):
                dve.wait_ge(zsilu_ready, g + 1)
                y = mix[:, 8 + 4 * g:12 + 4 * g, :]
                dve.tensor_tensor(y, y, proj[:, Z0 + 4 * g:Z0 + 4 * g + 4, :], ALU.mult).then_inc(gated_y, 1)

            def norm(k, c0, c1):
                n = k - 1
                v, r, t = cols(SEG + n * T, T), cols(MT + n * T, T), cols(CE + n * T, T)
                newton(k, v, r, t)
                for c in range(c0, c1):
                    ins = dve.scalar_tensor_tensor(out=mix[:, c, :], in0=mix[:, c, :],
                                                   scalar=smalls[:, GMIX + c:GMIX + c + 1], in1=r,
                                                   op0=ALU.mult, op1=ALU.mult)
                ins.then_inc(normed, 1)

            def m_lower(k, c0, c1):
                dve.wait_ge(m_hi_ready, k)
                dve.tensor_tensor(m_lo[:, c0:c1, :], mix[:, c0:c1, :], m_hi_f[:, c0:c1, :], ALU.subtract) \
                   .then_inc(m_lo_ready, 1)

            dve.wait_ge(y_added, 4)
            gate_y(0)
            b = base["out"]
            lo(b, 0, 0)
            dve.wait_ge(ssq_ready, 2)
            mean(flat[:, C:C + T], 1024, cols(SEG, T))
            project(IN_TILES - 1)
            lo(b, 0, 1)
            dve.wait_ge(sq_ready, 7)
            norm(1, 0, 8)
            gate_y(1)
            dve.wait_ge(ssq_ready, 3)
            mean(flat[:, C + 512:C + 512 + T], 512, cols(SEG + T, T))
            m_lower(1, 0, 8)
            norm(2, 8, 12)
            dve.wait_ge(ssq_ready, 4)
            mean(flat[:, B:B + T], 512, cols(SEG + 2 * T, T))
            m_lower(2, 8, 12)
            norm(3, 12, 16)
            m_lower(3, 12, 16)

            def add_x(s, ring):
                dve.wait_ge(w_used, s * 2 + (base["out"] + 2))
                dve.tensor_tensor(x1t[:, s, :], ps[:, ring, 0:T], xt[:, s, :], ALU.add).then_inc(evacuated, 1)
                dve.wait_ge(evacuated, s + (IN_TILES + 1))
                dve.tensor_scalar(cols(X1G + ring * T, T), x1t[:, s, :], gain2(s), None, ALU.mult) \
                   .then_inc(x1g_ready, 1)

            def lower_x(s, ring):
                dve.wait_ge(x_hi_ready, s + 5)
                dve.tensor_tensor(x_lo[:, s, :], cols(X1G + ring * T, T), x_hi_f[:, s, :], ALU.subtract) \
                   .then_inc(x_lo_ready, 1)

            gain2 = lambda s: smalls[:, G2:G2 + NC][:, s:s + 1] if isinstance(s, int) \
                else smalls[:, G2:G2 + NC].rearrange("p (c a) -> p c a", a=1)[:, s, :]

            for p in range(2, 2 * NC):
                lo(b, p // PIECES, p % PIECES)
                if p % 2:
                    s = (p - 3) // 2
                    add_x(s, s % 2)
                elif p >= 4:
                    lower_x((p - 4) // 2, (p - 4) // 2 % 2)
            b = base["q"]
            lo(b, 0, 0)
            lower_x(NC - 2, 0)
            lo(b, 0, 1)
            add_x(NC - 1, 1)
            lower_x(NC - 1, 1)
            dve.wait_ge(ssq_ready, 5)
            mean(flat[:, A:A + T], D, cols(CAND, T))
            lo(b, 0, 2)
            newton(4, cols(CAND, T), factor2, cols(CAND + T, T))

            def take_q(s, bank):
                dve.wait_ge(w_used, s * 2 + (base["q"] + 2))
                dve.tensor_tensor(qt[:, s, :], ps[:, bank, 0:T], factor2, ALU.mult).then_inc(evacuated, 1)

            lo(b, 0, 3)
            take_q(0, 0)

            def q_pair(i):
                for u in range(PIECES):
                    lo(b, i, u)
                    if u % 2:
                        take_q(i * 2 + (u // 2 - 1), (u // 2 + 1) % 2)
            pairs(dve, q_pair, 1, NC // 2)

            b = base["u"]

            def scale_u(s, bank):
                dve.wait_ge(w_used, s * 2 + (base["u"] + 2))
                dve.tensor_tensor(ps[:, bank, 0:T], ps[:, bank, 0:T], factor2, ALU.mult).then_inc(scaled, 1)

            def u_piece(i, u):
                lo(b, i, u)
                if isinstance(i, int) and i == 0 and u == 1:
                    take_q(NC - 1, 1)
                elif u % 2:
                    scale_u(i * 2 + (u // 2 - 1), (u // 2 + 1) % 2)

            at = [0]

            def next_piece():
                u_piece(at[0] // PIECES, at[0] % PIECES)
                at[0] += 1

            def top16(tiles, pieces):
                next_piece()
                for vals, idx, src, tmp in tiles:
                    chained(dve.max(vals[:, 0:8], src))
                settle()
                for vals, idx, src, tmp in tiles:
                    chained(dve.match_replace(tmp, vals[:, 0:8], src, -3e38))
                if pieces == 3:
                    next_piece()
                for vals, idx, src, tmp in tiles:
                    chained(dve.max_index(idx[:, 0:8], vals[:, 0:8], src))
                if pieces == 2:
                    next_piece()
                settle()
                for vals, idx, src, tmp in tiles:
                    chained(dve.max(vals[:, 8:16], tmp))
                if pieces == 3:
                    next_piece()
                settle()
                for vals, idx, src, tmp in tiles:
                    chained(dve.max_index(idx[:, 8:16], vals[:, 8:16], tmp))

            for _ in range(TOP_AT):
                next_piece()
            for n0 in range(0, TH * 2 * PH, 2):
                if n0 % 8 == 0:
                    dve.wait_ge(side_copied, n0 // 8 + 1)
                top16([(cols(TOPV + n * TOP, TOP), cols(TOPI + n * TOP, TOP).bitcast(U32),
                        cols(SCORES + n * P, P), cols((SCORES2, CAND)[n % 2], P)) for n in (n0, n0 + 1)], 2)
            next_piece()
            settle()
            chained(dve.tensor_copy(cols(TOPIF, 512), cols(TOPI, 512).bitcast(U32)))
            half = [P, PH // 2, TOP, TOP]
            for th in range(TH):
                v = cols(TOPV + th * 256, 256).rearrange("p (h c k) -> p h c k", c=2, k=TOP)
                idx = cols(TOPIF + th * 256, 256).rearrange("p (h c k) -> p h c k", c=2, k=TOP)
                cand = cols(CAND + th * 2048, 2048).rearrange("p (h a b) -> p h a b", a=TOP, b=TOP)
                for hh in range(2):
                    next_piece()
                    settle()
                    hs = slice(4 * hh, 4 * hh + 4)
                    chained(dve.tensor_tensor(cand[:, hs], v[:, hs, 0, :].unsqueeze(3).broadcast_to(half),
                                              v[:, hs, 1, :].unsqueeze(2).broadcast_to(half), ALU.add))
                for h0 in range(0, PH, 2):
                    settle()
                    top16([(cols(PICKV + th * P + h * TOP, TOP), cols(POS + th * P + h * TOP, TOP).bitcast(U32),
                            cols(CAND + th * 2048 + h * 256, 256), cols((CAND2, SCORES)[h % 2], 256))
                           for h in (h0, h0 + 1)], 3)
                next_piece()
                settle()
                pos = cols(POS + th * P, P).bitcast(U32)
                chained(dve.tensor_scalar(cols(POSF, P).bitcast(U32), pos, 4, None, ALU.logical_shift_right))
                chained(dve.tensor_scalar(cols(POSF + P, P).bitcast(U32), pos, 15, None, ALU.bitwise_and))
                settle()
                chained(dve.tensor_copy(cols(POSF + 2 * P, 2 * P), cols(POSF, 2 * P).bitcast(U32)))
                hot = cols(ONEHOT, 1024, TOP)
                hot4 = cols(ONEHOT, 1024).rearrange("p (h a b) -> p h a b", a=TOP, b=TOP)
                for c in range(2):
                    for hh in range(2):
                        hs = slice(4 * hh, 4 * hh + 4)
                        part = cols(POSF + (2 + c) * P + hh * 64, 64)
                        next_piece()
                        settle()
                        chained(dve.tensor_tensor(hot, part.unsqueeze(2).broadcast_to([P, 64, TOP]),
                                                  iota_f[:, 0:TOP].unsqueeze(1).broadcast_to([P, 64, TOP]),
                                                  ALU.is_equal))
                        next_piece()
                        settle()
                        chained(dve.tensor_tensor(hot4, hot4, idx[:, hs, c, :].unsqueeze(2).broadcast_to(half),
                                                  ALU.mult))
                        next_piece()
                        settle()
                        chained(dve.tensor_reduce(cols(KEEP + (c * TH + th) * P + hh * 64, 64), hot, AX_X, ALU.add))
            settle()
            assert at[0] <= PIECES * (GATES_AT - 1), at[0]
            while at[0] < PIECES * (GATES_AT - 1):
                next_piece()
            pick = cols(PICKV, 256, TOP)
            link(dve.tensor_copy(cols(POSF, 16), pick[:, :, 0]))
            dve.tensor_tensor(pick, pick, cols(POSF, 16).unsqueeze(2).broadcast_to([P, 16, TOP]), ALU.subtract) \
               .then_inc(gate_sub, 1)
            next_piece()
            next_piece()
            dve.wait_ge(gate_exp, 1)
            link(dve.tensor_reduce(cols(POSF, 16), pick, AX_X, ALU.add))
            link(dve.reciprocal(cols(POSF, 16), cols(POSF, 16)))
            dve.tensor_tensor(cols(KEEP + 2 * TH * P, 256, TOP), pick,
                              cols(POSF, 16).unsqueeze(2).broadcast_to([P, 16, TOP]), ALU.mult).then_inc(picks_ready, 1)
            next_piece()
            next_piece()

            def hot_rows(dst, a, g, signal):
                dve.tensor_tensor(dst[:, :, :], iota_f[:, :].unsqueeze(1).broadcast_to([P, 8, KEYS]),
                                  route[:, a, :].rearrange("p (g k) -> p g k", k=8)[:, g, :]
                                  .unsqueeze(2).broadcast_to([P, 8, KEYS]), ALU.is_equal).then_inc(signal, 1)

            def gates_pair(i):
                for u in range(PIECES):
                    u_piece(i, u)
                    if u == 2:
                        if isinstance(i, int):
                            dve.wait_ge(route_ready, 1)
                            hot_rows(hot2, 1, 0, hot2_ready)
                        else:
                            dve.wait_ge(gates_ready, i - GATES_AT)
                            hot_rows(hot2, 1, i - GATES_AT, hot2_ready)
                    if u == 3:
                        hot_rows(hot1, 0, 0 if isinstance(i, int) else i - GATES_AT, hot1_ready)
            gates_pair(GATES_AT)
            with dve.Fori(GATES_AT + 1, GATES_AT + NG) as i:
                gates_pair(i)

            def u_pair(i):
                for u in range(PIECES):
                    u_piece(i, u)
            pairs(dve, u_pair, GATES_AT + NG, KEYS // 2)

            b = base["v"]

            def gate(n, a, landed):
                dve.wait_ge(h_landed[a], landed)
                dve.tensor_tensor(act_f[:, a, :], h_in[:, a, :], G[:, n, :], ALU.mult).then_inc(acted, 1)

            def lower_a(a, ready):
                dve.wait_ge(acted, ready)
                dve.wait_ge(a_hi_ready, ready)
                dve.tensor_tensor(x_lo[:, a, :], act_f[:, a, :], x_hi_f[:, a, :], ALU.subtract).then_inc(a_lo_ready, 1)

            lo(b, 0, 0)
            lo(b, 0, 1)
            scale_u(KEYS - 1, 1)
            dve.wait_ge(gates_copied, NG)
            for a in range(2):
                gate(a, a, 16)
            for a in range(2):
                lower_a(a, a + 1)
            lo(b, 0, 2)
            lo(b, 0, 3)

            def v_pair(i):
                for u in range(PIECES):
                    a = u // 2
                    if u % 2 == 0:
                        gate(i * 2 + a, a, i * 16 + 16)
                    lo(b, i, u)
                    if u % 2 == 0:
                        lower_a(a, i * 2 + (a + 1))
            pairs(dve, v_pair, 1, KEYS // 2)

            dve.wait_ge(w_used, b + 2 * KEYS)
            dve.wait_ge(tail_landed, 32)
            for th in range(TH):
                dve.tensor_tensor(cols(8192 + th * D, D), flat[:, th * D:(th + 1) * D], cols(th * D, D), ALU.add) \
                   .then_inc(final_y, 1)
            dve.wait_ge(final_sq, TH)
            dve.tensor_scalar(dts[:, 3, 0:TH], dts[:, 2, 0:TH], 1.0 / D, EPS, ALU.mult, ALU.add).then_inc(final_mean, 1)
            dve.wait_ge(final_root, 1)
            r, t = dts[:, 1, 0:TH], dts[:, 4, 0:TH]
            link(dve.tensor_tensor(t, r, r, ALU.mult))
            link(dve.tensor_tensor(t, t, dts[:, 3, 0:TH], ALU.mult))
            link(dve.tensor_scalar(t, t, -0.5, 1.5, ALU.mult, ALU.add))
            link(dve.tensor_tensor(r, r, t, ALU.mult))
            for th in range(TH):
                y = cols(8192 + th * D, D)
                dve.scalar_tensor_tensor(out=y, in0=y, scalar=dts[:, 1, th:th + 1], in1=cols(TH * D, D),
                                         op0=ALU.mult, op1=ALU.mult).then_inc(final_ready, 1)


def slabs_of(w, tiles):
    return np.ascontiguousarray(w.reshape(NC, P, tiles, P).transpose(2, 1, 0, 3)).reshape(tiles, P, NC * P)


def kernel(**inputs):
    import concourse.bacc as bacc
    from concourse.bass_utils import run_bass_kernel_spmd

    a = {k: np.asarray(v) for k, v in inputs.items()}
    w_in = a["w_in"][0]
    main = IN_TILES * P
    wide = lambda row: np.broadcast_to(row, (P, row.shape[-1]))
    tiles = lambda v, n: v.reshape(n, P).T
    smalls = np.concatenate([
        tiles(a["attn_norm"][0], NC), tiles(a["ffn_norm"][0], NC),
        tiles(a["attn_out_norm"][0], 8), tiles(a["ssm_out_norm"][0], 8),
        a["conv_w"][0].reshape(CONV, CONV_TILES, P).transpose(2, 1, 0).reshape(P, CONV_TILES * CONV),
        tiles(a["conv_b"][0], CONV_TILES), wide(a["dt_bias"]), wide(a["a_log"]),
        tiles(np.repeat(a["d_skip"][0], HD), 8)], axis=1)
    arrays = {
        "x_t": a["x"][0].T.reshape(NC, P, T).transpose(1, 0, 2).reshape(P, NC * T),
        "w_in": slabs_of(np.concatenate([w_in[:, main - CONV_TILES * P:main],
                                         w_in[:, :main - (CONV_TILES + 8) * P],
                                         w_in[:, main - (CONV_TILES + 8) * P:main - CONV_TILES * P]], axis=1),
                         IN_TILES),
        "w_dt": w_in[:, main:].reshape(NC, P, SSM_HEADS).transpose(1, 0, 2).reshape(P, NC * SSM_HEADS),
        "w_out": slabs_of(a["w_out"][0], NC),
        "w_q": slabs_of(a["peer_wq"][0], NC),
        "subkeys": a["peer_subkeys"][0].transpose(3, 0, 1, 2).reshape(P, 2 * PH * KEYS),
        "u_tab": a["peer_u"][0].reshape(KEYS, KEYS, NC, P).transpose(0, 3, 2, 1).reshape(KEYS, P, D),
        "v_tab": a["peer_v"][0].reshape(KEYS, KEYS, D),
        "smalls_in": smalls,
        "rel_bias": a["rel_bias"],
        "selectors": bucket_selectors(),
        "final_gain": a["final_norm"],
    }
    nc = bacc.Bacc("TRN2", target_bir_lowering=False, num_devices=1)
    args, sent = [], {}
    for name, v in arrays.items():
        v = np.ascontiguousarray(v)
        sent["in_" + name] = v
        args.append(nc.dram_tensor("in_" + name, v.shape, mybir.dt.from_np(v.dtype), kind="ExternalInput").ap())
    out = nc.dram_tensor("out", (T, D), F32, kind="ExternalOutput").ap()
    layer(nc, *args, out)
    r = run_bass_kernel_spmd(nc, [sent], core_ids=[0])
    return r.results[0]["out"].reshape(1, T, D)
```

```python
from contextlib import ExitStack

import numpy as np

import concourse.bass as bass
from concourse import mybir

ALU = mybir.AluOpType
ACT = mybir.ActivationFunctionType
AX_X = mybir.AxisListType.X
F32 = mybir.dt.float32
F32R = mybir.dt.float32r
U32 = mybir.dt.uint32
I32 = mybir.dt.int32

P = 128
D = 2048
T = 256
TH = T // P
NC = D // P
HEADS = 8
BUCKETS = 32
MAX_DIST = 128
SSM_HEADS = 16
HD = 64
GROUPS = 2
CONV = 4
CONV_TILES = 12
KEYS = 128
PH = 8
TOP = 16
EPS = 1e-6
BIG = 1e30

XBC0, Q0, K0, V0, Z0 = 0, 12, 20, 28, 36
IN_TILES = 44
STAGES = {"in": IN_TILES, "out": NC, "q": NC, "u": KEYS, "v": KEYS}
PIECES = 4
PCOLS = NC * P // 2

XT, PROJ, CONVT, MIX, SCR = 0, 4096, 15360, 18432, 22528
ARENA = KEYS * T
XG = PROJ + 28 * T
WDT, RELB, SEL, BROW = SCR, SCR + 256, SCR + 512, SCR + 1024
WDTHI, WDTLO, DTF = SCR + 1408, SCR + 1664, SCR
XN, BN, XW, PREV = SCR, SCR + 2048, SCR + 2304, SCR + 3328
SEG, MT, CE, CB, BIAS = SCR + 4352, SCR + 5376, SCR + 6400, SCR + 7424, SCR + 7936
FACTOR0 = SCR + 9984
BIAS_UP = SEG
VN, SC0, SC1, PT = XN, XW, MIX, PROJ
MHI, MLO = PROJ, PROJ + 4096
X1T, SQ1, X1G = MIX, SCR, SCR + 4096
QT, SCORES, SUBK, X1 = PROJ, PROJ + 4096, XT, SCR
SCORES2, TOPV, TOPI, TOPIF, CAND, CAND2 = 12288, 12416, 12928, 13440, 13952, 18048
ONEHOT, PICKV, POS, POSF, KEEP = 2048, 27136, 27392, 27648, 28160
GAIN3, YT, YSQ, YG = 4096, 8192, 16384, 24576

G1, G2, GMIX, CONVW, CONVB, DTB, ALOG, DSK = 0, 16, 32, 48, 96, 108, 124, 140
SMALLS = 148

SSD_AT, SSD_STEP = 26, 7
SCORES_AT, EXP_AT, PROBS_AT, VT_AT, PT_AT, ATT_AT = 58, 66, 70, 73, 71, 76
NORM_AT = 82
TOP_AT = 7
GATES_AT = 25
NG = T // 8
MIXER_SQUARES = 9


def bucket_selectors():
    n = (T - 1) - np.arange(T + P - 1)
    exact = BUCKETS // 2
    nf = np.maximum(n, 1).astype(np.float32)
    large = exact + (np.log(nf / np.float32(exact)) / np.float32(np.log(MAX_DIST / exact))
                     * np.float32(BUCKETS - exact)).astype(np.int32)
    bucket = np.where(n < exact, np.maximum(n, 0), np.minimum(large, BUCKETS - 1))
    bucket = np.where(n < 0, BUCKETS, bucket)
    return (bucket[None, :] == np.arange(BUCKETS + 1)[:, None]).astype(np.float32)


def layer(nc, x_t, w_in, w_dt, w_out, w_q, subkeys, u_tab, v_tab, smalls_in, rel_bias,
          selectors, final_gain, out):
    scratch_bias = nc.dram_tensor("scratch_bias", (HEADS, T + P - 1), F32, kind="Internal").ap()
    scratch_x1 = nc.dram_tensor("scratch_x1", (P, TH * D), F32, kind="Internal").ap()
    scratch_h = nc.dram_tensor("scratch_h", (KEYS, P, T), F32, kind="Internal").ap()
    stage_src = {"in": w_in, "out": w_out, "q": w_q, "u": u_tab, "v": v_tab}
    base, at = {}, 0
    for name, slabs in STAGES.items():
        base[name] = at
        at += 2 * slabs

    ctx = ExitStack()
    with ctx:
        def sb(name, shape, dt=F32):
            return ctx.enter_context(nc.sbuf_tensor(name, shape, dt))

        def sem(name):
            return ctx.enter_context(nc.semaphore(name))

        arena = sb("arena", [P, ARENA])
        arena_at = nc.sbuf_base - 4 * ARENA
        m_hi = nc.alloc_sbuf_tensor_at("m_hi", [P, NC, T], F32R, offset=arena_at + 4 * MHI)
        m_lo = nc.alloc_sbuf_tensor_at("m_lo", [P, NC, T], F32R, offset=arena_at + 4 * MLO)
        wdt_hi = nc.alloc_sbuf_tensor_at("wdt_hi", [P, NC, SSM_HEADS], F32R, offset=arena_at + 4 * WDTHI)
        wdt_lo = nc.alloc_sbuf_tensor_at("wdt_lo", [P, NC, SSM_HEADS], F32R, offset=arena_at + 4 * WDTLO)
        x_hi = sb("x_hi", [P, NC, T], F32R)
        x_lo = sb("x_lo", [P, NC, T], F32R)
        raw = sb("raw", [P, PIECES, PCOLS])
        w_hi = sb("w_hi", [P, 2, PCOLS], F32R)
        w_lo = sb("w_lo", [P, 2, PCOLS], F32R)
        aux = sb("aux", [P, 512])
        tri, future, flip, ones = (aux[:, n * P:(n + 1) * P] for n in range(4))
        factor2 = aux[:, T:2 * T]
        ident = sb("ident", [P, P])
        iota_f = sb("iota_f", [P, P])
        smalls = sb("smalls", [P, SMALLS])
        dts = sb("dts", [P, 9, 32])
        gelu_out = [aux[:, 0:T], dts[:, 0:8, :].rearrange("p a b -> p (a b)")]
        route = sb("route", [P, 3, T])
        hot1 = sb("hot1", [P, 8, KEYS])
        hot2 = sb("hot2", [P, 8, KEYS])
        ps = ctx.enter_context(nc.psum_tensor("ps", [P, 8, 512], F32))
        h_in = hot1[:, 0:4, :].rearrange("p (a b) k -> p a (b k)", a=2)
        act_f = hot2[:, 0:4, :].rearrange("p (a b) k -> p a (b k)", a=2)

        def cols(a, n, m=None):
            v = arena[:, a:a + n]
            return v if m is None else v.rearrange("p (a b) -> p a b", b=m)

        xt, xg = cols(XT, 4096, T), cols(XG, 4096, T)
        proj = cols(PROJ, IN_TILES * T, T)
        convt = cols(CONVT, CONV_TILES * T, T)
        mix = cols(MIX, 4096, T)
        x1t, sq1 = cols(X1T, 4096, T), cols(SQ1, 4096, T)
        qt = cols(QT, 4096, T)
        G = arena[:, :].rearrange("p (i t) -> p i t", t=T)
        G_by_token = arena[:, :].rearrange("p (i g k) -> p g k i", g=NG, k=8)
        x_hi_f, x_lo_f, m_hi_f = (v[:, :, :].bitcast(F32) for v in (x_hi, x_lo, m_hi))
        flat = ps[:, :, :].rearrange("p b n -> p (b n)")
        A, B, C = 1024, 2048, 3072

        x_landed = [sem(f"x_landed{n}") for n in range(4)]
        smalls_landed = sem("smalls_landed")
        wdt_landed = sem("wdt_landed")
        bias_in_landed = sem("bias_in_landed")
        raw_landed = [sem(f"raw_landed{n}") for n in range(PIECES)]
        bias_staged = sem("bias_staged")
        bias_out = sem("bias_out")
        bias_landed = sem("bias_landed")
        bias_flipped = sem("bias_flipped")
        bias_copied = sem("bias_copied")
        sub_landed = sem("sub_landed")
        hi_ready = sem("hi_ready")
        lo_ready = sem("lo_ready")
        w_hi_used = sem("w_hi_used")
        w_used = sem("w_used")
        evacuated = sem("evacuated")
        pool_chain = sem("pool_chain")
        consts_ready = sem("consts_ready")
        xg_ready = sem("xg_ready")
        sq_ready = sem("sq_ready")
        sq0_added = sem("sq0_added")
        ssq_ready = sem("ssq_ready")
        mean_ready = sem("mean_ready")
        ln_ready = sem("ln_ready")
        root_ready = sem("root_ready")
        factor_ready = sem("factor_ready")
        x_hi_ready = sem("x_hi_ready")
        x_lo_ready = sem("x_lo_ready")
        normed = sem("normed")
        m_hi_ready = sem("m_hi_ready")
        m_lo_ready = sem("m_lo_ready")
        dve_chain = sem("dve_chain")
        bias_row = sem("bias_row")
        vt_ready = sem("vt_ready")
        v_copied = sem("v_copied")
        qk_ready = sem("qk_ready")
        negmax_ready = sem("negmax_ready")
        exp_ready = sem("exp_ready")
        probs_ready = sem("probs_ready")
        pt_ready = sem("pt_ready")
        pt_copied = sem("pt_copied")
        att_ready = sem("att_ready")
        att_copied = sem("att_copied")
        wdt_hi_ready = sem("wdt_hi_ready")
        wdt_lo_ready = sem("wdt_lo_ready")
        dtraw_ready = sem("dtraw_ready")
        dt_scaled = sem("dt_scaled")
        dt_t_ready = sem("dt_t_ready")
        dt_step = sem("dt_step")
        dt_act = sem("dt_act")
        da_ready = sem("da_ready")
        cs_ready = sem("cs_ready")
        conv_step = sem("conv_step")
        conv_ready = sem("conv_ready")
        silu_ready = sem("silu_ready")
        skip_ready = sem("skip_ready")
        xs_t_ready = sem("xs_t_ready")
        xs_copied = sem("xs_copied")
        bc_ready = sem("bc_ready")
        bc_copied = sem("bc_copied")
        w0_ready = sem("w0_ready")
        xw_ready = sem("xw_ready")
        state_ready = sem("state_ready")
        state_copied = sem("state_copied")
        csb_ready = sem("csb_ready")
        csb_read = sem("csb_read")
        seg_ready = sem("seg_ready")
        decay_ready = sem("decay_ready")
        grow_ready = sem("grow_ready")
        grown = sem("grown")
        m_ready = sem("m_ready")
        y_ready = sem("y_ready")
        y_added = sem("y_added")
        zsilu_ready = sem("zsilu_ready")
        gated_y = sem("gated_y")
        x1g_ready = sem("x1g_ready")
        sq_added = sem("sq_added")
        side_ready = sem("side_ready")
        side_copied = sem("side_copied")
        x1_saved = sem("x1_saved")
        gate_sub = sem("gate_sub")
        gate_exp = sem("gate_exp")
        picks_ready = sem("picks_ready")
        picks_t_ready = sem("picks_t_ready")
        route_ready = sem("route_ready")
        scaled = sem("scaled")
        h_stored = [sem(f"h_stored{n}") for n in range(2)]
        hot1_ready = sem("hot1_ready")
        hot2_ready = sem("hot2_ready")
        weighed = sem("weighed")
        gates_ready = sem("gates_ready")
        gates_copied = sem("gates_copied")
        h_landed = [sem(f"h_landed{n}") for n in range(2)]
        acted = sem("acted")
        a_hi_ready = sem("a_hi_ready")
        a_lo_ready = sem("a_lo_ready")
        tail_landed = sem("tail_landed")
        gelu_free = sem("gelu_free")
        first_half_done = sem("first_half_done")
        final_y = sem("final_y")
        final_sq = sem("final_sq")
        final_mean = sem("final_mean")
        final_root = sem("final_root")
        final_gained = sem("final_gained")
        final_factor = sem("final_factor")
        final_ready = [sem(f"final_ready{n}") for n in range(TH)]
        stored = sem("stored")

        def linker(eng, chain):
            n = [0]

            def chained(ins):
                n[0] += 1
                ins.then_inc(chain, 1)

            def settle():
                eng.wait_ge(chain, n[0])

            def link(ins):
                chained(ins)
                settle()
            return link, chained, settle

        def pairs(eng, pair, first, end):
            if first == 0:
                pair(0)
                first = 1
            if end - first > 1:
                with eng.Fori(first, end) as i:
                    pair(i)
            elif end > first:
                pair(first)

        block = ctx.enter_context(nc.Block())

        @block.sync
        def _(sp):
            def load(src, slab, u):
                sp.dma_start(raw[:, u, :], src[slab, :, (u % 2) * PCOLS:(u % 2 + 1) * PCOLS]) \
                  .then_inc(raw_landed[u], 16)

            for n in range(4):
                sp.dma_start(cols(XT + n * 1024, 1024), x_t[:, n * 1024:(n + 1) * 1024]).then_inc(x_landed[n], 16)
                if n % 2:
                    load(w_in, 0, n // 2)
            for u in range(2, PIECES):
                load(w_in, u // 2, u)
            for name in ("in", "out", "q"):
                src = stage_src[name]
                if name == "out":
                    for p in range(2 * PIECES):
                        half = p // PIECES
                        sp.wait_ge(lo_ready, base[name] + p - PIECES + 1)
                        sp.dma_start(raw[:, p % PIECES, :], src[p % PIECES, :, half * PCOLS:(half + 1) * PCOLS]) \
                          .then_inc(raw_landed[p % PIECES], 16)
                with sp.Fori({"in": 1, "out": 2, "q": 0}[name], STAGES[name] // 2) as i:
                    for u in range(PIECES):
                        sp.wait_ge(lo_ready, i * PIECES + (base[name] + u - PIECES + 1))
                        load(src, i * 2 + u // 2, u)

            def store_h(s, a):
                sp.wait_ge(evacuated, s + (IN_TILES + 2 * NC + 1))
                sp.dma_start(scratch_h[s], gelu_out[a]).then_inc(h_stored[a], 16)

            def u_pair(i):
                for u in range(PIECES):
                    sp.wait_ge(lo_ready, i * PIECES + (base["u"] + u - PIECES + 1))
                    load(u_tab, i * 2 + u // 2, u)
                    if u % 2 and not (isinstance(i, int) and i * 2 + u // 2 < 3):
                        store_h(i * 2 + (u // 2 - 3), (u // 2 + 1) % 2)
            u_pair(0)
            u_pair(1)
            pairs(sp, u_pair, 2, KEYS // 2)

            def load_h(n, a):
                sp.dma_start(h_in[:, a, :], scratch_h[n]).then_inc(h_landed[a], 16)

            sp.wait_ge(gates_ready, NG)
            for a in range(2):
                sp.wait_ge(h_stored[a], 32)
                load_h(a, a)
            for u in range(PIECES):
                sp.wait_ge(lo_ready, base["v"] + u - PIECES + 1)
                load(v_tab, u // 2, u)
                if u % 2:
                    store_h(KEYS - 3 + u // 2, (u // 2 + 1) % 2)
            store_h(KEYS - 1, 1)

            def v_pair(i):
                for u in range(PIECES):
                    sp.wait_ge(lo_ready, i * PIECES + (base["v"] + u - PIECES + 1))
                    load(v_tab, i * 2 + u // 2, u)
                    if u % 2:
                        sp.wait_ge(acted, i * 2 + (u // 2 - 1))
                        load_h(i * 2 + u // 2, u // 2)
            v_pair(1)
            for a in range(2):
                sp.wait_ge(h_stored[a], 16 * KEYS // 2)
            with sp.Fori(2, KEYS // 2) as i:
                v_pair(i)
            for n in range(2 * TH):
                th, c = n // 2, n % 2 * PCOLS
                sp.wait_ge(final_ready[th], n % 2 + 1)
                sp.dma_start(out[th * P:(th + 1) * P, c:c + PCOLS], cols(YT + th * D + c, PCOLS)) \
                  .then_inc(stored, 16)
            sp.wait_ge(stored, 16 * 2 * TH)

        @block.gpsimd
        def _(pool):
            link, _, _ = linker(pool, pool_chain)
            pool.memset(ones, 1.0).then_inc(consts_ready, 1)
            link(pool.memset(ident[:, :], 0.0))
            pool.affine_select(out=ident[:, :], in_=ident[:, :], compare_op=ALU.not_equal, fill=1.0,
                               base=0, pattern=[[-1, P]], channel_multiplier=1).then_inc(consts_ready, 1)
            link(pool.memset(tri, 1.0))
            pool.affine_select(out=tri, in_=tri, compare_op=ALU.is_ge, fill=0.0,
                               base=0, pattern=[[1, P]], channel_multiplier=-1).then_inc(consts_ready, 1)
            link(pool.memset(future, 0.0))
            pool.affine_select(out=future, in_=future, compare_op=ALU.is_ge, fill=-BIG,
                               base=0, pattern=[[1, P]], channel_multiplier=-1).then_inc(consts_ready, 1)
            link(pool.iota(hot1[:, 0, :].bitcast(I32), pattern=[[1, P]], base=0, channel_multiplier=0))
            pool.tensor_copy(iota_f[:, :], hot1[:, 0, :].bitcast(I32)).then_inc(consts_ready, 1)
            link(pool.memset(flip, 0.0))
            pool.affine_select(out=flip, in_=flip, compare_op=ALU.not_equal, fill=1.0,
                               base=1 - P, pattern=[[1, P]], channel_multiplier=1).then_inc(consts_ready, 1)

            for n in range(2):
                pool.wait_ge(sq_ready, 2 * n + 2)
                q = MIX + 2 * n * 1024
                pool.tensor_tensor(cols(q, 1024), cols(q, 1024), cols(q + 1024, 1024), ALU.add).then_inc(sq0_added, 1)

            pool.wait_ge(bias_staged, 1)
            pool.dma_start(scratch_bias, cols(BROW, T + P - 1)[0:HEADS, :]).then_inc(bias_out, 16)
            pool.wait_ge(bias_out, 16)
            toeplitz = bass.AP(tensor=scratch_bias.tensor, offset=0,
                               ap=[[1, P], [T + P - 1, HEADS], [1, T]])
            pool.dma_start(cols(BIAS_UP, HEADS * T, T), toeplitz).then_inc(bias_landed, 16)

            pool.wait_ge(xs_copied, 1)
            pool.wait_ge(w0_ready, 1)
            pool.tensor_tensor(cols(XW, 1024, HD), cols(XN, 1024, HD),
                               dts[:, 4, 0:16].unsqueeze(2).broadcast_to([P, 16, HD]), ALU.mult) \
                .then_inc(xw_ready, 1)
            pool.wait_ge(ssq_ready, 1)
            pool.tensor_tensor(mix[:, 8:16, :], convt[:, 0:8, :],
                               smalls[:, DSK:DSK + 8].unsqueeze(2).broadcast_to([P, 8, T]), ALU.mult) \
                .then_inc(skip_ready, 1)

            def add_sq(s):
                pool.wait_ge(sq_ready, s + (MIXER_SQUARES + 1))
                pool.tensor_tensor(sq1[:, 0, :], sq1[:, 0, :], sq1[:, s, :], ALU.add).then_inc(sq_added, 1)
            add_sq(1)
            with pool.Fori(2, NC - 1) as s:
                pool.wait_ge(sq_added, s - 1)
                add_sq(s)

            pool.wait_ge(evacuated, IN_TILES + NC)
            pool.dma_start(cols(SUBK, 2048), subkeys).then_inc(sub_landed, 16)
            pool.wait_ge(side_copied, 8)
            pool.dma_start(scratch_x1, cols(X1, TH * D)).then_inc(x1_saved, 16)

            def weigh(g, ready):
                pool.wait_ge(hot2_ready, ready)
                pool.tensor_tensor(hot2[:, :, :], hot2[:, :, :],
                                   route[:, 2, :].rearrange("p (g k) -> p g k", k=8)[:, g, :]
                                   .unsqueeze(2).broadcast_to([P, 8, KEYS]), ALU.mult).then_inc(weighed, 1)

            weigh(0, 1)
            with pool.Fori(1, NG) as g:
                weigh(g, g + 1)
            pool.wait_ge(x1_saved, 16)
            for n in range(4):
                pool.wait_ge(acted, 40 + 4 * n)
                pool.dma_start(cols(n * 1024, 1024), scratch_x1[:, n * 1024:(n + 1) * 1024]) \
                    .then_inc(tail_landed, 16)
            for n in range(2):
                pool.wait_ge(acted, 56 + 4 * n)
                pool.dma_start(cols(GAIN3 + n * PCOLS, PCOLS),
                               final_gain[n * PCOLS:(n + 1) * PCOLS].partition_broadcast(P)).then_inc(tail_landed, 16)
            pool.wait_ge(tail_landed, 16 * 6)
            for n in range(2):
                pool.wait_ge(final_y, n + 1)
                pool.tensor_tensor(cols(YG + n * PCOLS, PCOLS), cols(YT + n * PCOLS, PCOLS),
                                   cols(GAIN3 + n * PCOLS, PCOLS), ALU.mult).then_inc(final_gained, 1)

        @block.scalar
        def _(act):
            def hi(b, i, u):
                act.wait_ge(raw_landed[u], i * 16 + 16 * (b // PIECES + 1))
                if not (isinstance(i, int) and b + i * PIECES + u < 2):
                    act.wait_ge(w_hi_used, i * PIECES + (b + u - 1))
                    act.wait_ge(lo_ready, i * PIECES + (b + u - 1))
                act.activation(w_hi[:, u % 2, :], raw[:, u, :], ACT.Copy).then_inc(hi_ready, 1)

            def root(k, means, v, r):
                act.wait_ge(mean_ready, means)
                act.activation(r, v, ACT.Ln).then_inc(ln_ready, 1)
                act.wait_ge(ln_ready, k + 1)
                act.activation(r, r, ACT.Exp, scale=-0.5).then_inc(root_ready, 1)

            act.dma_start(smalls[:, :], smalls_in).then_inc(smalls_landed, 16)
            act.dma_start(cols(WDT, 256), w_dt).then_inc(wdt_landed, 16)
            act.dma_start(cols(RELB, 8)[0:BUCKETS, :], rel_bias).then_inc(bias_in_landed, 16)
            act.dma_start(cols(SEL, T + P - 1)[0:BUCKETS + 1, :], selectors).then_inc(bias_in_landed, 16)

            b = base["in"]
            for n in range(4):
                act.wait_ge(xg_ready, n + 1)
                act.activation(x_hi[:, 4 * n:4 * n + 4, :], xg[:, 4 * n:4 * n + 4, :], ACT.Copy) \
                   .then_inc(x_hi_ready, 1)
                if n % 2:
                    hi(b, 0, n // 2)
            act.wait_ge(wdt_landed, 16)
            act.activation(wdt_hi[:, :, :], cols(WDT, 256, SSM_HEADS), ACT.Copy).then_inc(wdt_hi_ready, 1)
            for n in range(4):
                act.activation(cols(MIX + n * 1024, 1024), cols(XT + n * 1024, 1024), ACT.Square) \
                   .then_inc(sq_ready, 1)
            hi(b, 0, 2)
            hi(b, 0, 3)
            root(0, 1, cols(CE, T), cols(FACTOR0, T))

            def silu_z(t0, t1, need):
                act.wait_ge(evacuated, need)
                act.activation(proj[:, Z0 + t0:Z0 + t1, :], proj[:, Z0 + t0:Z0 + t1, :], ACT.Silu) \
                   .then_inc(zsilu_ready, 1)

            def square_y(k, t0, t1):
                act.wait_ge(gated_y, k)
                act.activation(cols(CONVT + 2048 + t0 * T, (t1 - t0) * T), mix[:, 8 + t0:8 + t1, :], ACT.Square) \
                   .then_inc(sq_ready, 1)

            def m_upper(c0, c1, k):
                act.wait_ge(normed, k)
                act.activation(m_hi[:, c0:c1, :], mix[:, c0:c1, :], ACT.Copy).then_inc(m_hi_ready, 1)

            for p in range(PIECES, 2 * IN_TILES):
                hi(b, p // PIECES, p % PIECES)
                if p == 8:
                    act.wait_ge(dt_step, 1)
                    act.activation(dts[:, 2, :], dts[:, 1, :], ACT.Exp, scale=-1.0).then_inc(dt_act, 1)
                    act.activation(dts[:, 6, 0:16], smalls[:, ALOG:ALOG + 16], ACT.Exp).then_inc(dt_act, 1)
                if p == 10:
                    act.wait_ge(dt_step, 2)
                    act.activation(dts[:, 4, :], dts[:, 3, :], ACT.Ln).then_inc(dt_act, 1)
                if p in (18, 20):
                    n = (p - 18) // 2
                    act.wait_ge(bias_flipped, n + 1)
                    act.activation(cols(BIAS + n * 1024, 1024), flat[:, C:C + 1024], ACT.Copy).then_inc(bias_copied, 1)
                if p == 22:
                    act.wait_ge(dt_step, 3)
                    act.activation(dts[:, 4, 0:16], dts[:, 4, 0:16], ACT.Exp).then_inc(dt_act, 1)
                if p in (23, 25, 28):
                    t0, t1 = {23: (0, 8), 25: (8, 10), 28: (10, 12)}[p]
                    act.wait_ge(conv_ready, t1)
                    act.activation(convt[:, t0:t1, :], convt[:, t0:t1, :], ACT.Silu).then_inc(silu_ready, 1)
                if p in (26, 27):
                    n = p - 26
                    act.wait_ge(xs_t_ready, n + 1)
                    act.activation(cols(XN + n * 1024, 1024), flat[:, (A, B)[n]:(A, B)[n] + 1024], ACT.Copy) \
                       .then_inc(xs_copied, 1)
                if p == 32:
                    act.wait_ge(bc_ready, 1)
                    act.activation(cols(BN, 256), flat[:, C:C + 256], ACT.Copy).then_inc(bc_copied, 1)
                    act.activation(cols(CB, 512), flat[:, C + 512:C + 1024], ACT.Copy).then_inc(bc_copied, 1)
                if p == 36:
                    act.wait_ge(state_ready, 1)
                    act.activation(cols(PREV, 1024), flat[:, B:B + 1024], ACT.Copy).then_inc(state_copied, 1)
                n, at = (p - SSD_AT) // SSD_STEP, (p - SSD_AT) % SSD_STEP
                if n in (2, 3) and at == 3:
                    act.wait_ge(csb_read, n + 1)
                    if n == 3:
                        act.wait_ge(y_ready, 3)
                    act.activation(cols(CE, 1024), flat[:, A:A + 1024], ACT.Exp).then_inc(grow_ready, 1)
                if 0 <= n < 4 and at == 5:
                    act.wait_ge(seg_ready, n + 1)
                    act.activation(cols(SEG, 1024), cols(SEG, 1024), ACT.Exp).then_inc(decay_ready, 1)
                if EXP_AT <= p < EXP_AT + 4:
                    for n in range(4 * (p - EXP_AT), 4 * (p - EXP_AT) + 4):
                        act.wait_ge(negmax_ready, 1)
                        s = cols(SC0, 1024, P)[:, n, :] if n < HEADS else cols(SC1, 2048, T)[:, n - HEADS, :]
                        act.activation(s, s, ACT.Exp, bias=dts[:, 2, n:n + 1],
                                       accum_out=dts[:, 3, n:n + 1]).then_inc(exp_ready, 1)
                if p in (VT_AT + 2, VT_AT + 3):
                    n = p - VT_AT - 2
                    act.wait_ge(vt_ready, n + 1)
                    act.activation(cols(VN + n * 1024, 1024), flat[:, (A, B)[n]:(A, B)[n] + 1024], ACT.Copy) \
                       .then_inc(v_copied, 1)
                if PT_AT + 2 <= p < PT_AT + 5:
                    n = p - PT_AT - 2
                    act.wait_ge(pt_ready, n + 1)
                    act.activation(cols(PT + n * 1024, 1024), flat[:, (A, B, C)[n]:(A, B, C)[n] + 1024], ACT.Copy) \
                       .then_inc(pt_copied, 1)
                if p in (ATT_AT + 2, ATT_AT + 3):
                    n = p - ATT_AT - 2
                    act.wait_ge(att_ready, n + 1)
                    act.activation(cols(MIX + n * 1024, 1024), flat[:, (A, B)[n]:(A, B)[n] + 1024], ACT.Copy) \
                       .then_inc(att_copied, 1)
                    act.activation(cols(CONVT + n * 1024, 1024), flat[:, (A, B)[n]:(A, B)[n] + 1024], ACT.Square) \
                       .then_inc(sq_ready, 1)
                if p == NORM_AT:
                    silu_z(0, 4, Z0 + 4)
                if p == NORM_AT + 1:
                    root(1, 2, cols(SEG, T), cols(MT, T))
                if p == NORM_AT + 2:
                    square_y(1, 0, 4)
                if p == NORM_AT + 5:
                    m_upper(0, 8, 1)

            b = base["out"]
            hi(b, 0, 0)
            silu_z(4, 7, Z0 + 7)
            hi(b, 0, 1)
            silu_z(7, 8, IN_TILES)
            square_y(2, 4, 7)
            square_y(3, 7, 8)
            hi(b, 0, 2)
            hi(b, 0, 3)
            root(2, 4, cols(SEG + T, 2 * T), cols(MT + T, 2 * T))
            hi(b, 1, 0)
            m_upper(8, 12, 2)
            m_upper(12, 16, 3)

            def take_x1(s, ring):
                act.wait_ge(x1g_ready, s + 1)
                act.activation(x_hi[:, s, :], cols(X1G + ring * T, T), ACT.Copy).then_inc(x_hi_ready, 1)
                act.activation(sq1[:, s, :], x1t[:, s, :], ACT.Square).then_inc(sq_ready, 1)

            for p in range(5, 3 * PIECES):
                hi(b, p // PIECES, p % PIECES)
                if 6 <= p < 10:
                    take_x1(p - 6, p % 2)
                if p == 11:
                    take_x1(4, 0)

            def out_pair(i):
                for u in range(PIECES):
                    hi(b, i, u)
                    if u % 2:
                        take_x1(i * 2 + (u // 2 - 1), (u // 2 + 1) % 2)
            pairs(act, out_pair, 3, NC // 2)

            b = base["q"]
            for u in range(2):
                hi(b, 0, u)
            take_x1(NC - 1, 1)
            for u in range(2, PIECES):
                hi(b, 0, u)
            root(3, 5, cols(CAND, T), factor2)

            def plain_pair(i):
                for u in range(PIECES):
                    hi(b, i, u)
            pairs(act, plain_pair, 1, NC // 2)

            def gelu(i, bank):
                act.wait_ge(scaled, i * 2 + (bank + 1))
                if not (isinstance(i, int) and i == 0):
                    act.wait_ge(h_stored[bank], i * 16)
                act.activation(gelu_out[bank], ps[:, bank, 0:T], ACT.Gelu).then_inc(evacuated, 1)

            b = base["u"]

            def u_piece(i, u):
                hi(b, i, u)
                if u % 2 == 0 and not (isinstance(i, int) and i == 0):
                    gelu(i - 1, u // 2)

            for p in range(16):
                u_piece(p // PIECES, p % PIECES)
                if 5 <= p < 13:
                    n = p - 5
                    dst = (SCORES if n < 4 else X1) + n % 4 * 1024
                    act.wait_ge(side_ready, n + 1)
                    act.activation(cols(dst, 1024), flat[:, (A, B, C)[n % 3]:(A, B, C)[n % 3] + 1024], ACT.Copy) \
                       .then_inc(side_copied, 1)

            def u_pair(i):
                for u in range(PIECES):
                    u_piece(i, u)
            pairs(act, u_pair, 4, GATES_AT - 1)
            for u in range(PIECES):
                u_piece(GATES_AT - 1, u)
                if u == 0:
                    act.wait_ge(gate_sub, 1)
                    act.activation(cols(PICKV, 256), cols(PICKV, 256), ACT.Exp).then_inc(gate_exp, 1)
                if u == 3:
                    act.wait_ge(picks_t_ready, 1)
                    act.activation(route[:, :, :], flat[:, A:A + 768].rearrange("p (a b) -> p a b", b=T),
                                   ACT.Copy).then_inc(route_ready, 1)
            u_pair(GATES_AT)
            act.wait_ge(x1_saved, 16)
            with act.Fori(GATES_AT + 1, GATES_AT + 1 + NG) as i:
                for u in range(PIECES):
                    u_piece(i, u)
                    if u == 2:
                        act.wait_ge(gates_ready, i - GATES_AT)
                        act.activation(G_by_token[:, i - (GATES_AT + 1), :, :],
                                       flat[:, A:A + 1024].rearrange("p (k i) -> p k i", i=KEYS), ACT.Copy) \
                           .then_inc(gates_copied, 1)
            pairs(act, u_pair, GATES_AT + 1 + NG, KEYS // 2)

            b = base["v"]

            def v_pair(i):
                for u in range(PIECES):
                    hi(b, i, u)
                    if u % 2 == 0:
                        act.wait_ge(acted, i * 2 + (u // 2 + 1))
                        act.wait_ge(w_used, i * PIECES + (b + u - 2))
                        act.activation(x_hi[:, u // 2, :], act_f[:, u // 2, :], ACT.Copy).then_inc(a_hi_ready, 1)
            hi(b, 0, 0)
            gelu(KEYS // 2 - 1, 0)
            for n in range(2):
                act.wait_ge(acted, n + 1)
                act.wait_ge(w_used, b - 1)
                act.activation(x_hi[:, n, :], act_f[:, n, :], ACT.Copy).then_inc(a_hi_ready, 1)
            hi(b, 0, 1)
            gelu(KEYS // 2 - 1, 1)
            hi(b, 0, 2)
            hi(b, 0, 3)
            pairs(act, v_pair, 1, KEYS // 2)

            act.wait_ge(gelu_free, 1)
            act.activation(dts[:, 8, 2:3], dts[:, 8, 0:1], ACT.Sqrt)

            def square3(n):
                act.wait_ge(final_y, n + 1)
                act.activation(cols(YSQ + n * PCOLS, PCOLS), cols(YT + n * PCOLS, PCOLS), ACT.Square,
                               accum_out=dts[:, 7, n:n + 1]).then_inc(final_sq, 1)

            def root3(th):
                act.wait_ge(final_mean, th + 1)
                act.activation(dts[:, 1, th:th + 1], dts[:, 3, th:th + 1], ACT.Sqrt).then_inc(final_root, 1)

            def scale3(n):
                act.wait_ge(final_factor, 1)
                act.wait_ge(final_gained, n + 1)
                act.activation(cols(YT + n * PCOLS, PCOLS), cols(YG + n * PCOLS, PCOLS), ACT.Copy,
                               scale=dts[:, 5, 0:1]).then_inc(final_ready[0], 1)

            for n in range(2):
                square3(n)
            root3(0)
            for n in range(2, 4):
                square3(n)
            scale3(0)
            root3(1)
            scale3(1)

        @block.tensor
        def _(pe):
            def ssq(need, tiles, dst, need_last=None):
                pe.wait_ge(sq_ready, need)
                for c, tile in enumerate(tiles):
                    if need_last and c == len(tiles) - 1:
                        pe.wait_ge(sq_ready, need_last)
                    last = pe.matmul(dst, ones, tile, start=(c == 0), stop=(c == len(tiles) - 1))
                last.then_inc(ssq_ready, 1)

            def piece(b, i, u, xh, xl, slab=None, half=None, late=None):
                first = isinstance(i, int) and b == 0 and i == 0
                if slab is None:
                    slab, half = u // 2, u % 2
                if half == 0 and slab < 2 and not first:
                    pe.wait_ge(evacuated, i * 2 + (b // 2 + slab - 1))
                pe.wait_ge(hi_ready, i * PIECES + (b + u + 1))
                dst = ps[:, slab, 0:T]
                c0 = half * (NC // 2)
                for c in range(NC // 2):
                    if late and c0 + c == late[0]:
                        pe.wait_ge(late[1], late[2])
                    wh = w_hi[:, u % 2, c * P:(c + 1) * P]
                    pe.matmul(dst, wh, xh[:, c0 + c, :], start=(c0 + c == 0), stop=False)
                    last = pe.matmul(dst, wh, xl[:, c0 + c, :], start=False, stop=False)
                last.then_inc(w_hi_used, 1)
                pe.wait_ge(lo_ready, i * PIECES + (b + u + 1))
                for c in range(NC // 2):
                    last = pe.matmul(dst, w_lo[:, u % 2, c * P:(c + 1) * P], xh[:, c0 + c, :],
                                     start=False, stop=(c0 + c == NC - 1))
                last.then_inc(w_used, 1)

            b = base["in"]

            def in_piece(p):
                piece(b, p // PIECES, p % PIECES, x_hi, x_lo)

            def in_to(p0, p1):
                while p0 < p1 and p0 % PIECES:
                    in_piece(p0)
                    p0 += 1
                whole = (p1 - p0) // PIECES
                if whole > 0:
                    def one(i):
                        for u in range(PIECES):
                            piece(b, i, u, x_hi, x_lo)
                    pairs(pe, one, p0 // PIECES, p0 // PIECES + whole)
                    p0 += whole * PIECES
                for p in range(p0, p1):
                    in_piece(p)

            pe.wait_ge(consts_ready, 6)
            pe.wait_ge(x_lo_ready, 2)
            in_piece(0)
            pe.wait_ge(x_lo_ready, 4)
            in_piece(1)
            in_piece(2)
            pe.wait_ge(sq0_added, 2)
            ssq(4, [mix[:, c, :] for c in (0, 1, 2, 3, 8, 9, 10, 11)], flat[:, A:A + T])
            pe.wait_ge(bias_row, 1)
            pe.matmul(ps[0:HEADS, 3, 0:T + P - 1], cols(RELB, 8)[0:BUCKETS + 1, :],
                      cols(SEL, T + P - 1)[0:BUCKETS + 1, :], start=True, stop=True).then_inc(bias_row, 1)
            in_piece(3)
            pe.wait_ge(wdt_lo_ready, 1)
            for c in range(NC):
                for w, x in ((wdt_hi, x_hi), (wdt_hi, x_lo), (wdt_lo, x_hi)):
                    last = pe.matmul(ps[0:SSM_HEADS, 4, 0:T], w[:, c, :], x[:, c, :],
                                     start=(c == 0 and x is x_hi and w is wdt_hi), stop=(c == NC - 1 and w is wdt_lo))
            last.then_inc(dtraw_ready, 1)
            in_to(4, 6)
            pe.wait_ge(dt_scaled, 1)
            for th in range(TH):
                last = pe.transpose(flat[:, B + 512 + th * 16:B + 528 + th * 16],
                                    cols(DTF + th * P, P)[0:SSM_HEADS, :], ident[0:SSM_HEADS, 0:SSM_HEADS])
            last.then_inc(dt_t_ready, 1)
            in_to(6, 16)
            pe.wait_ge(da_ready, 1)
            pe.matmul(flat[:, B + 64:B + 96], tri, dts[:, 5, :], start=True, stop=True)
            pe.matmul(flat[:, B + 96:B + 112], ones, dts[:, 5, 0:16], start=True, stop=True) \
              .then_inc(cs_ready, 1)
            pe.wait_ge(bias_landed, 16)
            for n in range(2):
                if n:
                    in_to(16, 19)
                    pe.wait_ge(bias_copied, 1)
                for m in range(2):
                    last = pe.matmul(flat[:, C + m * 512:C + (m + 1) * 512], flip,
                                     cols(BIAS_UP + n * 1024 + m * 512, 512), start=True, stop=True)
                last.then_inc(bias_flipped, 1)
            in_to(19, 25)
            pe.wait_ge(silu_ready, 1)
            pe.wait_ge(dt_step, 3)
            pe.wait_ge(bias_staged, 1)
            for ch in range(2):
                for j in range(8):
                    last = pe.transpose(flat[:, (A, B)[ch] + j * P:(A, B)[ch] + (j + 1) * P],
                                        convt[:, j, ch * P:(ch + 1) * P], ident[:, :])
                last.then_inc(xs_t_ready, 1)

            def running(n):
                ch, g = n // 2, n % 2
                if n:
                    pe.wait_ge(csb_read, n)
                if n == 3:
                    pe.wait_ge(grow_ready, 1)
                for r in range(8):
                    h = ch * 16 + g * 8 + r
                    last = pe.matmul(flat[:, A + r * P:A + (r + 1) * P], dts[:, 5, h:h + 1].broadcast_to([P, P]),
                                     tri, start=True, stop=True)
                last.then_inc(csb_ready, 1)

            def b_and_cb():
                pe.wait_ge(silu_ready, 3)
                pe.wait_ge(bias_copied, 2)
                for g in range(GROUPS):
                    pe.transpose(flat[:, C + g * P:C + (g + 1) * P], convt[:, 8 + g, 0:P], ident[:, :])
                for n in range(4):
                    tok = slice(n // 2 * P, (n // 2 + 1) * P)
                    last = pe.matmul(flat[:, C + 512 + n * P:C + 512 + (n + 1) * P], convt[:, 8 + n % 2, tok],
                                     convt[:, 10 + n % 2, tok], start=True, stop=True)
                last.then_inc(bc_ready, 1)

            def state():
                pe.wait_ge(xw_ready, 1)
                pe.wait_ge(bc_copied, 1)
                pe.wait_ge(xs_copied, 2)
                for g in range(GROUPS):
                    last = pe.matmul(flat[:, B + g * 512:B + (g + 1) * 512], cols(BN, 256, P)[:, g, :],
                                     cols(XW + g * 512, 512), start=True, stop=True)
                last.then_inc(state_ready, 1)

            def outputs(n):
                ch, g = n // 2, n % 2
                pe.wait_ge(m_ready, n + 1)
                pe.wait_ge(bc_copied, 2)
                if ch == 1:
                    pe.wait_ge(state_copied, 1)
                    pe.wait_ge(grown, n - 1)
                if n >= 2:
                    pe.wait_ge(y_added, n - 1)
                for r in range(8):
                    head = g * 8 + r
                    rows = slice((r % 2) * HD, (r % 2 + 1) * HD)
                    dst = ps[rows, 6 + n % 2, (r // 2) * P:(r // 2 + 1) * P]
                    last = pe.matmul(dst, cols(XN + ch * 1024 + head * HD, HD), cols(MT + r * P, P),
                                     start=True, stop=(ch == 0))
                    if ch == 1:
                        last = pe.matmul(dst, cols(PREV + head * HD, HD), cols(CE + r * P, P),
                                         start=False, stop=True)
                last.then_inc(y_ready, 1)

            done = 25
            in_to(done, SSD_AT + 2)
            done = SSD_AT + 2
            pe.wait_ge(xs_copied, 1)
            running(0)
            in_to(done, 31)
            b_and_cb()
            in_to(31, 34)
            running(1)
            state()
            in_to(34, 35)
            outputs(0)
            in_to(35, 41)
            running(2)
            in_to(41, 42)
            outputs(1)
            in_to(42, 48)
            running(3)
            in_to(48, 49)
            outputs(2)
            in_to(49, 56)
            outputs(3)
            in_to(56, SCORES_AT + 1)
            pe.wait_ge(evacuated, V0)
            pe.wait_ge(y_added, 4)
            for h in range(HEADS):
                last = pe.matmul(flat[:, A + h * T:A + (h + 1) * T], proj[:, Q0 + h, P:T], proj[:, K0 + h, :],
                                 start=True, stop=True)
            last.then_inc(qk_ready, 1)
            in_to(SCORES_AT + 1, SCORES_AT + 2)
            for h in range(HEADS):
                last = pe.matmul(flat[:, C + h * P:C + (h + 1) * P], proj[:, Q0 + h, 0:P],
                                 proj[:, K0 + h, 0:P], start=True, stop=True)
            last.then_inc(qk_ready, 1)
            in_to(SCORES_AT + 2, PT_AT + 1)
            pe.wait_ge(probs_ready, 1)
            for n in range(24):
                if n < HEADS:
                    src = cols(SC0, 1024, P)[:, n, :]
                else:
                    h, sc = (n - HEADS) // 2, (n - HEADS) % 2
                    src = cols(SC1, 2048, T)[:, h, sc * P:(sc + 1) * P]
                last = pe.transpose(flat[:, A + n * P:A + (n + 1) * P], src, ident[:, :])
                if n % 8 == 7:
                    last.then_inc(pt_ready, 1)
            in_to(PT_AT + 1, VT_AT + 1)
            pe.wait_ge(evacuated, Z0)
            pe.wait_ge(pt_copied, 2)
            for sc in range(TH):
                for h in range(HEADS):
                    last = pe.transpose(flat[:, (A, B)[sc] + h * P:(A, B)[sc] + (h + 1) * P],
                                        proj[:, V0 + h, sc * P:(sc + 1) * P], ident[:, :])
                last.then_inc(vt_ready, 1)
            in_to(VT_AT + 1, ATT_AT + 1)
            pe.wait_ge(v_copied, 2)
            pe.wait_ge(pt_copied, 3)
            pt = cols(PT, 3072, P)
            vn = cols(VN, 2048, P)
            for h in range(HEADS):
                pe.matmul(flat[:, A + h * T:A + h * T + P], vn[:, h, :], pt[:, h, :], start=True, stop=True)
                for sc in range(TH):
                    last = pe.matmul(flat[:, A + h * T + P:A + (h + 1) * T], vn[:, sc * 8 + h, :],
                                     pt[:, HEADS + h * 2 + sc, :], start=(sc == 0), stop=(sc == 1))
                if h % 4 == 3:
                    last.then_inc(att_ready, 1)
            in_to(ATT_AT + 1, NORM_AT - 1)
            ssq(6, [convt[:, c, :] for c in range(8)], flat[:, C:C + T])
            in_to(NORM_AT - 1, NORM_AT + 3)
            ssq(7, [convt[:, 8 + c, :] for c in range(4)], flat[:, C + 512:C + 512 + T])
            in_to(NORM_AT + 3, 2 * IN_TILES)

            b = base["out"]
            pe.wait_ge(m_lo_ready, 1)
            for u in range(2):
                piece(b, 0, u, m_hi, m_lo, u, 0)
            ssq(8, [cols(CONVT + 2048 + (4 + c) * T, T) for c in range(4)], flat[:, B:B + T], 9)
            for u in range(2, PIECES):
                piece(b, 0, u, m_hi, m_lo, u, 0)
            pe.wait_ge(m_lo_ready, 2)
            piece(b, 1, 0, m_hi, m_lo, 0, 1, (12, m_lo_ready, 3))
            for u in range(1, PIECES):
                piece(b, 1, u, m_hi, m_lo, u, 1)

            def out_pair(i):
                for u in range(PIECES):
                    piece(b, i, u, m_hi, m_lo)
            pairs(pe, out_pair, 2, NC // 2)
            b = base["q"]
            pe.wait_ge(x_lo_ready, 4 + NC // 2)
            piece(b, 0, 0, x_hi, x_lo)
            pe.wait_ge(x_lo_ready, 4 + NC - 1)
            piece(b, 0, 1, x_hi, x_lo, None, None, (NC - 1, x_lo_ready, 4 + NC))
            pe.wait_ge(sq_added, NC - 2)
            ssq(MIXER_SQUARES + NC, [sq1[:, c, :] for c in (0, NC - 1)], flat[:, A:A + T])
            for u in range(2, PIECES):
                piece(b, 0, u, x_hi, x_lo)

            def x_pair(i):
                for u in range(PIECES):
                    piece(b, i, u, x_hi, x_lo)
            pairs(pe, x_pair, 1, NC // 2)

            b = base["u"]
            for p in range(12):
                piece(b, p // PIECES, p % PIECES, x_hi, x_lo)
                if p >= 4:
                    n = p - 4
                    bank = (A, B, C)[n % 3]
                    if n == 0:
                        pe.wait_ge(evacuated, IN_TILES + 2 * NC)
                        pe.wait_ge(sub_landed, 16)
                    if n >= 3:
                        pe.wait_ge(side_copied, n - 2)
                    th, c0 = n % 4 // 2, n % 2 * 8
                    for c in range(8):
                        dst = flat[:, bank + c * P:bank + (c + 1) * P]
                        if n < 4:
                            last = pe.matmul(dst, qt[:, c0 + c, th * P:(th + 1) * P],
                                             cols(SUBK, 2048, P)[:, c0 + c, :], start=True, stop=True)
                        else:
                            last = pe.transpose(dst, x1t[:, c0 + c, th * P:(th + 1) * P], ident[:, :])
                    last.then_inc(side_ready, 1)
            pairs(pe, x_pair, 3, GATES_AT - 1)
            for u in range(PIECES):
                piece(b, GATES_AT - 1, u, x_hi, x_lo)
                if u == 2:
                    pe.wait_ge(picks_ready, 1)
                    for a in range(3):
                        for th in range(TH):
                            last = pe.transpose(flat[:, A + a * T + th * P:A + a * T + (th + 1) * P],
                                                cols(KEEP + (a * TH + th) * P, P), ident[:, :])
                    last.then_inc(picks_t_ready, 1)
            x_pair(GATES_AT)

            def gates_pair(i):
                for u in range(PIECES):
                    piece(b, i, u, x_hi, x_lo)
                    if u == 0:
                        pe.wait_ge(weighed, i - GATES_AT)
                        pe.wait_ge(hot1_ready, i - GATES_AT)
                        if not isinstance(i, int):
                            pe.wait_ge(gates_copied, i - (GATES_AT + 1))
                        for k in range(8):
                            last = pe.matmul(flat[:, A + k * P:A + (k + 1) * P], hot2[:, k, :], hot1[:, k, :],
                                             start=True, stop=True)
                        last.then_inc(gates_ready, 1)
            gates_pair(GATES_AT + 1)
            with pe.Fori(GATES_AT + 2, GATES_AT + 1 + NG) as i:
                gates_pair(i)
            pairs(pe, x_pair, GATES_AT + 1 + NG, KEYS // 2)

            b = base["v"]
            pe.wait_ge(gates_copied, NG)

            def second(i, u, start, stop, token_halves=(0, 1)):
                a = u // 2
                bank = (1 - u % 2) * 2
                pe.wait_ge(hi_ready, i * PIECES + (b + u + 1))
                if u % 2 == 0:
                    pe.wait_ge(a_lo_ready, i * 2 + (a + 1))

                def products(x, w, start, stop):
                    for th in token_halves:
                        for n in range(2):
                            last = pe.matmul(ps[:, th * 4 + bank + n, :], x[:, a, th * P:(th + 1) * P],
                                             w[:, u % 2, n * 512:(n + 1) * 512], start=start, stop=stop)
                    return last
                products(x_hi, w_hi, start, False)
                last = products(x_lo, w_hi, False, False)
                if 1 in token_halves:
                    last.then_inc(w_hi_used, 1)
                pe.wait_ge(lo_ready, i * PIECES + (b + u + 1))
                last = products(x_hi, w_lo, False, stop)
                if 1 in token_halves:
                    last.then_inc(w_used, 1)
                elif u == PIECES - 1:
                    last.then_inc(first_half_done, 1)

            for u in range(PIECES):
                if u == 1:
                    pe.wait_ge(evacuated, IN_TILES + 2 * NC + KEYS)
                second(0, u, u < 2, False)
            with pe.Fori(1, KEYS // 2 - 1) as i:
                for u in range(PIECES):
                    second(i, u, False, False)
            for u in range(2):
                second(KEYS // 2 - 1, u, False, False)
            for th in range(TH):
                for u in range(2, PIECES):
                    second(KEYS // 2 - 1, u, False, True, (th,))

        @block.vector
        def _(dve):
            link, chained, settle = linker(dve, dve_chain)

            def mean(sums, features, v):
                dve.tensor_scalar(v, sums, 1.0 / features, EPS, ALU.mult, ALU.add).then_inc(mean_ready, 1)

            def newton(k, v, r, t):
                dve.wait_ge(root_ready, k + 1)
                link(dve.tensor_tensor(t, r, r, ALU.mult))
                link(dve.tensor_tensor(t, t, v, ALU.mult))
                link(dve.tensor_scalar(t, t, -0.5, 1.5, ALU.mult, ALU.add))
                dve.tensor_tensor(r, r, t, ALU.mult).then_inc(factor_ready, 1)
                dve.wait_ge(factor_ready, k + 1)

            def lo(b, i, u):
                dve.wait_ge(hi_ready, i * PIECES + (b + u + 1))
                if not (isinstance(i, int) and b + i * PIECES + u < 2):
                    dve.wait_ge(w_used, i * PIECES + (b + u - 1))
                dve.tensor_tensor(w_lo[:, u % 2, :], raw[:, u, :], w_hi[:, u % 2, :].bitcast(F32),
                                  ALU.subtract).then_inc(lo_ready, 1)

            def slab_done(slab):
                dve.wait_ge(w_used, slab * 2 + 2)

            dve.wait_ge(smalls_landed, 16)
            b = base["in"]
            for half in range(2):
                for n in (2 * half, 2 * half + 1):
                    dve.wait_ge(x_landed[n], 16)
                    for c in range(4 * n, 4 * n + 4):
                        ins = dve.tensor_scalar(xg[:, c, :], xt[:, c, :], smalls[:, G1 + c:G1 + c + 1], None, ALU.mult)
                    ins.then_inc(xg_ready, 1)
                for n in (2 * half, 2 * half + 1):
                    dve.wait_ge(x_hi_ready, n + 1)
                    dve.tensor_tensor(x_lo[:, 4 * n:4 * n + 4, :], xg[:, 4 * n:4 * n + 4, :],
                                      x_hi_f[:, 4 * n:4 * n + 4, :], ALU.subtract).then_inc(x_lo_ready, 1)
                lo(b, 0, half)
            dve.wait_ge(wdt_hi_ready, 1)
            dve.tensor_tensor(wdt_lo[:, :, :], cols(WDT, 256, SSM_HEADS), wdt_hi[:, :, :].bitcast(F32), ALU.subtract) \
               .then_inc(wdt_lo_ready, 1)
            dve.memset(cols(RELB, 8)[BUCKETS:BUCKETS + 1, :], -BIG)
            dve.wait_ge(bias_in_landed, 32)
            dve.memset(cols(BROW, T + P - 1), 0.0).then_inc(bias_row, 1)
            f0 = cols(FACTOR0, T)
            lo(b, 0, 2)
            lo(b, 0, 3)
            dve.wait_ge(ssq_ready, 1)
            mean(flat[:, A:A + T], D, cols(CE, T))
            newton(0, cols(CE, T), f0, cols(CE + T, T))
            dve.wait_ge(bias_row, 2)
            dve.tensor_copy(cols(BROW, T + P - 1)[0:HEADS, :], ps[0:HEADS, 3, 0:T + P - 1]) \
               .then_inc(bias_staged, 1)

            both = lambda a: smalls[:, a:a + 16].unsqueeze(1).broadcast_to([P, 2, 16])
            two = lambda k: dts[:, k, :].rearrange("p (a b) -> p a b", b=16)
            s0, s1 = cols(SC0, 1024, P), cols(SC1, 2048, T)
            bias = cols(BIAS, HEADS * T, T)
            scale = float(P) ** -0.5
            seg, mt, ce = cols(SEG, 1024, P), cols(MT, 1024, P), cols(CE, 1024, P)

            def project(s):
                slab_done(s)
                dve.tensor_tensor(proj[:, s, :], ps[:, s % 2, 0:T], f0, ALU.mult).then_inc(evacuated, 1)

            def convolve(j):
                dve.wait_ge(evacuated, j + 1)
                w = lambda k: smalls[:, CONVW + j * CONV + k:CONVW + j * CONV + k + 1]
                dve.tensor_scalar(convt[:, j, :], proj[:, XBC0 + j, :], w(CONV - 1),
                                  smalls[:, CONVB + j:CONVB + j + 1], ALU.mult, ALU.add).then_inc(conv_step, 1)
                for back in range(1, CONV):
                    dve.wait_ge(conv_step, j * (CONV - 1) + back)
                    dve.scalar_tensor_tensor(out=convt[:, j, back:T], in0=proj[:, XBC0 + j, 0:T - back],
                                             scalar=w(CONV - 1 - back), in1=convt[:, j, back:T],
                                             op0=ALU.mult, op1=ALU.add) \
                       .then_inc(conv_step if back < CONV - 1 else conv_ready, 1)

            def ssd(n, at):
                ch, g = n // 2, n % 2
                heads = slice(ch * 16 + g * 8, ch * 16 + g * 8 + 8)
                tok = slice(ch * P, (ch + 1) * P)
                if at == 2:
                    dve.wait_ge(csb_ready, n + 1)
                    if n:
                        dve.wait_ge(m_ready, n)
                    dve.tensor_tensor(seg, flat[:, A:A + 1024].rearrange("p (a b) -> p a b", b=P),
                                      dts[:, 1, heads].unsqueeze(2).broadcast_to([P, 8, P]), ALU.subtract) \
                       .then_inc(csb_read, 1)
                if at == 3:
                    dve.wait_ge(csb_read, n + 1)
                    dve.tensor_tensor(seg, seg, future.unsqueeze(1).broadcast_to([P, 8, P]), ALU.add) \
                       .then_inc(seg_ready, 1)
                if at == 5 and ch == 1:
                    dve.wait_ge(grow_ready, n - 1)
                    dve.tensor_tensor(ce, ce, convt[:, 10 + g, tok].unsqueeze(1).broadcast_to([P, 8, P]),
                                      ALU.mult).then_inc(grown, 1)
                if at == 6:
                    dve.wait_ge(decay_ready, n + 1)
                    dve.wait_ge(bc_copied, 2)
                    link(dve.tensor_tensor(seg, seg, cols(CB + n * P, P).unsqueeze(1).broadcast_to([P, 8, P]),
                                           ALU.mult))
                if at == 7:
                    if n:
                        dve.wait_ge(y_ready, n)
                    dve.tensor_tensor(mt, seg, dts[:, 0, heads].unsqueeze(2).broadcast_to([P, 8, P]), ALU.mult) \
                       .then_inc(m_ready, 1)
                if at == 10:
                    dve.wait_ge(y_ready, n + 1)
                    dve.wait_ge(skip_ready, 1)
                    y = mix[:, 8 + g * 4:12 + g * 4, tok]
                    dve.tensor_tensor(y, ps[:, 6 + n % 2, :].rearrange("p (a b) -> p a b", b=P), y, ALU.add) \
                       .then_inc(y_added, 1)

            def gate_y(k, t0, t1):
                dve.wait_ge(zsilu_ready, k)
                y = mix[:, 8 + t0:8 + t1, :]
                dve.tensor_tensor(y, y, proj[:, Z0 + t0:Z0 + t1, :], ALU.mult).then_inc(gated_y, 1)

            norm_at = lambda k: tuple(cols(a + (k - 1) * T, T) for a in (SEG, MT, CE))

            def norm(k, c0, c1, signal=True):
                for c in range(c0, c1):
                    ins = dve.scalar_tensor_tensor(out=mix[:, c, :], in0=mix[:, c, :],
                                                   scalar=smalls[:, GMIX + c:GMIX + c + 1], in1=norm_at(k)[1],
                                                   op0=ALU.mult, op1=ALU.mult)
                if signal:
                    ins.then_inc(normed, 1)

            def m_lower(k, c0, c1):
                dve.wait_ge(m_hi_ready, k)
                dve.tensor_tensor(m_lo[:, c0:c1, :], mix[:, c0:c1, :], m_hi_f[:, c0:c1, :], ALU.subtract) \
                   .then_inc(m_lo_ready, 1)

            for p in range(3, 2 * IN_TILES):
                if p > 3:
                    lo(b, p // PIECES, p % PIECES)
                if p == NORM_AT:
                    dve.wait_ge(ssq_ready, 2)
                    mean(flat[:, C:C + T], 1024, norm_at(1)[0])
                if p == NORM_AT + 1:
                    gate_y(1, 0, 4)
                if p == NORM_AT + 2:
                    newton(1, *norm_at(1))
                if p == NORM_AT + 3:
                    dve.wait_ge(att_copied, 2)
                    norm(1, 0, 3, False)
                if p == NORM_AT + 4:
                    dve.wait_ge(ssq_ready, 3)
                    mean(flat[:, C + 512:C + 512 + T], 512, norm_at(2)[0])
                    norm(1, 3, 8)
                if p == 4:
                    dve.wait_ge(dtraw_ready, 1)
                    dve.tensor_tensor(cols(DTF, T)[0:SSM_HEADS, :], ps[0:SSM_HEADS, 4, 0:T], f0[0:SSM_HEADS, :],
                                      ALU.mult).then_inc(dt_scaled, 1)
                if p % 2:
                    s = (p - 3) // 2
                    project(s)
                    if s < CONV_TILES:
                        convolve(s)
                if p == 7:
                    dve.wait_ge(dt_t_ready, 1)
                    link(dve.tensor_tensor(two(0), flat[:, B + 512:B + 544].rearrange("p (a b) -> p a b", b=16),
                                           both(DTB), ALU.add))
                    link(dve.tensor_scalar(dts[:, 1, :], dts[:, 0, :], -1.0, None, ALU.mult))
                    dve.tensor_tensor(dts[:, 1, :], dts[:, 0, :], dts[:, 1, :], ALU.max).then_inc(dt_step, 1)
                if p == 9:
                    dve.wait_ge(dt_act, 2)
                    dve.tensor_scalar(dts[:, 3, :], dts[:, 2, :], 1.0, None, ALU.add).then_inc(dt_step, 1)
                    dve.wait_ge(dt_step, 2)
                    link(dve.tensor_scalar(dts[:, 7, :], dts[:, 3, :], -1.0, None, ALU.add))
                    link(dve.tensor_tensor(dts[:, 7, :], dts[:, 2, :], dts[:, 7, :], ALU.subtract))
                    link(dve.reciprocal(dts[:, 8, :], dts[:, 3, :]))
                    link(dve.tensor_tensor(dts[:, 7, :], dts[:, 7, :], dts[:, 8, :], ALU.mult))
                if p == 11:
                    dve.wait_ge(dt_act, 3)
                    link(dve.tensor_tensor(dts[:, 7, :], dts[:, 7, :], dts[:, 4, :], ALU.add))
                    link(dve.scalar_tensor_tensor(out=dts[:, 0, :], in0=dts[:, 0, :], scalar=0.0, in1=dts[:, 7, :],
                                                  op0=ALU.max, op1=ALU.add))
                    link(dve.tensor_scalar(dts[:, 6, 0:16], dts[:, 6, 0:16], -1.0, None, ALU.mult))
                    dve.tensor_tensor(two(5), two(0), dts[:, 6, 0:16].unsqueeze(1).broadcast_to([P, 2, 16]),
                                      ALU.mult).then_inc(da_ready, 1)
                if p == 20:
                    dve.wait_ge(cs_ready, 1)
                    link(dve.tensor_copy(dts[:, 1, :], flat[:, B + 64:B + 96]))
                    dve.tensor_tensor(dts[:, 4, 0:16], flat[:, B + 96:B + 112], dts[:, 1, 0:16], ALU.subtract) \
                       .then_inc(dt_step, 1)
                if p == 24:
                    dve.wait_ge(dt_act, 4)
                    dve.tensor_tensor(dts[:, 4, 0:16], dts[:, 4, 0:16], dts[:, 0, 0:16], ALU.mult) \
                       .then_inc(w0_ready, 1)
                for n in range(4):
                    ssd(n, p - (SSD_AT + SSD_STEP * n))
                if p in (SCORES_AT + 2, SCORES_AT + 3):
                    h0 = 4 * (p - SCORES_AT - 2)
                    dve.wait_ge(qk_ready, 1)
                    dve.wait_ge(bias_copied, 2)
                    link(dve.scalar_tensor_tensor(
                        out=s1[:, h0:h0 + 4, :],
                        in0=flat[:, A + h0 * T:A + (h0 + 4) * T].rearrange("p (a b) -> p a b", b=T),
                        scalar=scale, in1=bias[:, h0:h0 + 4, :], op0=ALU.mult, op1=ALU.add))
                if p == SCORES_AT + 4:
                    dve.wait_ge(qk_ready, 2)
                    link(dve.scalar_tensor_tensor(out=s0, in0=flat[:, C:C + 1024].rearrange("p (a b) -> p a b", b=P),
                                                  scalar=scale, in1=bias[:, :, P:T], op0=ALU.mult, op1=ALU.add))
                if p in (SCORES_AT + 5, SCORES_AT + 6):
                    h0 = 4 * (p - SCORES_AT - 5)
                    link(dve.tensor_reduce(dts[:, 2, 8 + h0:12 + h0], s1[:, h0:h0 + 4, :], AX_X, ALU.max))
                if p == SCORES_AT + 7:
                    link(dve.tensor_reduce(dts[:, 2, 0:8], s0, AX_X, ALU.max))
                    dve.tensor_scalar(dts[:, 2, 0:16], dts[:, 2, 0:16], -1.0, None, ALU.mult).then_inc(negmax_ready, 1)
                if p == PROBS_AT:
                    dve.wait_ge(exp_ready, 2 * HEADS)
                    link(dve.reciprocal(dts[:, 3, 0:16], dts[:, 3, 0:16]))
                    link(dve.tensor_tensor(s0, s0, dts[:, 3, 0:8].unsqueeze(2).broadcast_to([P, 8, P]), ALU.mult))
                if p in (PROBS_AT + 1, PROBS_AT + 2):
                    h0 = 4 * (p - PROBS_AT - 1)
                    ins = dve.tensor_tensor(s1[:, h0:h0 + 4, :], s1[:, h0:h0 + 4, :],
                                            dts[:, 3, 8 + h0:12 + h0].unsqueeze(2).broadcast_to([P, 4, T]), ALU.mult)
                    if h0:
                        ins.then_inc(probs_ready, 1)

            b = base["out"]
            m_lower(1, 0, 8)
            lo(b, 0, 0)
            gate_y(2, 4, 7)
            project(IN_TILES - 1)
            lo(b, 0, 1)
            gate_y(3, 7, 8)
            dve.wait_ge(ssq_ready, 4)
            mean(flat[:, B:B + T], 512, norm_at(3)[0])
            lo(b, 0, 2)
            lo(b, 0, 3)
            newton(2, *(cols(a + T, 2 * T) for a in (SEG, MT, CE)))
            norm(2, 8, 12)
            norm(3, 12, 16)
            m_lower(2, 8, 12)
            lo(b, 1, 0)
            m_lower(3, 12, 16)

            def add_x(s, ring, bank=None):
                dve.wait_ge(w_used, s * 2 + (base["out"] + 2) if bank is None else base["out"] + s + 5)
                dve.tensor_tensor(x1t[:, s, :], ps[:, ring if bank is None else bank, 0:T], xt[:, s, :], ALU.add).then_inc(evacuated, 1)
                dve.wait_ge(evacuated, s + (IN_TILES + 1))
                dve.tensor_scalar(cols(X1G + ring * T, T), x1t[:, s, :], gain2(s), None, ALU.mult) \
                   .then_inc(x1g_ready, 1)

            def lower_x(s, ring):
                dve.wait_ge(x_hi_ready, s + 5)
                dve.tensor_tensor(x_lo[:, s, :], cols(X1G + ring * T, T), x_hi_f[:, s, :], ALU.subtract) \
                   .then_inc(x_lo_ready, 1)

            gain2 = lambda s: smalls[:, G2:G2 + NC][:, s:s + 1] if isinstance(s, int) \
                else smalls[:, G2:G2 + NC].rearrange("p (c a) -> p c a", a=1)[:, s, :]

            for p in range(5, 2 * NC):
                lo(b, p // PIECES, p % PIECES)
                if 7 <= p < 11:
                    lower_x(p - 7, (p - 7) % 2)
                if 6 <= p < 10:
                    add_x(p - 6, p % 2, p - 6)
                if p >= 11 and p % 2:
                    s = (p - 3) // 2
                    add_x(s, s % 2)
                elif p >= 11:
                    lower_x((p - 4) // 2, (p - 4) // 2 % 2)
            b = base["q"]
            lo(b, 0, 0)
            lower_x(NC - 2, 0)
            add_x(NC - 1, 1)
            lo(b, 0, 1)
            lower_x(NC - 1, 1)
            lo(b, 0, 2)
            lo(b, 0, 3)
            dve.wait_ge(ssq_ready, 5)
            mean(flat[:, A:A + T], D, cols(CAND, T))
            newton(3, cols(CAND, T), factor2, cols(CAND + T, T))

            def take_q(s, bank):
                dve.wait_ge(w_used, s * 2 + (base["q"] + 2))
                dve.tensor_tensor(qt[:, s, :], ps[:, bank, 0:T], factor2, ALU.mult).then_inc(evacuated, 1)

            take_q(0, 0)

            def q_pair(i):
                for u in range(PIECES):
                    lo(b, i, u)
                    if u % 2:
                        take_q(i * 2 + (u // 2 - 1), (u // 2 + 1) % 2)
            pairs(dve, q_pair, 1, NC // 2)

            b = base["u"]

            def scale_u(s, bank):
                dve.wait_ge(w_used, s * 2 + (base["u"] + 2))
                dve.tensor_tensor(ps[:, bank, 0:T], ps[:, bank, 0:T], factor2, ALU.mult).then_inc(scaled, 1)

            def u_piece(i, u):
                lo(b, i, u)
                if isinstance(i, int) and i == 0 and u == 1:
                    take_q(NC - 1, 1)
                elif u % 2:
                    scale_u(i * 2 + (u // 2 - 1), (u // 2 + 1) % 2)

            at = [0]

            def next_piece():
                u_piece(at[0] // PIECES, at[0] % PIECES)
                at[0] += 1

            def top16(tiles, pieces):
                next_piece()
                for vals, idx, src, tmp in tiles:
                    chained(dve.max(vals[:, 0:8], src))
                settle()
                for vals, idx, src, tmp in tiles:
                    chained(dve.match_replace(tmp, vals[:, 0:8], src, -3e38))
                if pieces == 3:
                    next_piece()
                for vals, idx, src, tmp in tiles:
                    chained(dve.max_index(idx[:, 0:8], vals[:, 0:8], src))
                if pieces == 2:
                    next_piece()
                settle()
                for vals, idx, src, tmp in tiles:
                    chained(dve.max(vals[:, 8:16], tmp))
                if pieces == 3:
                    next_piece()
                settle()
                for vals, idx, src, tmp in tiles:
                    chained(dve.max_index(idx[:, 8:16], vals[:, 8:16], tmp))

            for _ in range(TOP_AT):
                next_piece()
            for n0 in range(0, TH * 2 * PH, 2):
                if n0 % 8 == 0:
                    dve.wait_ge(side_copied, n0 // 8 + 1)
                top16([(cols(TOPV + n * TOP, TOP), cols(TOPI + n * TOP, TOP).bitcast(U32),
                        cols(SCORES + n * P, P), cols((SCORES2, CAND)[n % 2], P)) for n in (n0, n0 + 1)], 2)
            next_piece()
            settle()
            chained(dve.tensor_copy(cols(TOPIF, 512), cols(TOPI, 512).bitcast(U32)))
            half = [P, PH // 2, TOP, TOP]
            for th in range(TH):
                v = cols(TOPV + th * 256, 256).rearrange("p (h c k) -> p h c k", c=2, k=TOP)
                idx = cols(TOPIF + th * 256, 256).rearrange("p (h c k) -> p h c k", c=2, k=TOP)
                cand = cols(CAND + th * 2048, 2048).rearrange("p (h a b) -> p h a b", a=TOP, b=TOP)
                for hh in range(2):
                    next_piece()
                    settle()
                    hs = slice(4 * hh, 4 * hh + 4)
                    chained(dve.tensor_tensor(cand[:, hs], v[:, hs, 0, :].unsqueeze(3).broadcast_to(half),
                                              v[:, hs, 1, :].unsqueeze(2).broadcast_to(half), ALU.add))
                for h0 in range(0, PH, 2):
                    settle()
                    top16([(cols(PICKV + th * P + h * TOP, TOP), cols(POS + th * P + h * TOP, TOP).bitcast(U32),
                            cols(CAND + th * 2048 + h * 256, 256), cols((CAND2, SCORES)[h % 2], 256))
                           for h in (h0, h0 + 1)], 3)
                next_piece()
                settle()
                pos = cols(POS + th * P, P).bitcast(U32)
                chained(dve.tensor_scalar(cols(POSF, P).bitcast(U32), pos, 4, None, ALU.logical_shift_right))
                chained(dve.tensor_scalar(cols(POSF + P, P).bitcast(U32), pos, 15, None, ALU.bitwise_and))
                settle()
                chained(dve.tensor_copy(cols(POSF + 2 * P, 2 * P), cols(POSF, 2 * P).bitcast(U32)))
                hot = cols(ONEHOT, 1024, TOP)
                hot4 = cols(ONEHOT, 1024).rearrange("p (h a b) -> p h a b", a=TOP, b=TOP)
                for c in range(2):
                    for hh in range(2):
                        hs = slice(4 * hh, 4 * hh + 4)
                        part = cols(POSF + (2 + c) * P + hh * 64, 64)
                        next_piece()
                        settle()
                        chained(dve.tensor_tensor(hot, part.unsqueeze(2).broadcast_to([P, 64, TOP]),
                                                  iota_f[:, 0:TOP].unsqueeze(1).broadcast_to([P, 64, TOP]),
                                                  ALU.is_equal))
                        next_piece()
                        settle()
                        chained(dve.tensor_tensor(hot4, hot4, idx[:, hs, c, :].unsqueeze(2).broadcast_to(half),
                                                  ALU.mult))
                        next_piece()
                        settle()
                        chained(dve.tensor_reduce(cols(KEEP + (c * TH + th) * P + hh * 64, 64), hot, AX_X, ALU.add))
            settle()
            assert at[0] <= PIECES * (GATES_AT - 1), at[0]
            while at[0] < PIECES * (GATES_AT - 1):
                next_piece()
            pick = cols(PICKV, 256, TOP)
            link(dve.tensor_copy(cols(POSF, 16), pick[:, :, 0]))
            dve.tensor_tensor(pick, pick, cols(POSF, 16).unsqueeze(2).broadcast_to([P, 16, TOP]), ALU.subtract) \
               .then_inc(gate_sub, 1)
            next_piece()
            next_piece()
            dve.wait_ge(gate_exp, 1)
            link(dve.tensor_reduce(cols(POSF, 16), pick, AX_X, ALU.add))
            link(dve.reciprocal(cols(POSF, 16), cols(POSF, 16)))
            dve.tensor_tensor(cols(KEEP + 2 * TH * P, 256, TOP), pick,
                              cols(POSF, 16).unsqueeze(2).broadcast_to([P, 16, TOP]), ALU.mult).then_inc(picks_ready, 1)
            next_piece()
            next_piece()

            def hot_rows(dst, a, g, signal):
                dve.tensor_tensor(dst[:, :, :], iota_f[:, :].unsqueeze(1).broadcast_to([P, 8, KEYS]),
                                  route[:, a, :].rearrange("p (g k) -> p g k", k=8)[:, g, :]
                                  .unsqueeze(2).broadcast_to([P, 8, KEYS]), ALU.is_equal).then_inc(signal, 1)

            def gates_pair(i):
                for u in range(PIECES):
                    u_piece(i, u)
                    if u == 2:
                        if isinstance(i, int):
                            dve.wait_ge(route_ready, 1)
                            hot_rows(hot2, 1, 0, hot2_ready)
                        else:
                            dve.wait_ge(gates_ready, i - GATES_AT)
                            hot_rows(hot2, 1, i - GATES_AT, hot2_ready)
                    if u == 3:
                        hot_rows(hot1, 0, 0 if isinstance(i, int) else i - GATES_AT, hot1_ready)
            gates_pair(GATES_AT)
            with dve.Fori(GATES_AT + 1, GATES_AT + NG) as i:
                gates_pair(i)

            def u_pair(i):
                for u in range(PIECES):
                    u_piece(i, u)
            pairs(dve, u_pair, GATES_AT + NG, KEYS // 2)

            b = base["v"]

            def gate(n, a, landed):
                dve.wait_ge(h_landed[a], landed)
                dve.tensor_tensor(act_f[:, a, :], h_in[:, a, :], G[:, n, :], ALU.mult).then_inc(acted, 1)

            def lower_a(a, ready):
                dve.wait_ge(acted, ready)
                dve.wait_ge(a_hi_ready, ready)
                dve.tensor_tensor(x_lo[:, a, :], act_f[:, a, :], x_hi_f[:, a, :], ALU.subtract).then_inc(a_lo_ready, 1)

            lo(b, 0, 0)
            dve.wait_ge(gates_copied, NG)
            for a in range(2):
                gate(a, a, 16)
            for a in range(2):
                lower_a(a, a + 1)
            lo(b, 0, 1)
            scale_u(KEYS - 1, 1)
            lo(b, 0, 2)
            lo(b, 0, 3)

            def v_pair(i):
                for u in range(PIECES):
                    a = u // 2
                    if u % 2 == 0:
                        gate(i * 2 + a, a, i * 16 + 16)
                    lo(b, i, u)
                    if u % 2 == 0:
                        lower_a(a, i * 2 + (a + 1))
            pairs(dve, v_pair, 1, KEYS // 2)

            for a in range(2):
                dve.wait_ge(h_stored[a], 16 * KEYS // 2)
            dve.memset(dts[:, 8, 0:1], 1.0).then_inc(gelu_free, 1)
            dve.wait_ge(tail_landed, 16 * 6)

            def add_x1(n):
                dve.tensor_tensor(cols(YT + n * PCOLS, PCOLS), flat[:, (n ^ 1) * PCOLS:((n ^ 1) + 1) * PCOLS],
                                  cols(n * PCOLS, PCOLS), ALU.add).then_inc(final_y, 1)

            def mean3(th):
                dve.wait_ge(final_sq, 2 * th + 2)
                m = dts[:, 3, th:th + 1]
                link(dve.tensor_tensor(m, dts[:, 7, 2 * th:2 * th + 1], dts[:, 7, 2 * th + 1:2 * th + 2], ALU.add))
                dve.tensor_scalar(m, m, 1.0 / D, EPS, ALU.mult, ALU.add).then_inc(final_mean, 1)

            def factor3(th):
                dve.wait_ge(final_root, th + 1)
                m, r, t = (dts[:, k, th:th + 1] for k in (3, 5, 6))
                link(dve.reciprocal(r, dts[:, 1, th:th + 1]))
                link(dve.tensor_tensor(t, r, r, ALU.mult))
                link(dve.tensor_tensor(t, t, m, ALU.mult))
                link(dve.tensor_scalar(t, t, -0.5, 1.5, ALU.mult, ALU.add))
                dve.tensor_tensor(r, r, t, ALU.mult).then_inc(final_factor, 1)

            dve.wait_ge(first_half_done, 1)
            add_x1(0)
            add_x1(1)
            dve.wait_ge(w_used, b + 2 * KEYS)
            add_x1(2)
            mean3(0)
            add_x1(3)
            factor3(0)
            mean3(1)
            factor3(1)
            dve.wait_ge(final_factor, 2)
            for c in range(2):
                y = cols(YT + D + c * PCOLS, PCOLS)
                dve.scalar_tensor_tensor(out=y, in0=y, scalar=dts[:, 5, 1:2], in1=cols(GAIN3 + c * PCOLS, PCOLS),
                                         op0=ALU.mult, op1=ALU.mult).then_inc(final_ready[1], 1)


def slabs_of(w, tiles):
    return np.ascontiguousarray(w.reshape(NC, P, tiles, P).transpose(2, 1, 0, 3)).reshape(tiles, P, NC * P)


def kernel(**inputs):
    import concourse.bacc as bacc
    from concourse.bass_utils import run_bass_kernel_spmd

    a = {k: np.asarray(v) for k, v in inputs.items()}
    w_in = a["w_in"][0]
    main = IN_TILES * P
    wide = lambda row: np.broadcast_to(row, (P, row.shape[-1]))
    tiles = lambda v, n: v.reshape(n, P).T
    smalls = np.concatenate([
        tiles(a["attn_norm"][0], NC), tiles(a["ffn_norm"][0], NC),
        tiles(a["attn_out_norm"][0], 8), tiles(a["ssm_out_norm"][0], 8),
        a["conv_w"][0].reshape(CONV, CONV_TILES, P).transpose(2, 1, 0).reshape(P, CONV_TILES * CONV),
        tiles(a["conv_b"][0], CONV_TILES), wide(a["dt_bias"]), wide(a["a_log"]),
        tiles(np.repeat(a["d_skip"][0], HD), 8)], axis=1)
    arrays = {
        "x_t": a["x"][0].T.reshape(NC, P, T).transpose(1, 0, 2).reshape(P, NC * T),
        "w_in": slabs_of(np.concatenate([w_in[:, main - CONV_TILES * P:main],
                                         w_in[:, :main - (CONV_TILES + 8) * P],
                                         w_in[:, main - (CONV_TILES + 8) * P:main - CONV_TILES * P]], axis=1),
                         IN_TILES),
        "w_dt": w_in[:, main:].reshape(NC, P, SSM_HEADS).transpose(1, 0, 2).reshape(P, NC * SSM_HEADS),
        "w_out": slabs_of(a["w_out"][0], NC),
        "w_q": slabs_of(a["peer_wq"][0], NC),
        "subkeys": a["peer_subkeys"][0].transpose(3, 0, 1, 2).reshape(P, 2 * PH * KEYS),
        "u_tab": a["peer_u"][0].reshape(KEYS, KEYS, NC, P).transpose(0, 3, 2, 1).reshape(KEYS, P, D),
        "v_tab": a["peer_v"][0].reshape(KEYS, KEYS, D),
        "smalls_in": smalls,
        "rel_bias": a["rel_bias"],
        "selectors": bucket_selectors(),
        "final_gain": a["final_norm"],
    }
    nc = bacc.Bacc("TRN2", target_bir_lowering=False, num_devices=1)
    args, sent = [], {}
    for name, v in arrays.items():
        v = np.ascontiguousarray(v)
        sent["in_" + name] = v
        args.append(nc.dram_tensor("in_" + name, v.shape, mybir.dt.from_np(v.dtype), kind="ExternalInput").ap())
    out = nc.dram_tensor("out", (T, D), F32, kind="ExternalOutput").ap()
    layer(nc, *args, out)
    r = run_bass_kernel_spmd(nc, [sent], core_ids=[0])
    return r.results[0]["out"].reshape(1, T, D)
```
